# Optimizing a Trainium2 kernel written in Bass

```python
import math
import jax
import jax.numpy as jnp
from jax import lax
import numpy as np

D_MODEL = 1024
BATCH = 1
SEQ = 1024
DEPTH = 2
DEC_BATCH = 8
DEC_SEQ = 1
PAST_LEN = 1024
PAGE_SIZE = 128

N_A_LAYERS = DEPTH // 2
N_B_LAYERS = DEPTH - N_A_LAYERS
A_HEAD = 64
A_HEADS = D_MODEL // A_HEAD
DECAY_LORA = 64
AAA_LORA = 64
GATE_LORA = 160
GN_EPS = 64e-5
B_HEAD = 64
B_HEADS = D_MODEL // (2 * B_HEAD)
ATTN_SCALE = B_HEAD ** -0.5
Q_BLOCK = 128
SUBLN_EPS = 1e-5
NEG = -1e30
D_FF = 4 * D_MODEL
LN_EPS = 1e-5
DN_ALPHA = (2 * DEPTH) ** 0.25
DN_BETA = (8 * DEPTH) ** -0.25

kernel_name = 'yoco_rwkv7_diffattn_decode_step'

def layer_norm(x, g, b):
    xf = x.astype(jnp.float32)
    mu = jnp.mean(xf, -1, keepdims=True)
    var = jnp.mean(jnp.square(xf - mu), -1, keepdims=True)
    return ((xf - mu) * lax.rsqrt(var + LN_EPS) * g + b).astype(x.dtype)

def ada_mod(c, w, b, n):
    m = jnp.dot(jax.nn.silu(c), w) + b
    return jnp.split(m[:, None, :], n, axis=-1)

def sq_relu_mlp(h, w1, w2):
    return jnp.dot(jnp.square(jax.nn.relu(jnp.dot(h, w1))), w2)

def wkv7_scan(r, w, k, v, a, b, s0):
    def step(S, inp):
        rt, wt, kt, vt, at, bt = inp
        sa = jnp.einsum('bhij,bhj->bhi', S, at)
        S = S * wt[:, :, None, :] + sa[..., None] * bt[:, :, None, :] + vt[..., None] * kt[:, :, None, :]
        return S, jnp.einsum('bhij,bhj->bhi', S, rt)
    seq = tuple(jnp.moveaxis(t.astype(jnp.float32), 1, 0) for t in (r, w, k, v, a, b))
    s_fin, y = lax.scan(step, s0.astype(jnp.float32), seq)
    return jnp.moveaxis(y, 0, 1), s_fin

def rwkv7_mix(h, prev, s0, mu, w_rkv, w_o, w0, w1, w2, a0, a1, a2, g1, g2, k_k, k_a, r_k, gn_g, gn_b):
    Bn, T, D = h.shape
    h_prev = jnp.concatenate([prev[:, None, :].astype(h.dtype), h[:, :-1]], axis=1)
    xx = h_prev - h
    xs = h[None] + xx[None] * mu[:, None, None, :]
    r, k, v = jnp.einsum('pbtd,pde->pbte', xs[:3], w_rkv)
    xw, xa, xg = xs[3], xs[4], xs[5]
    w_log = -jax.nn.softplus(-(w0 + jnp.dot(jnp.tanh(jnp.dot(xw, w1)), w2))) - 0.5
    decay = jnp.exp(-jnp.exp(w_log.astype(jnp.float32)))
    a = jax.nn.sigmoid(a0 + jnp.dot(jnp.dot(xa, a1), a2))
    g = jnp.dot(jax.nn.sigmoid(jnp.dot(xg, g1)), g2)
    split = lambda t: t.reshape(Bn, T, A_HEADS, A_HEAD)
    kkf = split(k * k_k).astype(jnp.float32)
    kk = kkf / jnp.maximum(jnp.linalg.norm(kkf, axis=-1, keepdims=True), 1e-12)
    k = k * (1 + (a - 1) * k_a)
    r_h, k_h, v_h, a_h = split(r), split(k), split(v), split(a)
    y, s_fin = wkv7_scan(r_h, split(decay), k_h, v_h, -kk, kk * a_h, s0)
    mu_y = jnp.mean(y, -1, keepdims=True)
    var_y = jnp.mean(jnp.square(y - mu_y), -1, keepdims=True)
    yn = ((y - mu_y) * lax.rsqrt(var_y + GN_EPS)).reshape(Bn, T, D) * gn_g + gn_b
    bonus = jnp.sum(r_h * k_h * r_k, -1, keepdims=True) * v_h
    out = (yn + bonus.reshape(Bn, T, D)) * g
    return jnp.dot(out.astype(h.dtype), w_o), h[:, -1], s_fin

def diff_lambda(lam_q, lam_k, lam_init):
    lq = lam_q.astype(jnp.float32)
    lk = lam_k.astype(jnp.float32)
    return jnp.exp(jnp.sum(lq[0] * lk[0])) - jnp.exp(jnp.sum(lq[1] * lk[1])) + lam_init

def diff_combine(s, lam):
    p = jax.nn.softmax(s, axis=-1)
    return p[..., 0, :, :] - lam * p[..., 1, :, :]

def diff_attn_prompt(q, k, v, lam):
    Bn, S = q.shape[:2]
    nb = S // Q_BLOCK
    qb = q.reshape(Bn, nb, Q_BLOCK, B_HEADS, 2, B_HEAD).swapaxes(0, 1)
    k_pos = jnp.arange(S)

    def block(args):
        i, qi = args
        s = jnp.einsum('bqhmd,bkhmd->bhmqk', qi, k).astype(jnp.float32) * ATTN_SCALE
        q_pos = i * Q_BLOCK + jnp.arange(Q_BLOCK)
        s = jnp.where(k_pos[None, :] <= q_pos[:, None], s, NEG)
        attn = diff_combine(s, lam).astype(v.dtype)
        return jnp.einsum('bhqk,bkhe->bqhe', attn, v)

    o = lax.map(block, (jnp.arange(nb), qb))
    return o.swapaxes(0, 1).reshape(Bn, S, B_HEADS, 2 * B_HEAD)

def diff_attn_sample(q, k_new, v_new, k_past, v_past, lam):
    T = q.shape[1]
    P = k_past.shape[1]
    s_past = jnp.einsum('bqhmd,bkhmd->bhmqk', q, k_past).astype(jnp.float32) * ATTN_SCALE
    s_new = jnp.einsum('bqhmd,bkhmd->bhmqk', q, k_new).astype(jnp.float32) * ATTN_SCALE
    causal = jnp.arange(T)[None, :] <= jnp.arange(T)[:, None]
    s_new = jnp.where(causal, s_new, NEG)
    attn = diff_combine(jnp.concatenate([s_past, s_new], axis=-1), lam).astype(v_new.dtype)
    return (jnp.einsum('bhqk,bkhe->bqhe', attn[..., :P], v_past)
            + jnp.einsum('bhqk,bkhe->bqhe', attn[..., P:], v_new))

def diff_head_out(o, g, lam_init, w_o):
    of = o.astype(jnp.float32)
    on = of * lax.rsqrt(jnp.mean(jnp.square(of), -1, keepdims=True) + SUBLN_EPS) * g * (1.0 - lam_init)
    Bn, T = o.shape[:2]
    return jnp.dot(on.reshape(Bn, T, -1).astype(o.dtype), w_o)

def setup_inputs(seed: int = 0) -> dict:
    key = jax.random.key(seed)
    ks = iter(jax.random.split(key, 64))
    f32 = jnp.float32
    D = D_MODEL
    NA, NB = N_A_LAYERS, N_B_LAYERS

    def nrm(shape, scale=1.0):
        return jax.random.normal(next(ks), shape, f32) * scale

    def unif(shape, lo, hi):
        return jax.random.uniform(next(ks), shape, f32, lo, hi)

    n_pages = PAST_LEN // PAGE_SIZE
    n_used = DEC_BATCH * n_pages
    n_pool = n_used + max(1, n_used // 4)
    perm = jax.random.permutation(next(ks), n_pool)
    page_table = perm[:n_used].reshape(DEC_BATCH, n_pages).astype(jnp.int32)
    sd = D ** -0.5
    rkv_scale = jnp.array([1.0, 1.0, DN_BETA], f32)[None, :, None, None]
    return {
        'x_prompt': nrm((BATCH, SEQ, D)),
        'x_sample': nrm((DEC_BATCH, DEC_SEQ, D)),
        'cache_k': nrm((n_pool, PAGE_SIZE, B_HEADS, 2, B_HEAD)),
        'cache_v': nrm((n_pool, PAGE_SIZE, B_HEADS, 2 * B_HEAD)),
        'state_wkv': nrm((NA, DEC_BATCH, A_HEADS, A_HEAD, A_HEAD), 0.1),
        'state_shift': nrm((NA, DEC_BATCH, D)),
        'page_table': page_table,
        'c_prompt': nrm((BATCH, D)),
        'c_sample': nrm((DEC_BATCH, D)),
        'ln_g': 1.0 + nrm((DEPTH, 2, D), 0.02),
        'ln_b': nrm((DEPTH, 2, D), 0.02),
        'ada_w': nrm((DEPTH, D, 6 * D), 0.1 * sd),
        'ada_b': nrm((DEPTH, 6 * D), 0.01),
        'ffn_w1': nrm((DEPTH, D, D_FF), sd * DN_BETA),
        'ffn_w2': nrm((DEPTH, D_FF, D), D_FF ** -0.5 * DN_BETA),
        'a_mu': unif((NA, 6, D), 0.0, 1.0),
        'a_w_rkv': nrm((NA, 3, D, D), sd) * rkv_scale,
        'a_w_o': nrm((NA, D, D), sd * DN_BETA),
        'a_w0': unif((NA, D), -6.0, 1.0),
        'a_w1': nrm((NA, D, DECAY_LORA), sd),
        'a_w2': nrm((NA, DECAY_LORA, D), 0.1 * DECAY_LORA ** -0.5),
        'a_a0': nrm((NA, D), 0.1),
        'a_a1': nrm((NA, D, AAA_LORA), sd),
        'a_a2': nrm((NA, AAA_LORA, D), 0.1 * AAA_LORA ** -0.5),
        'a_g1': nrm((NA, D, GATE_LORA), sd),
        'a_g2': nrm((NA, GATE_LORA, D), GATE_LORA ** -0.5),
        'a_k_k': 0.85 + nrm((NA, D), 0.02),
        'a_k_a': 1.0 + nrm((NA, D), 0.02),
        'a_r_k': nrm((NA, A_HEADS, A_HEAD), 0.1),
        'a_gn_g': 1.0 + nrm((NA, D), 0.02),
        'a_gn_b': nrm((NA, D), 0.02),
        'kv_ada_w': nrm((D, 2 * D), 0.1 * sd),
        'kv_ada_b': nrm((2 * D,), 0.01),
        'kv_w_k': nrm((D, D), sd),
        'kv_w_v': nrm((D, D), sd * DN_BETA),
        'b_w_q': nrm((NB, D, D), sd),
        'b_w_o': nrm((NB, D, D), sd * DN_BETA),
        'b_lam_q': nrm((NB, 2, B_HEAD), 0.1),
        'b_lam_k': nrm((NB, 2, B_HEAD), 0.1),
        'b_subln_g': 1.0 + nrm((NB, 2 * B_HEAD), 0.02),
    }

def reference(x_prompt, x_sample, cache_k, cache_v, state_wkv, state_shift, page_table, c_prompt, c_sample,
              ln_g, ln_b, ada_w, ada_b, ffn_w1, ffn_w2,
              a_mu, a_w_rkv, a_w_o, a_w0, a_w1, a_w2, a_a0, a_a1, a_a2, a_g1, a_g2,
              a_k_k, a_k_a, a_r_k, a_gn_g, a_gn_b,
              kv_ada_w, kv_ada_b, kv_w_k, kv_w_v,
              b_w_q, b_w_o, b_lam_q, b_lam_k, b_subln_g):

    def trunk(x, c, shift0, wkv0, attend):
        Bn, T, _ = x.shape
        shifts, wkvs = [], []
        k_sh = v_sh = None
        for l in range(DEPTH):
            sh_m, sc_m, gt_m, sh_f, sc_f, gt_f = ada_mod(c, ada_w[l], ada_b[l], 6)
            h = x * (1 + sc_m) + sh_m
            if l < N_A_LAYERS:
                j = l
                mix, last, s_fin = rwkv7_mix(h, shift0[j], wkv0[j], a_mu[j], a_w_rkv[j], a_w_o[j],
                                             a_w0[j], a_w1[j], a_w2[j], a_a0[j], a_a1[j], a_a2[j],
                                             a_g1[j], a_g2[j], a_k_k[j], a_k_a[j], a_r_k[j],
                                             a_gn_g[j], a_gn_b[j])
                shifts.append(last)
                wkvs.append(s_fin)
            else:
                j = l - N_A_LAYERS
                lam_init = 0.8 - 0.6 * math.exp(-0.3 * l)
                lam = diff_lambda(b_lam_q[j], b_lam_k[j], lam_init)
                q = jnp.dot(h, b_w_q[j]).reshape(Bn, T, B_HEADS, 2, B_HEAD)
                o = attend(q, k_sh, v_sh, lam)
                mix = diff_head_out(o, b_subln_g[j], lam_init, b_w_o[j])
            x = layer_norm(DN_ALPHA * x + (1 + gt_m) * mix, ln_g[l, 0], ln_b[l, 0])
            hf = x * (1 + sc_f) + sh_f
            x = layer_norm(DN_ALPHA * x + (1 + gt_f) * sq_relu_mlp(hf, ffn_w1[l], ffn_w2[l]),
                           ln_g[l, 1], ln_b[l, 1])
            if l == N_A_LAYERS - 1:
                sh_kv, sc_kv = ada_mod(c, kv_ada_w, kv_ada_b, 2)
                hkv = x * (1 + sc_kv) + sh_kv
                k_sh = jnp.dot(hkv, kv_w_k).reshape(Bn, T, B_HEADS, 2, B_HEAD)
                v_sh = jnp.dot(hkv, kv_w_v).reshape(Bn, T, B_HEADS, 2 * B_HEAD)
        return x, k_sh, v_sh, jnp.stack(wkvs), jnp.stack(shifts)

    bp = x_prompt.shape[0]
    shift0_p = jnp.zeros((N_A_LAYERS, bp, D_MODEL), x_prompt.dtype)
    wkv0_p = jnp.zeros((N_A_LAYERS, bp, A_HEADS, A_HEAD, A_HEAD), jnp.float32)
    y_prompt, k_prompt, v_prompt, wkv_prompt, shift_prompt = trunk(
        x_prompt, c_prompt, shift0_p, wkv0_p, diff_attn_prompt)

    bd, n_pages = page_table.shape
    k_past = cache_k[page_table].reshape(bd, n_pages * PAGE_SIZE, B_HEADS, 2, B_HEAD)
    v_past = cache_v[page_table].reshape(bd, n_pages * PAGE_SIZE, B_HEADS, 2 * B_HEAD)

    def attend_sample(q, k_new, v_new, lam):
        return diff_attn_sample(q, k_new, v_new, k_past, v_past, lam)

    y_sample, k_sample, v_sample, wkv_sample, shift_sample = trunk(
        x_sample, c_sample, state_shift, state_wkv, attend_sample)

    return (y_prompt, y_sample, k_prompt, v_prompt, wkv_prompt, shift_prompt,
            k_sample, v_sample, wkv_sample, shift_sample)


_drawn_inputs = setup_inputs


def setup_inputs(seed=0):
    import zlib

    import numpy as np

    out = dict(_drawn_inputs(seed))
    spreads = {}
    factors = {'a_w1': 8.0,
     'a_w2': 8.0,
     'a_k_k': 8.722,
     'a_k_a': 2.862,
     'a_gn_g': 8.0,
     'a_gn_b': 8.0,
     'kv_ada_b': 3.577,
     'b_lam_q': 2.857,
     'b_subln_g': 24.288,
     'a_r_k': 4.051}
    for name, (base, spread) in spreads.items():
        noise = np.random.default_rng([zlib.crc32(name.encode()), seed]).standard_normal(out[name].shape)
        drawn = base * np.exp(spread * noise) if base else spread * noise
        out[name] = jnp.asarray(drawn.astype(out[name].dtype))
    for name, factor in factors.items():
        out[name] = (out[name] * factor).astype(out[name].dtype)
    return out
```

```python
from contextlib import ExitStack
import math

import concourse.bass as bass
from concourse import mybir

F32 = mybir.dt.float32
F32R = mybir.dt.float32r
I32 = mybir.dt.int32
ALU = mybir.AluOpType
ACT = mybir.ActivationFunctionType
AX = mybir.AxisListType

P = 128
D = 1024
KC = D // P
SEQ = 1024
NS = 8
T = SEQ + NS
NG = 3
G = T // NG
SLAB = KC * P
ALPHA = 4.0 ** 0.25
LN_EPS = 1e-5
GN_EPS = 64e-5
SUBLN_EPS = 1e-5
LAM_INIT = 0.8 - 0.6 * math.exp(-0.3)
ATTN_SCALE = 64 ** -0.5
NEG = -1e30
DECAY_SCALE = -math.exp(-0.5)

VEC_NAMES = (["ada_b0"] * 6 + ["ada_b1"] * 6 + ["kv_b"] * 2 + ["ln_g"] * 4 + ["ln_b"] * 4 + ["mu"] * 6
             + ["w0", "a0", "k_k", "k_a", "r_k", "gn_g", "gn_b"])
NV = len(VEC_NAMES)
V_LNG, V_LNB, V_MU = 14, 18, 22
V_W0, V_A0, V_KK, V_KA, V_RK, V_GNG, V_GNB = range(28, 35)
NM = 14
M_SHM, M_SCM, M_GTM, M_SHF, M_SCF, M_GTF = range(6)
M_KVSH, M_KVSC = 12, 13
S_R, S_K, S_V, S_LW, S_A, S_G, S_MIX = range(1, 8)


C_LEVEL = 0
C_UPPER = 7 * P
C_BLOCK = C_UPPER + 2 * P
C_CAUSAL = C_BLOCK + P
C_RESET = C_CAUSAL + P
C_SIGN = C_RESET + P
C_ALL = C_SIGN + 1


class Machine:

    def __init__(self, nc, io, ctx):
        self.nc, self.io = nc, io

        def sb(name, shape, dt=F32):
            return ctx.enter_context(nc.sbuf_tensor(name, shape, dt))

        self.ident = sb("ident", [P, P])
        self.mean = sb("mean_matrix", [P, P])
        self.eps = sb("eps", [P, 1])
        self.mods = sb("mods", [P, NM, KC, 1 + NS])
        self.vecs = sb("vecs", [P, NV * KC])
        self.w_raw = sb("w_raw", [P, 2, KC, P])
        self.w_hi = sb("w_hi", [P, 2, KC, P], F32R)
        self.w_lo = sb("w_lo", [P, 2, KC, P], F32R)
        self.acc = [ctx.enter_context(nc.psum_tensor(f"acc{i}", [P, NG, 512], F32)) for i in range(2)]
        self.aux2 = ctx.enter_context(nc.psum_tensor("aux", [P, 2, 512], F32))
        self.aux = [self.aux2[:, i, :] for i in range(2)]

        def sem(name):
            return ctx.enter_context(nc.semaphore(name))

        self.w_landed = [sem("w_landed0"), sem("w_landed1")]
        self.hi_done = sem("w_hi_done")
        self.lo_done = sem("w_lo_done")
        self.mm_done = sem("mm_done")
        self.acc_free = [sem("acc_free0"), sem("acc_free1")]
        self.t_free = sem("stage_free")
        self.staged = 0
        self.phase_sems = []
        self.sem_names = set()
        self.phases = 0
        self.slabs = 0
        self.xt = nc.dram_tensor("scratch_x", (KC, P, T), F32, kind="Internal").ap()
        self.srows = nc.dram_tensor("scratch_sample_rows", (6, NS, D), F32, kind="Internal").ap()
        self.yrows = nc.dram_tensor("scratch_sample_y", (NS, D), F32, kind="Internal").ap()
        self.scr = nc.dram_tensor("scratch_mix", (8, KC, P, T), F32, kind="Internal").ap()

    def phase_sem(self, name):
        self.phase_sems.append(self.nc.alloc_semaphore(name=f"{name}_{self.phases}" if name in self.sem_names else name))
        self.sem_names.add(name)
        return self.phase_sems[-1]

    def end_phase(self):
        self.nc.clear_and_free_semaphores(self.phase_sems)
        self.nc.all_engine_barrier()
        self.phase_sems = []
        self.phases += 1

    def vec(self, v, c):
        return self.vecs[:, v * KC + c:v * KC + c + 1]

    def mod(self, m, c):
        return self.mods[:, m, c, 0:1]


def landed_at(s):
    return 16 * (s // 2 + 1)


def slab_of(w, mo, width=P):
    return w[:, mo * P:mo * P + width].rearrange("(k p) n -> p k n", p=P)


def slab_at(w, mo):
    return w[:, bass.ds(mo * P, P)].rearrange("(k p) n -> p k n", p=P)



def ring_load(m, sp, src, s, p, width=P, first=False):
    if not first:
        sp.wait_ge(m.lo_done, s - 1)
    m.nc.sync.dma_start(m.w_raw[:, p, :, 0:width], src).then_inc(m.w_landed[p], 16)


def ring_high(m, act, s, p, n, width=P, first=False):
    act.wait_ge(m.w_landed[p], n)
    if not first:
        act.wait_ge(m.mm_done, s - 1)
    m.nc.scalar.activation(m.w_hi[:, p, :, 0:width], m.w_raw[:, p, :, 0:width], ACT.Copy).then_inc(m.hi_done, 1)


def ring_low(m, pool, s, p, width=P):
    pool.wait_ge(m.hi_done, s + 1)
    m.nc.gpsimd.tensor_tensor(m.w_lo[:, p, :, 0:width], m.w_raw[:, p, :, 0:width],
                              m.w_hi[:, p, :, 0:width].bitcast(F32), ALU.subtract).then_inc(m.lo_done, 1)


def ring_mul(m, pe, s, p, xh, xl, width=P, first=False):
    pe.wait_ge(m.lo_done, s + 1)
    if not first:
        pe.wait_ge(m.acc_free[p], s - p)
    for k in range(KC):
        hi, lo = m.w_hi[:, p, k, 0:width], m.w_lo[:, p, k, 0:width]
        for g in range(NG):
            out = m.acc[p][0:width, g, 0:G]
            cols = slice(g * G, (g + 1) * G)
            m.nc.tensor.matmul(out, hi, xh[:, k, cols], start=(k == 0), stop=False)
            m.nc.tensor.matmul(out, hi, xl[:, k, cols], start=False, stop=False)
            last = m.nc.tensor.matmul(out, lo, xh[:, k, cols], start=False, stop=(k == KC - 1))
    last.then_inc(m.mm_done, 1)


def acc_view(m, p, rows=P):
    return m.acc[p][0:rows, :, 0:G]


def as3(ap):
    return ap.rearrange("p (g n) -> p g n", g=NG)


def setup_phase(m):
    nc, io = m.nc, m.io
    with ExitStack() as ctx:
        def sb(name, shape, dt=F32):
            return ctx.enter_context(nc.sbuf_tensor(name, shape, dt))

        def sem(name):
            return m.phase_sem(name)

        rows = sb("vec_rows", [P, 3, P])
        crow = sb("c_rows", [1 + NS, D])
        cexp = sb("c_exp", [1 + NS, D])
        cden = sb("c_den", [1 + NS, D])
        cT = sb("c_cols", [P, KC, 1 + NS])
        NB = 4
        wide = sb("ada_slab", [P, NB, KC, 512])
        mrow = sb("mod_rows", [1 + NS, 2, 512])
        small, c_in, ident0, ident1 = sem("rows_in"), sem("c_in"), sem("ident_zero"), sem("ident_done")
        landed = [sem(f"ada_landed{i}") for i in range(NB)]
        cexped, csteps, ct_done, ct_in = sem("c_exped"), sem("c_steps"), sem("c_turned"), sem("c_cols_in")
        vt_done, vt_in = sem("vecs_turned"), sem("vecs_in")
        ada_mm, row_in, mod_t, mod_in = sem("ada_mm"), sem("mod_row_in"), sem("mod_turned"), sem("mod_in")
        block = ctx.enter_context(nc.Block())
        NU = 2 * NM

        def ada_src(u):
            mod, half = u // 2, u % 2
            if mod < 12:
                w = io["ada_w"][mod // 6, :, (mod % 6) * D + half * 512:(mod % 6) * D + half * 512 + 512]
            else:
                w = io["kv_ada_w"][:, (mod - 12) * D + half * 512:(mod - 12) * D + half * 512 + 512]
            return w.rearrange("(k p) n -> p k n", p=P)

        @block.sync
        def _(sp):
            nc.sync.dma_start(crow[0:1, :], io["c_prompt"]).then_inc(c_in, 16)
            nc.sync.dma_start(crow[1:1 + NS, :], io["c_sample"]).then_inc(c_in, 16)
            at = 0
            for src, n in ((io["ada_b"], 12), (io["kv_ada_b"], 2), (io["ln_g"], 4), (io["ln_b"], 4), (io["a_mu"], 6),
                           (io["a_w0"], 1), (io["a_a0"], 1), (io["a_k_k"], 1), (io["a_k_a"], 1), (io["a_r_k"], 1),
                           (io["a_gn_g"], 1), (io["a_gn_b"], 1)):
                flat = src
                if len(src.shape) == 3:
                    flat = src.rearrange("a b c -> (a b c)")
                elif len(src.shape) == 2:
                    flat = src.rearrange("a b -> (a b)")
                flat = flat.rearrange("(r n) -> r n", n=P)
                done = 0
                while done < n * KC:
                    q = min(n * KC - done, P - at % P)
                    nc.sync.dma_start(rows[at % P:at % P + q, at // P, :], flat[done:done + q, :]).then_inc(small, 16)
                    at += q
                    done += q
            for u in range(NU):
                if u >= NB:
                    sp.wait_ge(ada_mm, u - NB + 1)
                nc.sync.dma_start(wide[:, u % NB, :, :], ada_src(u)).then_inc(landed[u % NB], 16)

        @block.gpsimd
        def _(pool):
            nc.gpsimd.memset(m.mean[:], 1.0 / D)
            nc.gpsimd.memset(m.eps[:], LN_EPS).then_inc(m.t_free, 2)
            nc.gpsimd.memset(m.ident[:], 0.0).then_inc(ident0, 1)
            pool.wait_ge(ident0, 1)
            nc.gpsimd.affine_select(out=m.ident[:], in_=m.ident[:], compare_op=ALU.not_equal, fill=1.0, base=0,
                                    pattern=[[-1, P]], channel_multiplier=1).then_inc(ident1, 1)

        @block.scalar
        def _(act):
            act.wait_ge(c_in, 32)
            nc.scalar.activation(cexp[:], crow[:], ACT.Exp, scale=-1.0).then_inc(cexped, 1)
            for u in range(NU):
                act.wait_ge(ada_mm, u + 1)
                if u >= 2:
                    act.wait_ge(mod_t, u - 1)
                nc.scalar.activation(mrow[:, u % 2, :], m.acc[0][0:1 + NS, u % 3, :], ACT.Copy).then_inc(row_in, 1)

        @block.vector
        def _(dve):
            dve.wait_ge(cexped, 1)
            nc.vector.tensor_scalar_add(cden[:], cexp[:], 1.0).then_inc(csteps, 1)
            dve.wait_ge(csteps, 1)
            nc.vector.reciprocal(cexp[:], cden[:]).then_inc(csteps, 1)
            dve.wait_ge(csteps, 2)
            nc.vector.tensor_tensor(crow[:], crow[:], cexp[:], ALU.mult).then_inc(csteps, 1)
            dve.wait_ge(vt_done, 1)
            nc.vector.tensor_copy(m.vecs[:], m.aux[0][:, 0:NV * KC]).then_inc(vt_in, 1)
            dve.wait_ge(ct_done, 1)
            nc.vector.tensor_copy(cT[:], m.aux[1][:, 0:KC * (1 + NS)].rearrange("p (k n) -> p k n", k=KC)).then_inc(ct_in, 1)
            dve.wait_ge(vt_in, 1)
            for u in range(NU):
                mod, half = u // 2, u % 2
                dve.wait_ge(mod_t, u + 1)
                nc.vector.tensor_tensor(
                    m.mods[:, mod, 4 * half:4 * half + 4, :],
                    m.aux[u % 2][:, 0:4 * (1 + NS)].rearrange("p (k n) -> p k n", k=4),
                    m.vecs[:, mod * KC + 4 * half:mod * KC + 4 * half + 4].unsqueeze(2).to_broadcast([P, 4, 1 + NS]),
                    ALU.add).then_inc(mod_in, 1)
            dve.wait_ge(mod_in, NU)
            for mod in (1, 2, 4, 5, 7, 8, 10, 11, 13):
                nc.vector.tensor_scalar_add(m.mods[:, mod, :, :], m.mods[:, mod, :, :], 1.0).then_inc(mod_in, 1)

        @block.tensor
        def _(pe):
            pe.wait_ge(ident1, 1)
            pe.wait_ge(small, 16 * N_SMALL)
            left = NV * KC
            for t in range(3):
                q = min(P, left - t * P)
                last = nc.tensor.transpose(m.aux[0][:, t * P:t * P + q], rows[0:q, t, :], m.ident[0:q, 0:q])
            last.then_inc(vt_done, 1)
            pe.wait_ge(csteps, 3)
            n = 1 + NS
            for k in range(KC):
                last = nc.tensor.transpose(m.aux[1][:, k * n:(k + 1) * n], crow[:, k * P:(k + 1) * P], m.ident[0:n, 0:n])
            last.then_inc(ct_done, 1)

            def turn(u):
                pe.wait_ge(row_in, u + 1)
                if u < 2:
                    pe.wait_ge(ct_in, 1)
                    pe.wait_ge(vt_in, 1)
                else:
                    pe.wait_ge(mod_in, u - 1)
                for q in range(4):
                    last = nc.tensor.transpose(m.aux[u % 2][:, q * n:(q + 1) * n], mrow[:, u % 2, q * P:(q + 1) * P],
                                               m.ident[0:n, 0:n])
                last.then_inc(mod_t, 1)

            pe.wait_ge(ct_in, 1)
            for u in range(NU):
                pe.wait_ge(landed[u % NB], 16 * (u // NB + 1))
                if u >= 3:
                    pe.wait_ge(row_in, u - 2)
                for k in range(KC):
                    last = nc.tensor.matmul(m.acc[0][0:n, u % 3, :], cT[:, k, :], wide[:, u % NB, k, :],
                                            start=(k == 0), stop=(k == KC - 1))
                last.then_inc(ada_mm, 1)
                if u >= 1:
                    turn(u - 1)
            turn(NU - 1)


N_SMALL = 13


def input_phase(m, h, xx):
    nc, io = m.nc, m.io
    with ExitStack() as ctx:
        def sb(name, shape, dt=F32):
            return ctx.enter_context(nc.sbuf_tensor(name, shape, dt))

        def sem(name):
            return m.phase_sem(name)

        xin = sb("x_rows", [P, KC, D])
        xs = sb("x_sample_rows", [NS, D])
        shin = sb("shift_rows", [NS, D])
        shT = sb("shift_cols", [P, KC, NS])
        stage = sb("x_cols", [P, 2, T])
        lastrows = sb("last_rows", [1 + NS, D])
        x_in = [sem(f"x_in{i}") for i in range(KC)]
        xs_in, turned, staged, h_done, xt_out = sem("xs_in"), sem("x_turned"), sem("x_staged"), sem("h_done"), [sem("xt_out0"), sem("xt_out1")]
        sh_t, sh_in, hs_done, xx_done = sem("shift_turned"), sem("shift_in"), sem("h_sample_done"), sem("xx_done")
        rows_t, rows_in, rows_out = sem("last_turned"), sem("last_in"), sem("last_out")
        block = ctx.enter_context(nc.Block())

        @block.sync
        def _(sp):
            nc.sync.dma_start(xs[:], io["x_sample"].rearrange("b o d -> (b o) d")).then_inc(xs_in, 16)
            nc.sync.dma_start(shin[:], io["state_shift"][0]).then_inc(xs_in, 16)
            for t in range(KC):
                nc.sync.dma_start(xin[:, t, :], io["x_prompt"][0, t * P:(t + 1) * P, :]).then_inc(x_in[t], 16)
            for c in range(KC):
                sp.wait_ge(staged, c + 1)
                nc.sync.dma_start(m.xt[c], stage[:, c % 2, :]).then_inc(xt_out[c % 2], 16)
            sp.wait_ge(rows_in, 1)
            nc.sync.dma_start(io["shift_prompt"][0], lastrows[0:1, :]).then_inc(rows_out, 16)
            nc.sync.dma_start(io["shift_sample"][0], lastrows[1:1 + NS, :]).then_inc(rows_out, 16)
            sp.wait_ge(rows_out, 32)
            for p in range(2):
                sp.wait_ge(xt_out[p], 16 * KC // 2)

        @block.tensor
        def _(pe):
            pe.wait_ge(xs_in, 32)
            for k in range(KC):
                last = nc.tensor.transpose(m.aux[0][:, k * NS:(k + 1) * NS], shin[:, k * P:(k + 1) * P], m.ident[0:NS, 0:NS])
            last.then_inc(sh_t, 1)
            for c in range(KC):
                if c >= 2:
                    pe.wait_ge(staged, c - 1)
                for t in range(KC):
                    if c == 0:
                        pe.wait_ge(x_in[t], 16)
                    nc.tensor.transpose(m.acc[c % 2][:, t // 4, (t % 4) * P:(t % 4 + 1) * P], xin[:, t, c * P:(c + 1) * P],
                                        m.ident[:])
                nc.tensor.transpose(m.acc[c % 2][:, 2, 0:NS], xs[:, c * P:(c + 1) * P], m.ident[0:NS, 0:NS]).then_inc(turned, 1)
            pe.wait_ge(h_done, KC)
            pe.wait_ge(hs_done, 2)
            n = 1 + NS
            for c in range(KC):
                last = nc.tensor.transpose(m.acc[0][0:n, c // 4, (c % 4) * P:(c % 4 + 1) * P], h[:, c, SEQ - 1:T], m.ident[:])
            last.then_inc(rows_t, 1)

        @block.scalar
        def _(act):
            for c in range(KC):
                act.wait_ge(turned, c + 1)
                if c >= 2:
                    act.wait_ge(xt_out[c % 2], 16 * (c // 2))
                    act.wait_ge(h_done, c - 1)
                nc.scalar.activation(stage[:, c % 2, 0:SEQ].rearrange("p (a n) -> p a n", a=2), m.acc[c % 2][:, 0:2, :],
                                     ACT.Copy)
                nc.scalar.activation(stage[:, c % 2, SEQ:T], m.acc[c % 2][:, 2, 0:NS], ACT.Copy).then_inc(staged, 1)
            act.wait_ge(rows_t, 1)
            nc.scalar.activation(lastrows[:].rearrange("p (a n) -> p a n", a=2), m.acc[0][0:1 + NS, 0:2, :],
                                 ACT.Copy).then_inc(rows_in, 1)

        @block.vector
        def _(dve):
            dve.wait_ge(sh_t, 1)
            nc.vector.tensor_copy(shT[:], m.aux[0][:, 0:KC * NS].rearrange("p (k n) -> p k n", k=KC)).then_inc(sh_in, 1)
            for c in range(KC):
                dve.wait_ge(staged, c + 1)
                nc.vector.tensor_copy(h[:, c, SEQ:T], stage[:, c % 2, SEQ:T])
                nc.vector.tensor_scalar(h[:, c, 0:SEQ], stage[:, c % 2, 0:SEQ], m.mod(M_SCM, c), m.mod(M_SHM, c),
                                        ALU.mult, ALU.add).then_inc(h_done, 1)
            dve.wait_ge(h_done, KC)
            hs = h[:, :, SEQ:T]
            nc.vector.tensor_tensor(hs, hs, m.mods[:, M_SCM, :, 1:], ALU.mult).then_inc(hs_done, 1)
            dve.wait_ge(hs_done, 1)
            nc.vector.tensor_tensor(hs, hs, m.mods[:, M_SHM, :, 1:], ALU.add).then_inc(hs_done, 1)
            dve.wait_ge(hs_done, 2)
            nc.vector.tensor_tensor(xx[:, :, 1:SEQ], h[:, :, 0:SEQ - 1], h[:, :, 1:SEQ], ALU.subtract)
            nc.vector.tensor_scalar(xx[:, :, 0:1], h[:, :, 0:1], -1.0, None, ALU.mult)
            dve.wait_ge(sh_in, 1)
            nc.vector.tensor_tensor(xx[:, :, SEQ:T], shT[:], hs, ALU.subtract).then_inc(xx_done, 1)


def project_phase(m, h, xx):
    nc, io = m.nc, m.io
    with ExitStack() as ctx:
        def sb(name, shape, dt=F32):
            return ctx.enter_context(nc.sbuf_tensor(name, shape, dt))

        def sem(name):
            return m.phase_sem(name)

        xh = sb("mix_hi", [P, KC, T], F32R)
        xl = sb("mix_lo", [P, KC, T], F32R)
        lw1 = sb("lora_w", [64, T])
        la1 = sb("lora_a", [64, T])
        lg1 = sb("lora_g", [P, T])
        lg2 = sb("lora_g_tail", [32, T])
        w2w = sb("w2_w", [64, D])
        w2a = sb("w2_a", [64, D])
        w2g = sb("w2_g", [P, D])
        w2t = sb("w2_g_tail", [32, D])
        tmp = sb("mix_tmp", [P, T])
        stage = sb("proj_stage", [P, 2, T])
        mixes = [(0, [P] * KC), (1, [P] * KC), (2, [P] * KC), (3, [64]), (4, [64]), (5, [P, 32])]
        w_src = {3: io["a_w1"][0], 4: io["a_a1"][0], 5: io["a_g1"][0]}
        scr_flat = m.scr.rearrange("j c p t -> (j c) p t")
        mix_f, mix_h, mix_l = sem("mix_made"), sem("mix_hi_made"), sem("mix_lo_made")
        w2_in, out_done = sem("w2_in"), [sem("scratch_out0"), sem("scratch_out1")]
        mm2, st2, fin2, out2 = sem("mm2"), sem("stage2_in"), sem("decay_done"), [sem("out2_0"), sem("out2_1")]
        block = ctx.enter_context(nc.Block())
        s0 = m.slabs
        NL = 4
        sL = s0 + 3 * KC

        @block.sync
        def _(sp):
            for j in range(3):
                w = io["a_w_rkv"][0, j]
                for q in range(2):
                    ring_load(m, sp, slab_of(w, q), s0 + j * KC + q, q, first=(j == 0 and s0 == 0))
                with sp.Fori(1, KC // 2) as i:
                    for q in range(2):
                        ring_load(m, sp, slab_at(w, i * 2 + q), i * 2 + (s0 + j * KC + q), q)
            n = 0
            for j in (3, 4, 5):
                for mo, width in enumerate(mixes[j][1]):
                    ring_load(m, sp, slab_of(w_src[j], mo, width), sL + n, n % 2, width)
                    n += 1

        @block.gpsimd
        def _(pool):
            nc.gpsimd.dma_start(w2w[:], io["a_w2"][0]).then_inc(w2_in, 16)
            nc.gpsimd.dma_start(w2a[:], io["a_a2"][0]).then_inc(w2_in, 16)
            nc.gpsimd.dma_start(w2g[:], io["a_g2"][0, 0:P, :]).then_inc(w2_in, 16)
            nc.gpsimd.dma_start(w2t[:], io["a_g2"][0, P:160, :]).then_inc(w2_in, 16)
            for j in range(3):
                with pool.Fori(0, KC // 2) as i:
                    for q in range(2):
                        ring_low(m, pool, i * 2 + (s0 + j * KC + q), q)
            n = 0
            for j in (3, 4, 5):
                for width in mixes[j][1]:
                    ring_low(m, pool, sL + n, n % 2, width)
                    n += 1

        @block.tensor
        def _(pe):
            for j in range(3):
                pe.wait_ge(mix_l, KC * (j + 1))
                for q in range(2):
                    ring_mul(m, pe, s0 + j * KC + q, q, xh, xl, first=(j == 0 and s0 == 0))
                with pe.Fori(1, KC // 2) as i:
                    for q in range(2):
                        ring_mul(m, pe, i * 2 + (s0 + j * KC + q), q, xh, xl)
            n = 0
            for j in (3, 4, 5):
                pe.wait_ge(mix_l, KC * (j + 1))
                for width in mixes[j][1]:
                    ring_mul(m, pe, sL + n, n % 2, xh, xl, width)
                    n += 1
            pe.wait_ge(w2_in, 64)
            for p in range(2):
                pe.wait_ge(m.acc_free[p], sL + NL)
            for u in range(3 * KC):
                kind, mo = u // KC, u % KC
                if u >= 2:
                    pe.wait_ge(st2, u - 1)
                parts = {0: [(w2w, lw1)], 1: [(w2a, la1)], 2: [(w2g, lg1), (w2t, lg2)]}[kind]
                for g in range(NG):
                    for i, (w, x) in enumerate(parts):
                        last = nc.tensor.matmul(m.acc[u % 2][:, g, 0:G], w[:, mo * P:(mo + 1) * P], x[:, g * G:(g + 1) * G],
                                                start=(i == 0), stop=(i == len(parts) - 1))
                last.then_inc(mm2, 1)

        @block.vector
        def _(dve):
            for j in range(6):
                for c in range(KC):
                    if j and c == 0:
                        dve.wait_ge(m.mm_done, s0 + KC * j if j <= 3 else sL + {4: 1, 5: 2}[j])
                    if j or c:
                        dve.wait_ge(mix_l, j * KC + c)
                    nc.vector.scalar_tensor_tensor(tmp[:], xx[:, c, :], m.vec(V_MU + j, c), h[:, c, :],
                                                   ALU.mult, ALU.add).then_inc(mix_f, 1)
                    dve.wait_ge(mix_f, j * KC + c + 1)
                    nc.vector.tensor_copy(xh[:, c, :], tmp[:]).then_inc(mix_h, 1)
                    dve.wait_ge(mix_h, j * KC + c + 1)
                    nc.vector.tensor_tensor(xl[:, c, :], tmp[:], xh[:, c, :].bitcast(F32), ALU.subtract).then_inc(mix_l, 1)
            for u in range(KC):
                dve.wait_ge(st2, u + 1)
                nc.vector.tensor_scalar(stage[:, u % 2, :], stage[:, u % 2, :], DECAY_SCALE, None,
                                        ALU.mult).then_inc(fin2, 1)

        @block.scalar
        def _(act):
            def store(s, chunk, p, stored):
                act.wait_ge(m.mm_done, s + 1)
                if stored is not None:
                    act.wait_ge(out_done[p], stored)
                nc.scalar.activation(as3(stage[:, p, :]), acc_view(m, p), ACT.Copy).then_inc(m.acc_free[p], 2)
                act.wait_ge(m.acc_free[p], s - p + 2)
                nc.scalar.dma_start(scr_flat[bass.ds(chunk + S_R * KC, 1)].rearrange("a p t -> (a p) t"),
                                    stage[:, p, :]).then_inc(out_done[p], 16)

            widths = [64, 64, P, 32]
            for p in range(2):
                ring_high(m, act, s0 + p, p, landed_at(s0 + p), first=(s0 == 0))
            for p in range(2):
                ring_high(m, act, s0 + 2 + p, p, landed_at(s0 + 2 + p))
                store(s0 + p, p, p, None)
            with act.Fori(1, 3 * KC // 2 - 1) as i:
                for p in range(2):
                    ring_high(m, act, i * 2 + (s0 + 2 + p), p, i * 16 + landed_at(s0 + 2 + p))
                    store(i * 2 + (s0 + p), i * 2 + p, p, i * 16)
            for p in range(2):
                ring_high(m, act, sL + p, p, landed_at(sL + p), widths[p])
                store(sL - 2 + p, 3 * KC - 2 + p, p, 16 * (3 * KC // 2 - 1))
            outs = [(lw1, ACT.Tanh, 1.0), (la1, ACT.Copy, 1.0), (lg1, ACT.Sigmoid, 1.0), (lg2, ACT.Sigmoid, 1.0)]
            for n in range(NL):
                s = sL + n
                act.wait_ge(m.mm_done, s + 1)
                if n + 2 < NL:
                    ring_high(m, act, s + 2, n % 2, landed_at(s + 2), widths[n + 2])
                t, f, sc = outs[n]
                nc.scalar.activation(as3(t[:]), acc_view(m, n % 2, widths[n]), f, scale=sc).then_inc(m.acc_free[n % 2], 2)
            for u in range(3 * KC):
                kind, mo, p = u // KC, u % KC, u % 2
                act.wait_ge(mm2, u + 1)
                if u < 2:
                    act.wait_ge(out_done[p], 16 * 12)
                else:
                    act.wait_ge(out2[p], 16 * (u // 2))
                if kind < 2:
                    nc.scalar.activation(as3(stage[:, p, :]), acc_view(m, p), ACT.Sigmoid,
                                         bias=m.vec(V_W0 + kind, mo)).then_inc(st2, 1)
                    if kind == 0:
                        act.wait_ge(fin2, u + 1)
                    else:
                        act.wait_ge(st2, u + 1)
                else:
                    nc.scalar.activation(as3(stage[:, p, :]), acc_view(m, p), ACT.Copy).then_inc(st2, 1)
                    act.wait_ge(st2, u + 1)
                nc.scalar.dma_start(m.scr[S_LW + kind, mo], stage[:, p, :]).then_inc(out2[p], 16)
            for p in range(2):
                act.wait_ge(out_done[p], 16 * 12)
                act.wait_ge(out2[p], 16 * 12)
        m.slabs = sL + NL


def scan_phase(m, bs, gs):
    nc, io = m.nc, m.io
    with ExitStack() as ctx:
        def sb(name, shape, dt=F32):
            return ctx.enter_context(nc.sbuf_tensor(name, shape, dt))

        sems = {}

        def S(name):
            if name not in sems:
                sems[name] = m.phase_sem(name)
            return sems[name]

        def need(eng, name, c, n=1, k=1):
            eng.wait_ge(S(name), c * n + k)

        consts = sb("scan_masks", [P, C_ALL])
        r, k, v, lw, a, g = (sb(f"pair_{x}", [P, T]) for x in ("r", "k", "v", "lw", "a", "g"))
        loads = [("k", k, S_K), ("a", a, S_A), ("lw", lw, S_LW), ("r", r, S_R), ("v", v, S_V), ("g", g, S_G)]
        t1, t2, t3, k2, kb = (sb(x, [P, T]) for x in ("t1", "t2", "t3", "k2", "kk_a"))
        kk = sb("kk", [P, T])
        cum = sb("cum", [P, SEQ])
        bonus = sb("bonus", [P, T])
        reset = sb("reset", [P, SEQ])
        ar = sb("ar", [P, KC, 2, P])
        bt, kt = sb("bt", [P, KC, P]), sb("kt", [P, KC, P])
        vT, bT, kT = sb("vT", [P, KC, P]), sb("bT", [P, KC, P]), sb("kT", [P, KC, P])
        fac = sb("fac", [P, KC])
        smp = sb("smp", [P, P // NS, NS])
        smprow = sb("smprow", [48, P])
        ntrb = sb("ntrb", [P, 4, 4, 2, P])
        akrk = sb("akrk", [P, 4, 4, 2, P])
        xT = sb("xT", [P, 4, 4, P])
        x = sb("x", [P, 2, 4, P])
        tm = sb("tm", [P, 2, 4, P])
        st = sb("st", [P, P])
        rs, sa = sb("rs", [P, P]), sb("sa", [P, P])
        y = sb("y", [P, 16, 64])
        ysq = t1
        stat, stat2 = sb("stat", [P, 16]), sb("stat2", [P, 16])
        wkv = sb("wkv_out", [64, P])
        epst = sb("eps_gn", [P, 1])
        omka = sb("one_minus_ka", [P, KC])
        ones64 = consts[:, C_BLOCK:C_BLOCK + P]
        upper = consts[:, C_UPPER:C_UPPER + 2 * P]
        psx, pst, psT = [m.acc[q][:, 1, :] for q in range(2)], [m.acc[q][:, 0, :] for q in range(2)], \
            [m.acc[q][:, 2, :] for q in range(2)]
        chunks = "p (j n) -> p j n"
        block = ctx.enter_context(nc.Block())

        def lev(l):
            return consts[:, C_LEVEL + l * P:C_LEVEL + (l + 1) * P].unsqueeze(1).to_broadcast([P, 4, P])

        def loop(eng, body):
            body(0, True)
            with eng.Fori(1, KC) as c:
                body(c, False)

        def col(vi, c):
            return m.vecs[:, bass.ds(c + vi * KC, 1)]

        def whole(tile):
            return tile[:]

        @block.sync
        def _(sp):
            nc.sync.dma_start(consts[:], io["masks"]).then_inc(S("masks_in"), 16)
            last_use = {"k": "k2", "a": "kb", "lw": "at", "r": "smp_v", "v": "yn", "g": "gated"}

            def body(c, first):
                for name, tile, j in loads:
                    if not first:
                        need(sp, last_use[name], c - 1)
                    nc.sync.dma_start(tile[:], m.scr[j, bass.ds(c, 1)].rearrange("a p t -> (a p) t")).then_inc(S("in_" + name), 16)
                need(sp, "smprow", c)
                nc.sync.dma_start(m.srows[:, :, bass.ds(c * P, P)].rearrange("v b n -> (v b) n"), smprow[:]).then_inc(S("smp_out"), 16)
                need(sp, "wkv", c)
                nc.sync.dma_start(io["wkv_prompt"][0, 0, bass.ds(c * 2, 2)].rearrange("h i j -> i h j"),
                                  wkv[:].rearrange("i (h j) -> i h j", h=2)).then_inc(S("wkv_out"), 16)
                need(sp, "gated", c)
                nc.sync.dma_start(m.scr[S_MIX, bass.ds(c, 1), :, 0:SEQ].rearrange("a p t -> (a p) t"), t1[:, 0:SEQ]).then_inc(S("mixed_out"), 16)

            loop(sp, body)
            for name in ("smp_out", "wkv_out", "mixed_out"):
                sp.wait_ge(S(name), 16 * KC)

        @block.gpsimd
        def _(pool):
            def body(c, first):
                for q in range(4):
                    need(pool, "ntrb", c, 4, q + 1)
                    if not first:
                        need(pool, "y_mm", c - 1, KC, KC)
                    nc.gpsimd.tensor_tensor(xT[:, q], ntrb[:, q, :, 0, :], lev(0), ALU.mult).then_inc(S("xt0"), 1)
                    need(pool, "xt0", c, 4, q + 1)
                    nc.gpsimd.tensor_tensor(xT[:, q], xT[:, q], m.ident[:].unsqueeze(1).to_broadcast([P, 4, P]),
                                            ALU.add).then_inc(S("xt1"), 1)
            pool.wait_ge(S("masks_in"), 16)
            loop(pool, body)

        @block.tensor
        def _(pe):
            def body(c, first):
                def cols3(dst, src):
                    for gi in range(NG):
                        last = nc.tensor.matmul(dst[:, gi, 0:G], ones64, src[:, gi * G:(gi + 1) * G], start=True, stop=True)
                    return last

                if not first:
                    need(pe, "yT_in", c - 1)
                    need(pe, "st_in", c - 1, KC, KC)
                need(pe, "sq", c)
                cols3(m.acc[0], t1).then_inc(S("ss_mm"), 1)
                need(pe, "rk", c)
                cols3(m.acc[1], t3).then_inc(S("bonus_mm"), 1)
                need(pe, "smp_v", c)
                nc.tensor.transpose(m.aux[0][:, 0:P], smp[:].rearrange("p v b -> p (v b)"), m.ident[:]).then_inc(S("smp_t"), 1)
                need(pe, "nrm", c)
                for name, src, dst, q in (("vT_t", v, vT, 0), ("bT_t", bt, bT, 1), ("kT_t", kt, kT, 0)):
                    if name == "bT_t":
                        need(pe, "bt", c)
                        need(pe, "bonus", c)
                    if name == "kT_t":
                        need(pe, "kt", c)
                        need(pe, "vT", c)
                    for j in range(KC):
                        s_ = src[:, j * P:(j + 1) * P] if name == "vT_t" else src[:, j, :]
                        last = nc.tensor.transpose(m.acc[q][:, j // 4, (j % 4) * P:(j % 4 + 1) * P], s_, m.ident[:])
                    last.then_inc(S(name), 1)
                need(pe, "at", c)
                need(pe, "rt", c)

                def unit(gq, u):
                    return 2 * gq + u % 2, 64 * (u // 2)

                def products(gq):
                    q = gq % 2
                    if gq < 2:
                        need(pe, "bT" if q == 1 else "kT", c)
                    else:
                        need(pe, "xt_in", c, 4 * 7, 14)
                    for lhs, name, back in ((bt, "ntrb_mm", None), (kt, "akrk_mm", "ntrb")):
                        if back:
                            need(pe, back, c, 4, gq + 1)
                        for u in range(4):
                            j, h0 = unit(gq, u)
                            last = nc.tensor.matmul(m.acc[q][:, u // 2, (u % 2) * 256:(u % 2) * 256 + 256],
                                                    lhs[h0:h0 + 64, j, :],
                                                    ar[h0:h0 + 64, j].rearrange("p a n -> p (a n)"), start=True, stop=True)
                        last.then_inc(S(name), 1)

                def seed(gq):
                    q = gq % 2
                    need(pe, "xt1", c, 4, gq + 1)
                    need(pe, "akrk", c, 4, gq + 1)
                    for u in range(4):
                        nc.tensor.matmul(psx[q][:, u * P:(u + 1) * P], xT[:, gq, u, :], m.ident[:], start=(u == 0), stop=(u == 3),
                                         skip_group_check=True)
                        last = nc.tensor.matmul(psT[q][:, u * P:(u + 1) * P], m.ident[:], xT[:, gq, u, :], start=(u == 0),
                                                stop=(u == 3), skip_group_check=True)
                    last.then_inc(S("lev_mm"), 1)

                def level_t(gq, l):
                    q = gq % 2
                    need(pe, "x_in", c, 4 * 6, 6 * 2 * (gq // 2) + 2 * (l - 1) + q + 1)
                    for u in range(4):
                        last = nc.tensor.matmul(pst[q][:, u * P:(u + 1) * P], ntrb[:, gq, u, 0, :], x[:, q, u, :],
                                                start=True, stop=True)
                    last.then_inc(S("t_mm"), 1)

                def level_x(gq, l):
                    q = gq % 2
                    need(pe, "t_in", c, 4 * 6, 6 * 2 * (gq // 2) + 2 * (l - 1) + q + 1)
                    need(pe, "xt_in", c, 4 * 7, 7 * 2 * (gq // 2) + 2 * (l - 1) + q + 1)
                    for u in range(4):
                        if l < 6:
                            nc.tensor.matmul(psx[q][:, u * P:(u + 1) * P], xT[:, gq, u, :], tm[:, q, u, :], start=False, stop=False,
                                             skip_group_check=True)
                        last = nc.tensor.matmul(psT[q][:, u * P:(u + 1) * P], tm[:, q, u, :], xT[:, gq, u, :], start=False,
                                                stop=False, skip_group_check=True)
                    last.then_inc(S("lev_mm"), 1)

                def chain_r(j):
                    gq, ub = j // 2, j % 2
                    if j == 0:
                        need(pe, "smprow", c)
                    if j:
                        need(pe, "y", c, KC, j)
                    else:
                        need(pe, "st_zero", c)
                    need(pe, "xt_in", c, 4 * 7, 28 if j > 3 else 14)
                    for hd in range(2):
                        h = slice(64 * hd, 64 * hd + 64)
                        nc.tensor.matmul(m.aux[hd][:, 0:64], ar[h, j, 0, :], st[h, 0:64], start=True, stop=False)
                        last = nc.tensor.matmul(m.aux[hd][:, 0:64], akrk[:, gq, ub + 2 * hd, 0, :], vT[:, j, h], start=False, stop=True)
                    last.then_inc(S("r_mm"), 1)

                def chain_s(j):
                    gq, ub = j // 2, j % 2
                    need(pe, "rs", c, KC, j + 1)
                    for hd in range(2):
                        h = slice(64 * hd, 64 * hd + 64)
                        last = nc.tensor.matmul(m.aux[hd][:, 64:128], xT[:, gq, ub + 2 * hd, :], rs[:, h], start=True, stop=True)
                    last.then_inc(S("sa_mm"), 1)

                def chain_y(j):
                    gq, ub = j // 2, j % 2
                    need(pe, "sa", c, KC, j + 1)
                    if j:
                        need(pe, "y", c, KC, j)
                    elif not first:
                        need(pe, "wkv", c - 1)
                    for hd in range(2):
                        h = slice(64 * hd, 64 * hd + 64)
                        o = m.aux[hd][h, 256:320]
                        nc.tensor.matmul(o, kT[:, j, h], vT[:, j, h], start=True, stop=False)
                        nc.tensor.matmul(o, bT[:, j, h], sa[:, h], start=False, stop=False)
                        last = nc.tensor.matmul(o, m.ident[:, h], st[:, 0:64], start=False, stop=True)
                    last.then_inc(S("st_mm"), 1)
                    for hd in range(2):
                        h = slice(64 * hd, 64 * hd + 64)
                        o = m.aux[hd][:, 128:192]
                        nc.tensor.matmul(o, ar[h, j, 1, :], st[h, 0:64], start=True, stop=False)
                        nc.tensor.matmul(o, akrk[:, gq, ub + 2 * hd, 1, :], vT[:, j, h], start=False, stop=False)
                        last = nc.tensor.matmul(o, ntrb[:, gq, ub + 2 * hd, 1, :], sa[:, h], start=False, stop=True)
                    last.then_inc(S("y_mm"), 1)

                def chain(n):
                    j, step = n // 3, n % 3
                    (chain_r, chain_s, chain_y)[step](j)

                for half in range(2):
                    products(2 * half)
                    products(2 * half + 1)
                    seed(2 * half)
                    seed(2 * half + 1)
                    n = 0
                    for l in range(1, 7):
                        for stage in (level_t, level_x):
                            stage(2 * half, l)
                            stage(2 * half + 1, l)
                            if half:
                                chain(n)
                                n += 1
                for n in range(12, 24):
                    chain(n)
                need(pe, "y", c, KC, KC)
                nc.tensor.transpose(m.aux[1][:, 384:512], st[:], m.ident[:]).then_inc(S("wkv_t"), 1)
                need(pe, "yn", c)
                for j in range(KC):
                    last = nc.tensor.transpose(m.acc[0][:, j // 4, (j % 4) * P:(j % 4 + 1) * P],
                                               y[:, 2 * j:2 * j + 2, :].rearrange("p h n -> p (h n)"), m.ident[:])
                last.then_inc(S("yT_t"), 1)
            pe.wait_ge(S("masks_in"), 16)
            loop(pe, body)

        @block.scalar
        def _(act):
            def body(c, first):
                need(act, "in_k", c, 16, 16)
                if not first:
                    act.wait_ge(S("mixed_out"), c * 16)
                    need(act, "bonus_mm", c - 1)
                nc.scalar.activation(t1[:], k[:], ACT.Square, scale=col(V_KK, c)).then_inc(S("sq"), 1)
                need(act, "ss_mm", c)
                nc.scalar.activation(as3(t2[:]), m.acc[0][:, :, 0:G], ACT.Sqrt).then_inc(S("nrm"), 1)
                need(act, "lc", c)
                nc.scalar.activation(t1[:, 0:SEQ], cum[:], ACT.Exp).then_inc(S("ep"), 1)
                need(act, "lx", c)
                nc.scalar.activation(lw[:, 0:SEQ], lw[:, 0:SEQ], ACT.Exp).then_inc(S("ex"), 1)
                need(act, "smp_w", c)
                nc.scalar.activation(smp[:, 1, :], smp[:, 1, :], ACT.Exp).then_inc(S("smp_w2"), 1)
                need(act, "kk_done", c)
                need(act, "bonus_mm", c)
                nc.scalar.activation(t3[:, 0:SEQ], cum[:], ACT.Exp, scale=-1.0).then_inc(S("en"), 1)
                need(act, "fac0", c, 2, 2)
                nc.scalar.activation(fac[:], fac[:], ACT.Exp).then_inc(S("fac"), 1)
                need(act, "smp_t", c)
                if not first:
                    act.wait_ge(S("smp_out"), c * 16)
                nc.scalar.activation(smprow[:], m.aux[0][0:48, 0:P], ACT.Copy).then_inc(S("smprow"), 1)
                for name, dst, q in (("vT", vT, 0), ("bT", bT, 1), ("kT", kT, 0)):
                    need(act, name + "_t", c)
                    nc.scalar.activation(dst[:].rearrange("p (a j) n -> p a (j n)", a=2), m.acc[q][:, 0:2, :],
                                         ACT.Copy).then_inc(S(name), 1)
                ch = [0]

                def chain_in(n):
                    j, step = n // 3, n % 3
                    if step == 0:
                        need(act, "r_mm", c, KC, j + 1)
                        nc.scalar.activation(rs[:].rearrange("p (h n) -> p h n", h=2), m.aux2[:, :, 0:64], ACT.Copy).then_inc(S("rs"), 1)
                    elif step == 1:
                        need(act, "sa_mm", c, KC, j + 1)
                        nc.scalar.activation(sa[:].rearrange("p (h n) -> p h n", h=2), m.aux2[:, :, 64:128], ACT.Copy).then_inc(S("sa"), 1)
                    else:
                        need(act, "y_mm", c, KC, j + 1)
                        for h in (slice(0, 64), slice(64, P)):
                            last = nc.scalar.activation(st[h, 0:64], m.aux2[h, h.start // 64, 256:320], ACT.Copy,
                                                        scale=fac[h, j:j + 1])
                        last.then_inc(S("st_in"), 1)
                        nc.scalar.activation(y[:, 2 * j:2 * j + 2, :], m.aux2[:, :, 128:192],
                                             ACT.Copy).then_inc(S("y"), 1)

                for half in range(2):
                    def x_in(q, l):
                        if l < 6:
                            nc.scalar.activation(x[:, q].rearrange("p u n -> p (u n)"), psx[q], ACT.Copy).then_inc(S("x_in"), 1)
                        nc.scalar.activation(xT[:, 2 * half + q].rearrange("p u n -> p (u n)"), psT[q],
                                             ACT.Copy).then_inc(S("xt_in"), 1)

                    for q in range(2):
                        need(act, "lev_mm", c, 4 * 7, 14 * half + q + 1)
                        x_in(q, 0)
                    for l in range(1, 7):
                        for q in range(2):
                            if half and q == 0:
                                chain_in(2 * (l - 1))
                            need(act, "lev_mm", c, 4 * 7, 14 * half + 2 * l + q + 1)
                            x_in(q, l)
                        if half:
                            chain_in(2 * (l - 1) + 1)
                for n in range(12, 24):
                    chain_in(n)
                need(act, "wkv_t", c)
                if not first:
                    act.wait_ge(S("wkv_out"), c * 16)
                nc.scalar.activation(wkv[:], m.aux[1][0:64, 384:512], ACT.Copy).then_inc(S("wkv"), 1)
                need(act, "yc", c)
                nc.scalar.activation(ysq[:, 0:SEQ], y[:].rearrange("p h n -> p (h n)"), ACT.Square).then_inc(S("ysq"), 1)
                need(act, "var", c)
                nc.scalar.activation(stat2[:], stat[:], ACT.Sqrt, bias=epst[:, 0:1], scale=1.0 / 64).then_inc(S("std"), 1)
                need(act, "yT_t", c)
                nc.scalar.activation(t1[:, 0:SEQ].rearrange("p (a n) -> p a n", a=2), m.acc[0][:, 0:2, :], ACT.Identity,
                                     bias=col(V_GNB, c), scale=col(V_GNG, c)).then_inc(S("yT_in"), 1)
            act.wait_ge(S("consts"), 5)
            loop(act, body)

        @block.vector
        def _(dve):
            dve.wait_ge(S("masks_in"), 16)
            nc.vector.memset(epst[:], GN_EPS).then_inc(S("consts"), 1)
            nc.vector.memset(st[:], 0.0).then_inc(S("consts"), 1)
            nc.vector.memset(smp[:], 0.0).then_inc(S("consts"), 1)
            nc.vector.tensor_scalar(omka[:], m.vecs[:, V_KA * KC:(V_KA + 1) * KC], -1.0, 1.0, ALU.mult, ALU.add).then_inc(S("consts"), 1)
            nc.vector.tensor_copy(reset[:].rearrange(chunks, j=KC),
                                  consts[:, C_RESET:C_RESET + P].unsqueeze(1).to_broadcast([P, KC, P])).then_inc(S("consts"), 1)
            dve.wait_ge(S("consts"), 5)

            def body(c, first):
                V = nc.vector
                need(dve, "in_lw", c, 16, 16)
                V.tensor_tensor_scan(cum[:], reset[:], lw[:, 0:SEQ], 0.0, ALU.mult, ALU.add).then_inc(S("scan"), 1)
                if not first:
                    need(dve, "smp_t", c - 1)
                V.tensor_copy(smp[:, 1, :], lw[:, SEQ:T]).then_inc(S("smp_w"), 1)
                need(dve, "scan", c)
                c3 = cum[:].rearrange(chunks, j=KC)
                if not first:
                    need(dve, "st_in", c - 1, KC, KC)
                V.tensor_tensor(fac[:, 0:KC - 1], c3[:, 0:KC - 1, P - 1], c3[:, 1:KC, 63], ALU.add)
                V.tensor_copy(fac[:, KC - 1:KC], c3[:, KC - 1, P - 1:P]).then_inc(S("fac0"), 1)
                need(dve, "fac0", c, 2, 1)
                V.tensor_tensor(fac[:], fac[:], c3[:, :, 63], ALU.subtract).then_inc(S("fac0"), 1)
                V.tensor_copy(stat2[:, 0:KC], c3[:, :, 63]).then_inc(S("mid"), 1)
                need(dve, "mid", c)
                need(dve, "fac0", c, 2, 2)
                V.tensor_tensor(c3, c3, stat2[:, 0:KC].unsqueeze(2).to_broadcast([P, KC, P]), ALU.subtract).then_inc(S("lc"), 1)
                need(dve, "lc", c)
                V.tensor_tensor(lw[:, 0:SEQ], cum[:], lw[:, 0:SEQ], ALU.subtract).then_inc(S("lx"), 1)
                need(dve, "in_a", c, 16, 16)
                need(dve, "in_k", c, 16, 16)
                V.tensor_scalar(k2[:], a[:], col(V_KA, c), omka[:, bass.ds(c, 1)], ALU.mult, ALU.add).then_inc(S("k2a"), 1)
                V.tensor_scalar(kk[:], k[:], col(V_KK, c), None, ALU.mult).then_inc(S("kkf"), 1)
                need(dve, "k2a", c)
                V.tensor_tensor(k2[:], k2[:], k[:], ALU.mult).then_inc(S("k2"), 1)
                need(dve, "in_r", c, 16, 16)
                need(dve, "k2", c)
                if not first:
                    need(dve, "kt", c - 1)
                V.scalar_tensor_tensor(t3[:], r[:], col(V_RK, c), k2[:], ALU.mult, ALU.mult).then_inc(S("rk"), 1)
                need(dve, "nrm", c)
                V.tensor_scalar_max(t2[:], t2[:], 1e-12).then_inc(S("nrm2"), 1)
                need(dve, "nrm2", c)
                V.reciprocal(t2[:], t2[:]).then_inc(S("rinv"), 1)
                need(dve, "rinv", c)
                need(dve, "kkf", c)
                V.tensor_tensor(kk[:], kk[:], t2[:], ALU.mult).then_inc(S("kk_done"), 1)
                need(dve, "kk_done", c)
                V.tensor_tensor(kb[:], kk[:], a[:], ALU.mult).then_inc(S("kb"), 1)
                need(dve, "ex", c)
                V.scalar_tensor_tensor(ar[:, :, 0, :], kk[:, 0:SEQ].rearrange(chunks, j=KC), -1.0,
                                       lw[:, 0:SEQ].rearrange(chunks, j=KC), ALU.mult, ALU.mult).then_inc(S("at"), 1)
                need(dve, "ep", c)
                V.tensor_tensor(ar[:, :, 1, :], r[:, 0:SEQ].rearrange(chunks, j=KC), t1[:, 0:SEQ].rearrange(chunks, j=KC),
                                ALU.mult).then_inc(S("rt"), 1)
                need(dve, "en", c)
                need(dve, "kb", c)
                V.tensor_tensor(bt[:].rearrange("p j n -> p (j n)"), kb[:, 0:SEQ], t3[:, 0:SEQ], ALU.mult).then_inc(S("bt"), 1)
                V.tensor_tensor(kt[:].rearrange("p j n -> p (j n)"), k2[:, 0:SEQ], t3[:, 0:SEQ], ALU.mult).then_inc(S("kt"), 1)
                need(dve, "bonus_mm", c)
                need(dve, "in_v", c, 16, 16)
                V.tensor_tensor(as3(bonus[:]), m.acc[1][:, :, 0:G], as3(v[:]), ALU.mult).then_inc(S("bonus"), 1)
                for i, src in ((0, r), (2, k2), (3, v), (5, kb)):
                    V.tensor_copy(smp[:, i, :], src[:, SEQ:T])
                need(dve, "in_g", c, 16, 16)
                need(dve, "bonus", c)
                V.tensor_copy(gs[:, bass.ds(c, 1), :].rearrange("p a n -> p (a n)"), g[:, SEQ:T])
                V.tensor_copy(bs[:, bass.ds(c, 1), :].rearrange("p a n -> p (a n)"), bonus[:, SEQ:T]).then_inc(S("gs"), 1)
                need(dve, "smp_w2", c)
                V.tensor_scalar(smp[:, 4, :], kk[:, SEQ:T], -1.0, None, ALU.mult).then_inc(S("smp_v"), 1)
                need(dve, "fac", c)
                V.memset(st[:, 0:64], 0.0).then_inc(S("st_zero"), 1)

                mask4 = upper.unsqueeze(1).to_broadcast([P, 4, 2 * P])
                for half in range(2):
                    for gq in (2 * half, 2 * half + 1):
                        q = gq % 2
                        need(dve, "ntrb_mm", c, 4, gq + 1)
                        V.tensor_tensor(ntrb[:, gq].rearrange("p u a n -> p u (a n)"),
                                        m.acc[q][:, 0:2, :].rearrange("p b (u n) -> p (b u) n", u=2), mask4,
                                        ALU.mult).then_inc(S("ntrb"), 1)
                        need(dve, "akrk_mm", c, 4, gq + 1)
                        V.tensor_tensor(akrk[:, gq].rearrange("p u a n -> p u (a n)"),
                                        m.acc[q][:, 0:2, :].rearrange("p b (u n) -> p (b u) n", u=2), mask4,
                                        ALU.mult).then_inc(S("akrk"), 1)
                    for l in range(1, 7):
                        for q in range(2):
                            need(dve, "t_mm", c, 4 * 6, 12 * half + 2 * (l - 1) + q + 1)
                            V.tensor_tensor(tm[:, q], pst[q].rearrange("p (u n) -> p u n", u=4), lev(l), ALU.mult).then_inc(S("t_in"), 1)
                need(dve, "y", c, KC, KC)
                V.tensor_reduce(stat[:], y[:], AX.X, ALU.add).then_inc(S("ysum"), 1)
                need(dve, "ysum", c)
                V.tensor_scalar(stat2[:], stat[:], 1.0 / 64, None, ALU.mult).then_inc(S("ymean"), 1)
                need(dve, "ymean", c)
                V.tensor_tensor(y[:], y[:], stat2[:].unsqueeze(2).to_broadcast([P, 16, 64]), ALU.subtract).then_inc(S("yc"), 1)
                need(dve, "ysq", c)
                V.tensor_reduce(stat[:], ysq[:, 0:SEQ].rearrange("p (h n) -> p h n", n=64), AX.X, ALU.add).then_inc(S("var"), 1)
                need(dve, "std", c)
                V.reciprocal(stat[:], stat2[:]).then_inc(S("rstd"), 1)
                need(dve, "rstd", c)
                V.tensor_tensor(y[:], y[:], stat[:].unsqueeze(2).to_broadcast([P, 16, 64]), ALU.mult).then_inc(S("yn"), 1)
                need(dve, "yT_in", c)
                V.tensor_tensor(t1[:, 0:SEQ], t1[:, 0:SEQ], bonus[:, 0:SEQ], ALU.add).then_inc(S("plus"), 1)
                need(dve, "plus", c)
                V.tensor_tensor(t1[:, 0:SEQ], t1[:, 0:SEQ], g[:, 0:SEQ], ALU.mult).then_inc(S("gated"), 1)
            loop(dve, body)


def sample_scan_phase(m, bs, gs):
    nc, io = m.nc, m.io
    with ExitStack() as ctx:
        def sb(name, shape, dt=F32):
            return ctx.enter_context(nc.sbuf_tensor(name, shape, dt))

        sems = {}

        def S(name):
            if name not in sems:
                sems[name] = m.phase_sem(name)
            return sems[name]

        vec = sb("sample_vecs", [P, 6, 64])
        st = sb("sample_state", [P, 64, 64])
        tmp = sb("sample_tmp", [P, 64, 64])
        sa, y, y2 = sb("sample_sa", [P, 64]), sb("sample_y", [P, 64]), sb("sample_y2", [P, 64])
        s1, s2, eps = sb("sum1", [P, 1]), sb("sum2", [P, 1]), sb("eps_gn_sample", [P, 1])
        yr = sb("sample_rows", [NS, D])
        yT = sb("sample_cols", [P, KC, NS])
        r, w, k, v, a, b = range(6)
        block = ctx.enter_context(nc.Block())

        def over_i(n):
            return vec[:, n, :].unsqueeze(1).to_broadcast([P, 64, 64])

        def over_j(t):
            return t.unsqueeze(2).to_broadcast([P, 64, 64])

        @block.sync
        def _(sp):
            nc.sync.dma_start(st[:], io["state_wkv"][0].rearrange("b h i j -> (b h) i j")).then_inc(S("in"), 16)
            nc.sync.dma_start(vec[:], m.srows.rearrange("v b (h n) -> (b h) v n", n=64)).then_inc(S("in"), 16)
            sp.wait_ge(S("state"), 3)
            nc.sync.dma_start(io["wkv_sample"][0].rearrange("b h i j -> (b h) i j"), st[:]).then_inc(S("state_out"), 16)
            sp.wait_ge(S("yn"), 1)
            nc.sync.dma_start(m.yrows.rearrange("b (h n) -> (b h) n", n=64), y2[:]).then_inc(S("y_out"), 16)
            sp.wait_ge(S("y_out"), 16)
            nc.sync.dma_start(yr[:], m.yrows).then_inc(S("y_back"), 16)
            sp.wait_ge(S("out"), 4)
            nc.sync.dma_start(m.scr[S_MIX, :, :, SEQ:T].rearrange("c p n -> p c n"), yT[:]).then_inc(S("mixed"), 16)
            sp.wait_ge(S("mixed"), 16)
            sp.wait_ge(S("state_out"), 16)

        @block.vector
        def _(dve):
            V = nc.vector
            V.memset(eps[:], GN_EPS).then_inc(S("eps"), 1)
            dve.wait_ge(S("in"), 32)
            V.tensor_tensor(tmp[:], st[:], over_i(a), ALU.mult).then_inc(S("sa"), 1)
            dve.wait_ge(S("sa"), 1)
            V.tensor_reduce(sa[:], tmp[:], AX.X, ALU.add).then_inc(S("sa"), 1)
            V.tensor_tensor(st[:], st[:], over_i(w), ALU.mult).then_inc(S("state"), 1)
            dve.wait_ge(S("sa"), 2)
            V.tensor_tensor(tmp[:], over_j(sa[:]), over_i(b), ALU.mult).then_inc(S("ab"), 1)
            dve.wait_ge(S("ab"), 1)
            dve.wait_ge(S("state"), 1)
            V.tensor_tensor(st[:], st[:], tmp[:], ALU.add).then_inc(S("state"), 1)
            dve.wait_ge(S("state"), 2)
            V.tensor_tensor(tmp[:], over_j(vec[:, v, :]), over_i(k), ALU.mult).then_inc(S("vk"), 1)
            dve.wait_ge(S("vk"), 1)
            V.tensor_tensor(st[:], st[:], tmp[:], ALU.add).then_inc(S("state"), 1)
            dve.wait_ge(S("state"), 3)
            V.tensor_tensor(tmp[:], st[:], over_i(r), ALU.mult).then_inc(S("sr"), 1)
            dve.wait_ge(S("sr"), 1)
            V.tensor_reduce(y[:], tmp[:], AX.X, ALU.add).then_inc(S("y"), 1)
            dve.wait_ge(S("y"), 1)
            V.tensor_reduce(s1[:], y[:], AX.X, ALU.add).then_inc(S("gn"), 1)
            dve.wait_ge(S("gn"), 1)
            V.tensor_scalar(s1[:], s1[:], -1.0 / 64, None, ALU.mult).then_inc(S("gn"), 1)
            dve.wait_ge(S("gn"), 2)
            V.tensor_scalar(y[:], y[:], s1[:, 0:1], None, ALU.add).then_inc(S("gn"), 1)
            dve.wait_ge(S("gn"), 3)
            V.tensor_tensor(y2[:], y[:], y[:], ALU.mult).then_inc(S("gn"), 1)
            dve.wait_ge(S("gn"), 4)
            V.tensor_reduce(s2[:], y2[:], AX.X, ALU.add).then_inc(S("gn"), 1)
            dve.wait_ge(S("std"), 1)
            V.reciprocal(s1[:], s2[:]).then_inc(S("gn"), 1)
            dve.wait_ge(S("gn"), 6)
            V.tensor_scalar(y2[:], y[:], s1[:, 0:1], None, ALU.mult).then_inc(S("yn"), 1)
            dve.wait_ge(S("turned"), 1)

            def per_channel(vi):
                return m.vecs[:, vi * KC:(vi + 1) * KC].unsqueeze(2).to_broadcast([P, KC, NS])

            V.tensor_tensor(yT[:], m.aux[0][:, 0:KC * NS].rearrange("p (c n) -> p c n", c=KC), per_channel(V_GNG),
                            ALU.mult).then_inc(S("out"), 1)
            for n, other, op in ((1, per_channel(V_GNB), ALU.add), (2, bs[:], ALU.add), (3, gs[:], ALU.mult)):
                dve.wait_ge(S("out"), n)
                V.tensor_tensor(yT[:], yT[:], other, op).then_inc(S("out"), 1)

        @block.scalar
        def _(act):
            act.wait_ge(S("eps"), 1)
            act.wait_ge(S("gn"), 5)
            nc.scalar.activation(s2[:], s2[:], ACT.Sqrt, bias=eps[:, 0:1], scale=1.0 / 64).then_inc(S("std"), 1)

        @block.tensor
        def _(pe):
            pe.wait_ge(S("y_back"), 16)
            for c in range(KC):
                last = nc.tensor.transpose(m.aux[0][:, c * NS:(c + 1) * NS], yr[:, c * P:(c + 1) * P], m.ident[0:NS, 0:NS])
            last.then_inc(S("turned"), 1)


class Piece:

    def __init__(self, m, ctx, tag):
        self.m, self.nc, self.ctx, self.tag, self.sems = m, m.nc, ctx, tag, {}

    def sb(self, name, shape, dt=F32):
        return self.ctx.enter_context(self.nc.sbuf_tensor(f"{self.tag}_{name}", shape, dt))

    def S(self, name):
        if name not in self.sems:
            self.sems[name] = self.m.phase_sem(f"{self.tag}_{name}")
        return self.sems[name]


class Norm(Piece):

    def __init__(self, m, ctx, tag, z, which, tmp):
        super().__init__(m, ctx, tag)
        self.z, self.which, self.tmp = z, which, tmp
        self.rstd = self.sb("rstd", [P, T])

    def tensor(self, pe):
        m, nc = self.m, self.nc
        for k in range(KC):
            for g in range(NG):
                last = nc.tensor.matmul(m.acc[0][:, g, 0:G], m.mean[:], self.z[:, k, g * G:(g + 1) * G],
                                        start=(k == 0), stop=(k == KC - 1))
        last.then_inc(self.S("mean"), 1)
        for k in range(KC):
            pe.wait_ge(self.S("squared"), k + 1)
            for g in range(NG):
                last = nc.tensor.matmul(m.acc[1][:, g, 0:G], m.mean[:], self.tmp[:, k % 2, g * G:(g + 1) * G],
                                        start=(k == 0), stop=(k == KC - 1))
            last.then_inc(self.S("var"), 1)

    def vector(self, dve):
        m, nc, z = self.m, self.nc, self.z
        dve.wait_ge(self.S("mean"), 1)
        for k in range(KC):
            nc.vector.tensor_tensor(as3(z[:, k, :]), as3(z[:, k, :]), acc_view(m, 0), ALU.subtract).then_inc(self.S("centred"), 1)
        dve.wait_ge(self.S("std"), 1)
        nc.vector.reciprocal(self.rstd[:], self.rstd[:]).then_inc(self.S("rstd"), 1)
        dve.wait_ge(self.S("rstd"), 1)
        for k in range(KC):
            nc.vector.tensor_tensor(z[:, k, :], z[:, k, :], self.rstd[:], ALU.mult).then_inc(self.S("scaled"), 1)

    def scalar(self, act):
        m, nc, z = self.m, self.nc, self.z
        for k in range(KC):
            act.wait_ge(self.S("centred"), k + 1)
            if k >= 2:
                act.wait_ge(self.S("var"), k - 1)
            nc.scalar.activation(self.tmp[:, k % 2, :], z[:, k, :], ACT.Square).then_inc(self.S("squared"), 1)
        act.wait_ge(self.S("var"), KC)
        nc.scalar.activation(as3(self.rstd[:]), acc_view(m, 1), ACT.Sqrt, bias=m.eps[:, 0:1]).then_inc(self.S("std"), 1)
        for k in range(KC):
            act.wait_ge(self.S("scaled"), k + 1)
            nc.scalar.activation(z[:, k, :], z[:, k, :], ACT.Identity, bias=m.vec(V_LNB + self.which, k),
                                 scale=m.vec(V_LNG + self.which, k)).then_inc(self.S("x"), 1)


class Modulate(Piece):

    def __init__(self, m, ctx, tag, x, scale, shift, xh, xl, tmp, alpha=False):
        super().__init__(m, ctx, tag)
        self.x, self.scale, self.shift, self.xh, self.xl, self.tmp, self.alpha = x, scale, shift, xh, xl, tmp, alpha

    def vector(self, dve, ready):
        m, nc = self.m, self.nc
        for k in range(KC):
            ready(k)
            if k >= 2:
                dve.wait_ge(self.S("lo"), k - 1)
            t, s = self.tmp[:, k % 2, :], slice(SEQ, T)
            nc.vector.tensor_tensor(t[:, s], self.x[:, k, s], m.mods[:, self.scale, k, 1:], ALU.mult).then_inc(self.S("s1"), 1)
            nc.vector.tensor_scalar(t[:, 0:SEQ], self.x[:, k, 0:SEQ], m.mod(self.scale, k), m.mod(self.shift, k),
                                    ALU.mult, ALU.add)
            dve.wait_ge(self.S("s1"), k + 1)
            nc.vector.tensor_tensor(t[:, s], t[:, s], m.mods[:, self.shift, k, 1:], ALU.add).then_inc(self.S("h"), 1)
            dve.wait_ge(self.S("h"), k + 1)
            nc.vector.tensor_copy(self.xh[:, k, :], t).then_inc(self.S("hi"), 1)

    def gpsimd(self, pool):
        for k in range(KC):
            pool.wait_ge(self.S("hi"), k + 1)
            self.nc.gpsimd.tensor_tensor(self.xl[:, k, :], self.tmp[:, k % 2, :], self.xh[:, k, :].bitcast(F32),
                                         ALU.subtract).then_inc(self.S("lo"), 1)

    def scalar(self, act):
        for k in range(KC):
            act.wait_ge(self.S("h"), k + 1)
            self.nc.scalar.activation(self.x[:, k, :], self.x[:, k, :], ACT.Copy, scale=ALPHA).then_inc(self.S("alpha"), 1)


def job_loads(m, sp, w, s, col0=0):
    with sp.Fori(0, KC // 2) as i:
        for p in range(2):
            ring_load(m, sp, slab_at(w, i * 2 + (col0 + p)), i * 2 + (s + p), p)


def job_lows(m, pool, s, n=KC):
    with pool.Fori(0, n // 2) as i:
        for p in range(2):
            ring_low(m, pool, i * 2 + (s + p), p)


def job_muls(m, pe, s, xh, xl):
    with pe.Fori(0, KC // 2) as i:
        for p in range(2):
            ring_mul(m, pe, i * 2 + (s + p), p, xh, xl)


def add_gated(m, dve, z, gate, c, s, p, sums, tmp8):
    nc = m.nc
    dve.wait_ge(m.mm_done, s + 1)
    zc = z[:, bass.ds(c, 1), :].rearrange("p a t -> p (a t)")
    sg = m.mods[:, gate, bass.ds(c, 1), 1:].rearrange("p a n -> p (a n)")
    pg = m.mods[:, gate, bass.ds(c, 1), 0:1].rearrange("p a n -> p (a n)")
    nc.vector.tensor_tensor(tmp8[:], m.acc[p][:, 2, G - NS:G], sg, ALU.mult).then_inc(sums, 1)
    nc.vector.scalar_tensor_tensor(zc[:, 0:2 * G].rearrange("p (g n) -> p g n", g=2), m.acc[p][:, 0:2, 0:G], pg,
                                   zc[:, 0:2 * G].rearrange("p (g n) -> p g n", g=2), ALU.mult, ALU.add)
    nc.vector.scalar_tensor_tensor(zc[:, 2 * G:SEQ], m.acc[p][:, 2, 0:G - NS], pg, zc[:, 2 * G:SEQ],
                                   ALU.mult, ALU.add).then_inc(m.acc_free[p], 2)


def add_sample(m, dve, z, c, sums, tmp8, n):
    dve.wait_ge(sums, n)
    zs = z[:, bass.ds(c, 1), SEQ:T].rearrange("p a t -> p (a t)")
    m.nc.vector.tensor_tensor(zs, zs, tmp8[:], ALU.add).then_inc(sums, 1)
    dve.wait_ge(sums, n + 1)


def output_phase(m, z, layer, gate):
    nc, io = m.nc, m.io
    with ExitStack() as ctx:
        pc = Piece(m, ctx, f"out{layer}")
        xh, xl = pc.sb("hi", [P, KC, T], F32R), pc.sb("lo", [P, KC, T], F32R)
        tmp, tmp8 = pc.sb("in", [P, 2, T]), pc.sb("tmp8", [P, NS])
        w = io["a_w_o" if layer == 0 else "b_w_o"][0]
        s0 = m.slabs
        S = pc.S
        block = ctx.enter_context(nc.Block())

        @block.sync
        def _(sp):
            ring_load(m, sp, slab_of(w, 0), s0, 0)
            ring_load(m, sp, slab_of(w, 1), s0 + 1, 1)
            for k in range(KC):
                if k >= 2:
                    sp.wait_ge(S("lo"), k - 1)
                nc.sync.dma_start(tmp[:, k % 2, :], m.scr[S_MIX, k]).then_inc(S(f"in{k % 2}"), 16)
            with sp.Fori(1, KC // 2) as i:
                for p in range(2):
                    ring_load(m, sp, slab_at(w, i * 2 + p), i * 2 + (s0 + p), p)

        @block.gpsimd
        def _(pool):
            nc.gpsimd.dma_start(z[:], m.xt.rearrange("c p t -> p c t")).then_inc(S("x"), 16)
            for k in range(KC):
                pool.wait_ge(S("hi"), k + 1)
                nc.gpsimd.tensor_tensor(xl[:, k, :], tmp[:, k % 2, :], xh[:, k, :].bitcast(F32), ALU.subtract).then_inc(S("lo"), 1)
            job_lows(m, pool, s0)

        @block.tensor
        def _(pe):
            pe.wait_ge(S("lo"), KC)
            job_muls(m, pe, s0, xh, xl)

        @block.scalar
        def _(act):
            ring_high(m, act, s0, 0, landed_at(s0))
            ring_high(m, act, s0 + 1, 1, landed_at(s0 + 1))
            act.wait_ge(S("x"), 16)
            for k in range(KC):
                nc.scalar.activation(z[:, k, :], z[:, k, :], ACT.Copy, scale=ALPHA).then_inc(S("alpha"), 1)
            with act.Fori(0, KC // 2 - 1) as i:
                for p in range(2):
                    ring_high(m, act, i * 2 + (s0 + 2 + p), p, i * 16 + landed_at(s0 + 2 + p))

        @block.vector
        def _(dve):
            for k in range(KC):
                dve.wait_ge(S(f"in{k % 2}"), 16 * (k // 2 + 1))
                nc.vector.tensor_copy(xh[:, k, :], tmp[:, k % 2, :]).then_inc(S("hi"), 1)
            dve.wait_ge(S("alpha"), KC)
            with dve.Fori(0, KC // 2) as i:
                for p in range(2):
                    add_gated(m, dve, z, gate, i * 2 + p, i * 2 + (s0 + p), p, S("sum8"), tmp8)
                    add_sample(m, dve, z, i * 2 + p, S("sum8"), tmp8, i * 4 + (2 * p + 1))
        m.slabs = s0 + KC


def mlp_phase(m, z, layer):
    nc, io = m.nc, m.io
    with ExitStack() as ctx:
        pc = Piece(m, ctx, f"mlp{layer}")
        tmp = pc.sb("tmp", [P, 2, T])
        xh, xl = pc.sb("hi", [P, KC, T], F32R), pc.sb("lo", [P, KC, T], F32R)
        hh, hl = pc.sb("hid_hi", [P, KC, T], F32R), pc.sb("hid_lo", [P, KC, T], F32R)
        tmp8 = pc.sb("tmp8", [P, NS])
        norm = Norm(m, ctx, f"norm{2 * layer}", z, 2 * layer, tmp)
        mod = Modulate(m, ctx, f"modf{layer}", z, 6 * layer + M_SCF, 6 * layer + M_SHF, xh, xl, tmp, alpha=True)
        gate = 6 * layer + M_GTF
        w1, w2 = io["ffn_w1"][layer], io["ffn_w2"][layer]
        NF = 4
        s0, e0 = m.slabs, m.staged
        S = pc.S
        block = ctx.enter_context(nc.Block())

        @block.sync
        def _(sp):
            for f in range(NF):
                job_loads(m, sp, w1, s0 + 16 * f, f * KC)
                job_loads(m, sp, w2[f * D:(f + 1) * D, :], s0 + 16 * f + 8)

        @block.gpsimd
        def _(pool):
            ring_low(m, pool, s0, 0)
            ring_low(m, pool, s0 + 1, 1)
            mod.gpsimd(pool)
            job_lows(m, pool, s0 + 2, 16 * NF - 2)

        @block.tensor
        def _(pe):
            norm.tensor(pe)
            pe.wait_ge(mod.S("lo"), KC)
            with pe.Fori(0, NF) as f:
                with pe.Fori(0, KC // 2) as i:
                    for p in range(2):
                        ring_mul(m, pe, f * 16 + (i * 2 + (s0 + p)), p, xh, xl)
                pe.wait_ge(S("hid"), f * 8 + 8)
                for p in range(2):
                    ring_mul(m, pe, f * 16 + (s0 + 8 + p), p, hh, hl)
                with pe.Fori(1, KC // 2) as i:
                    for p in range(2):
                        ring_mul(m, pe, f * 16 + (i * 2 + (s0 + 8 + p)), p, hh, hl)

        @block.scalar
        def _(act):
            ring_high(m, act, s0, 0, landed_at(s0))
            ring_high(m, act, s0 + 1, 1, landed_at(s0 + 1))
            norm.scalar(act)
            mod.scalar(act)

            def hidden(s, p, e):
                act.wait_ge(m.mm_done, s + 1)
                act.wait_ge(m.t_free, e + 1)
                nc.scalar.activation(as3(tmp[:, p, :]), acc_view(m, p), ACT.Relu).then_inc(m.acc_free[p], 2)

            def first_block(f, base, n):
                with act.Fori(0, KC // 2) as i:
                    for p in range(2):
                        s = f * 16 + (i * 2 + (s0 + p))
                        ring_high(m, act, s + 2, p, f * 128 + (i * 16 + landed_at(s0 + 2 + p)))
                        hidden(s, p, f * 8 + (i * 2 + (e0 + p)))

            with act.Fori(0, NF - 1) as f:
                first_block(f, None, None)
                with act.Fori(0, KC // 2) as i:
                    for p in range(2):
                        ring_high(m, act, f * 16 + (i * 2 + (s0 + 10 + p)), p, f * 128 + (i * 16 + landed_at(s0 + 10 + p)))
            f = NF - 1
            first_block(f, None, None)
            with act.Fori(0, KC // 2 - 1) as i:
                for p in range(2):
                    ring_high(m, act, i * 2 + (s0 + 16 * f + 10 + p), p, i * 16 + landed_at(s0 + 16 * f + 10 + p))

        @block.vector
        def _(dve):
            norm.vector(dve)
            mod.vector(dve, lambda k: dve.wait_ge(norm.S("x"), k + 1))
            dve.wait_ge(mod.S("alpha"), KC)
            dve.wait_ge(mod.S("lo"), KC)
            with dve.Fori(0, NF) as f:
                with dve.Fori(0, KC // 2) as i:
                    for p in range(2):
                        c, n = i * 2 + p, f * 8 + (i * 2 + p)
                        t = tmp[:, p, :]
                        dve.wait_ge(m.acc_free[p], f * 16 + (i * 2 + (s0 + 2)))
                        nc.vector.tensor_tensor(t, t, t, ALU.mult).then_inc(S("sq"), 1)
                        dve.wait_ge(S("sq"), n + 1)
                        hc = hh[:, bass.ds(c, 1), :].rearrange("p a t -> p (a t)")
                        lc = hl[:, bass.ds(c, 1), :].rearrange("p a t -> p (a t)")
                        nc.vector.tensor_copy(hc, t).then_inc(S("hid_hi"), 1)
                        dve.wait_ge(S("hid_hi"), n + 1)
                        nc.vector.tensor_tensor(lc, t, hc.bitcast(F32), ALU.subtract).then_inc(S("hid"), 1)
                        dve.wait_ge(S("hid"), n + 1)
                        dve.sem_inc(m.t_free, 1)
                with dve.Fori(0, KC // 2) as i:
                    for p in range(2):
                        s = f * 16 + (i * 2 + (s0 + 8 + p))
                        add_gated(m, dve, z, gate, i * 2 + p, s, p, S("sum8"), tmp8)
                        add_sample(m, dve, z, i * 2 + p, S("sum8"), tmp8, f * 16 + (i * 4 + (2 * p + 1)))
        m.slabs = s0 + 16 * NF
        m.staged = e0 + KC * NF


def qkv_phase(m, z):
    nc, io = m.nc, m.io
    with ExitStack() as ctx:
        pc = Piece(m, ctx, "qkv")
        tmp = pc.sb("tmp", [P, 2, T])
        stage = pc.sb("stage", [P, 2, T])
        xh, xl = pc.sb("hi", [P, KC, T], F32R), pc.sb("lo", [P, KC, T], F32R)
        norm = Norm(m, ctx, "norm1", z, 1, tmp)
        mods = [Modulate(m, ctx, "modkv", z, M_KVSC, M_KVSH, xh, xl, tmp),
                Modulate(m, ctx, "modq", z, 6 + M_SCM, 6 + M_SHM, xh, xl, tmp)]
        jobs = [(io["kv_w_k"], S_K), (io["kv_w_v"], S_V), (io["b_w_q"][0], S_R)]
        s0 = m.slabs
        S = pc.S
        block = ctx.enter_context(nc.Block())

        @block.sync
        def _(sp):
            for j, (w, _) in enumerate(jobs):
                job_loads(m, sp, w, s0 + KC * j)

        @block.gpsimd
        def _(pool):
            ring_low(m, pool, s0, 0)
            ring_low(m, pool, s0 + 1, 1)
            mods[0].gpsimd(pool)
            job_lows(m, pool, s0 + 2, 2 * KC)
            mods[1].gpsimd(pool)
            job_lows(m, pool, s0 + 2 + 2 * KC, KC - 2)
            for k in range(KC):
                pool.wait_ge(norm.S("x"), k + 1)
            nc.gpsimd.dma_start(m.xt.rearrange("c p t -> p c t"), z[:]).then_inc(S("x_out"), 16)
            pool.wait_ge(S("x_out"), 16)

        @block.tensor
        def _(pe):
            norm.tensor(pe)
            pe.wait_ge(mods[0].S("lo"), KC)
            job_muls(m, pe, s0, xh, xl)
            job_muls(m, pe, s0 + KC, xh, xl)
            pe.wait_ge(mods[1].S("lo"), KC)
            job_muls(m, pe, s0 + 2 * KC, xh, xl)

        @block.vector
        def _(dve):
            norm.vector(dve)
            mods[0].vector(dve, lambda k: dve.wait_ge(norm.S("x"), k + 1))
            dve.wait_ge(mods[0].S("lo"), KC)
            dve.wait_ge(m.mm_done, s0 + 2 * KC)
            mods[1].vector(dve, lambda k: None)

        @block.scalar
        def _(act):
            def store(s, j, c, p, stored):
                act.wait_ge(m.mm_done, s + 1)
                if stored is not None:
                    act.wait_ge(S(f"out{p}"), stored)
                nc.scalar.activation(as3(stage[:, p, :]), acc_view(m, p), ACT.Copy).then_inc(m.acc_free[p], 2)
                act.wait_ge(m.acc_free[p], s - p + 2)
                dst = m.scr[j, bass.ds(c, 1)].rearrange("a p t -> (a p) t")
                nc.scalar.dma_start(dst, stage[:, p, :]).then_inc(S(f"out{p}"), 16)

            ring_high(m, act, s0, 0, landed_at(s0))
            ring_high(m, act, s0 + 1, 1, landed_at(s0 + 1))
            norm.scalar(act)
            for j, (_, dst) in enumerate(jobs):
                b = s0 + KC * j
                n = 4 * j
                for p in range(2):
                    ring_high(m, act, b + 2 + p, p, landed_at(b + 2 + p))
                    store(b + p, dst, p, p, 16 * n if n else None)
                with act.Fori(1, KC // 2 - 1) as i:
                    for p in range(2):
                        ring_high(m, act, i * 2 + (b + 2 + p), p, i * 16 + landed_at(b + 2 + p))
                        store(i * 2 + (b + p), dst, i * 2 + p, p, i * 16 + 16 * n)
                for p in range(2):
                    if j < 2:
                        ring_high(m, act, b + KC + p, p, landed_at(b + KC + p))
                    store(b + KC - 2 + p, dst, KC - 2 + p, p, 16 * (n + 3))
            for p in range(2):
                act.wait_ge(S(f"out{p}"), 16 * 12)
        m.slabs = s0 + 3 * KC


def attention_phase(m, qs, ks, vs, lam):
    nc, io = m.nc, m.io
    with ExitStack() as ctx:
        pc = Piece(m, ctx, "attn")
        S = pc.S
        q, k, v = (pc.sb(x, [P, 2, T]) for x in ("q", "k", "v"))
        krow, vrow = pc.sb("k_rows", [P, 2, KC, P]), pc.sb("v_rows", [P, 2, KC, P])
        causal = pc.sb("causal", [P, P])
        pm = pc.sb("probs", [P, 2, 2, SEQ])
        at = pc.sb("attn", [P, 2, SEQ])
        aT = pc.sb("attn_cols", [P, 2, SEQ])
        o, osq = pc.sb("o", [P, KC, P]), pc.sb("o_sq", [P, KC, P])
        outT = pc.sb("out_cols", [P, SEQ])
        mx, nb, l, rl = (pc.sb(x, [P, 2, 2]) for x in ("max", "neg_max", "sums", "weights"))
        ss, rs = pc.sb("ss", [P, KC]), pc.sb("rms", [P, KC])
        lq, eps, gcol = pc.sb("lam_rows", [P, 2, P]), pc.sb("eps", [P, 1]), pc.sb("subln_g", [P, 1])
        ls = pc.sb("lam_sums", [P, 2])
        block = ctx.enter_context(nc.Block())
        tiles = (("k", k, S_K), ("v", v, S_V), ("q", q, S_R))

        def need(eng, name, c, par, n=1, j=1, back=0):
            eng.wait_ge(S(name), c * (2 * n) + ((par - back) * n + j))

        def loop(eng, body):
            for par in range(2):
                body(0, par, True)
            with eng.Fori(1, KC // 2) as c:
                for par in range(2):
                    body(c, par, False)

        def chunk(t, base, c, par):
            return t[base, bass.ds(c * 2 + par, 1)].rearrange("a p t -> (a p) t")

        def rows_of(out, c, par):
            flat = out[0].rearrange("(t p) h n -> h p t n", p=P) if len(out.shape) == 4 else \
                out[0].rearrange("(t p) h m n -> h p t (m n)", p=P)
            return flat[bass.ds(c * 2 + par, 1)].rearrange("a p t n -> (a p) t n")

        @block.sync
        def _(sp):
            nc.sync.dma_start(causal[:], io["masks"][:, C_CAUSAL:C_CAUSAL + P]).then_inc(S("const_in"), 16)
            for i, name in enumerate(("b_lam_q", "b_lam_k")):
                nc.sync.dma_start(lq[:, i, :], io[name].rearrange("a m n -> a (m n)").to_broadcast([P, P])).then_inc(S("const_in"), 16)
            nc.sync.dma_start(gcol[:], io["b_subln_g"].rearrange("a (n o) -> (a n) o", o=1)).then_inc(S("const_in"), 16)

            def body(c, par, first):
                for name, tile, base in tiles:
                    if not first:
                        need(sp, "o_mm", c, par, KC, KC, 2)
                    nc.sync.dma_start(tile[:, par, :], chunk(m.scr, base, c, par)).then_inc(S(f"in_{name}{par}"), 16)
            loop(sp, body)

        @block.gpsimd
        def _(pool):
            def body(c, par, first):
                for name, tile, dst in (("q", q, qs), ("k", k, ks), ("v", v, vs)):
                    pool.wait_ge(S(f"in_{name}{par}"), c * 16 + 16)
                    last = nc.gpsimd.tensor_copy(dst[:, bass.ds(c * 2 + par, 1), :].rearrange("p a n -> p (a n)"),
                                                 tile[:, par, SEQ:T])
                last.then_inc(S("cols"), 1)
                need(pool, "o", c, par, KC, KC)
                if not (first and par == 0):
                    need(pool, "ss", c, par, 1, 1, 1)
                nc.gpsimd.tensor_tensor(osq[:], o[:], o[:], ALU.mult).then_inc(S("osq"), 1)
            loop(pool, body)

        @block.tensor
        def _(pe):
            def body(c, par, first):
                start = first and par == 0

                def turn(tile, name):
                    for j in range(KC):
                        last = nc.tensor.transpose(m.aux[j // 4][:, (j % 4) * P:(j % 4 + 1) * P],
                                                   tile[:, par, j * P:(j + 1) * P], m.ident[:])
                    last.then_inc(S(name), 1)

                def scores(i):
                    for mp in range(2):
                        if i:
                            need(pe, f"exp{mp}", c, par, KC, i)
                        elif not start:
                            need(pe, f"exp{mp}", c, par, KC, KC, 1)
                        h = slice(64 * mp, 64 * mp + 64)
                        n = (i + 1) * P
                        for b in range((n + 511) // 512):
                            w = min(512, n - 512 * b)
                            last = nc.tensor.matmul(m.acc[mp][:, b, 0:w], q[h, par, i * P:(i + 1) * P],
                                                    k[h, par, 512 * b:512 * b + w], start=True, stop=True)
                        last.then_inc(S(f"qk{mp}"), 1)

                def turn_attn(i):
                    need(pe, "attn", c, par, KC, i + 1)
                    if i:
                        need(pe, "aT", c, par, KC, i)
                    for j in range(i + 1):
                        last = nc.tensor.transpose(m.aux[j // 4][:, (j % 4) * P:(j % 4 + 1) * P],
                                                   at[:, i % 2, j * P:(j + 1) * P], m.ident[:])
                    last.then_inc(S("attn_t"), 1)

                def values(i):
                    need(pe, "aT", c, par, KC, i + 1)
                    if i >= 2:
                        need(pe, "o", c, par, KC, i - 1)
                    for j in range(i + 1):
                        last = nc.tensor.matmul(m.acc[i % 2][:, 2, 0:P], aT[:, i % 2, j * P:(j + 1) * P], vrow[:, par, j, :],
                                                start=(j == 0), stop=(j == i))
                    last.then_inc(S("o_mm"), 1)

                pe.wait_ge(S(f"in_k{par}"), c * 16 + 16)
                if not start:
                    need(pe, "outT", c, par, 1, 1, 1)
                turn(k, "k_t")
                pe.wait_ge(S(f"in_q{par}"), c * 16 + 16)
                scores(0)
                pe.wait_ge(S(f"in_v{par}"), c * 16 + 16)
                need(pe, "krow", c, par)
                turn(v, "v_t")
                need(pe, "vrow", c, par)
                for i in range(1, KC):
                    scores(i)
                    turn_attn(i - 1)
                    values(i - 1)
                turn_attn(KC - 1)
                values(KC - 1)
                need(pe, "on", c, par)
                for j in range(KC):
                    last = nc.tensor.transpose(m.aux[j // 4][:, (j % 4) * P:(j % 4 + 1) * P], o[:, j, :], m.ident[:])
                last.then_inc(S("o_t"), 1)
            loop(pe, body)

        @block.vector
        def _(dve):
            V = nc.vector
            V.memset(eps[:], SUBLN_EPS).then_inc(S("eps"), 1)
            dve.wait_ge(S("const_in"), 64)
            V.tensor_tensor(lq[:, 0, :], lq[:, 0, :], lq[:, 1, :], ALU.mult).then_inc(S("lam"), 1)
            dve.wait_ge(S("lam"), 1)
            V.tensor_reduce(ls[:], lq[:, 0, :].rearrange("p (a n) -> p a n", a=2), AX.X, ALU.add).then_inc(S("lam"), 1)
            dve.wait_ge(S("lam_exp"), 1)
            V.tensor_tensor(lam[:], ls[:, 1:2], ls[:, 0:1], ALU.subtract).then_inc(S("lam"), 1)
            dve.wait_ge(S("lam"), 3)
            V.tensor_scalar_add(lam[:], lam[:], -LAM_INIT).then_inc(S("lam"), 1)
            V.tensor_scalar(gcol[:], gcol[:], 1.0 - LAM_INIT, None, ALU.mult).then_inc(S("lam"), 1)
            dve.wait_ge(S("lam"), 5)

            def body(c, par, first):
                start = first and par == 0

                def maxima(i):
                    n, ip = (i + 1) * P, i % 2
                    for mp in range(2):
                        need(dve, f"qk{mp}", c, par, KC, i + 1)
                        d = m.acc[mp][:, i // 4, (i % 4) * P:(i % 4 + 1) * P]
                        V.tensor_tensor(d, d, causal[:], ALU.add).then_inc(S(f"masked{mp}"), 1)
                        need(dve, f"masked{mp}", c, par, KC, i + 1)
                        V.tensor_reduce(mx[:, ip, mp:mp + 1], m.acc[mp][:].rearrange("p b n -> p (b n)")[:, 0:n], AX.X,
                                        ALU.max).then_inc(S(f"max{mp}"), 1)
                        need(dve, f"max{mp}", c, par, KC, i + 1)
                        V.tensor_scalar(nb[:, ip, mp:mp + 1], mx[:, ip, mp:mp + 1], -ATTN_SCALE, None,
                                        ALU.mult).then_inc(S(f"nb{mp}"), 1)

                def combine(i):
                    n, ip = (i + 1) * P, i % 2
                    for mp in range(2):
                        need(dve, f"exp{mp}", c, par, KC, i + 1)
                    V.reciprocal(rl[:, ip, :], l[:, ip, :]).then_inc(S("rl"), 1)
                    need(dve, "rl", c, par, KC, i + 1)
                    if i >= 2:
                        need(dve, "attn_t", c, par, KC, i - 1)
                    V.tensor_scalar(at[:, ip, 0:n], pm[:, ip, 0, 0:n], rl[:, ip, 0:1], None, ALU.mult).then_inc(S("at0"), 1)
                    V.tensor_tensor(rl[:, ip, 1:2], rl[:, ip, 1:2], lam[:], ALU.mult).then_inc(S("rl1"), 1)
                    need(dve, "at0", c, par, KC, i + 1)
                    need(dve, "rl1", c, par, KC, i + 1)
                    V.scalar_tensor_tensor(at[:, ip, 0:n], pm[:, ip, 1, 0:n], rl[:, ip, 1:2], at[:, ip, 0:n], ALU.mult,
                                           ALU.add).then_inc(S("attn"), 1)

                maxima(0)
                for i in range(1, KC):
                    combine(i - 1)
                    maxima(i)
                need(dve, "cols", c, par)
                combine(KC - 1)
                need(dve, "osq", c, par)
                V.tensor_reduce(ss[:], osq[:], AX.X, ALU.add).then_inc(S("ss"), 1)
                need(dve, "rms", c, par)
                V.reciprocal(rs[:], ss[:]).then_inc(S("rrms"), 1)
                need(dve, "rrms", c, par)
                V.tensor_tensor(o[:], o[:], rs[:].unsqueeze(2).to_broadcast([P, KC, P]), ALU.mult).then_inc(S("on"), 1)
            loop(dve, body)

        @block.scalar
        def _(act):
            act.wait_ge(S("lam"), 2)
            act.wait_ge(S("eps"), 1)
            nc.scalar.activation(ls[:], ls[:], ACT.Exp).then_inc(S("lam_exp"), 1)

            def body(c, par, first):
                start = first and par == 0

                def two(name, dst, dram, c, par):
                    need(act, name + "_t", c, par)
                    if not first:
                        act.wait_ge(S(f"{name}_out{par}"), c * 16)
                        if name == "v":
                            need(act, "o_mm", c, par, KC, KC, 2)
                    nc.scalar.activation(dst[:, par].rearrange("p (a j) n -> p a (j n)", a=2), m.aux2[:, :, :],
                                         ACT.Copy).then_inc(S(name + "row"), 1)
                    need(act, name + "row", c, par)
                    nc.scalar.dma_start(rows_of(dram, c, par), dst[:, par]).then_inc(S(f"{name}_out{par}"), 16)

                def exps(i):
                    n, ip = (i + 1) * P, i % 2
                    for mp in range(2):
                        need(act, f"nb{mp}", c, par, KC, i + 1)
                        if i >= 2:
                            need(act, "attn", c, par, KC, i - 1)
                        elif not start:
                            need(act, "attn", c, par, KC, KC - 1 + i, 1)
                        nc.scalar.activation(pm[:, ip, mp, 0:n], m.acc[mp][:].rearrange("p b n -> p (b n)")[:, 0:n], ACT.Exp,
                                             bias=nb[:, ip, mp:mp + 1], scale=ATTN_SCALE,
                                             accum_out=l[:, ip, mp:mp + 1]).then_inc(S(f"exp{mp}"), 1)

                def turned(i):
                    need(act, "attn_t", c, par, KC, i + 1)
                    n = (i + 1) * P
                    if i >= 2:
                        need(act, "o_mm", c, par, KC, i - 1)
                    nc.scalar.activation(aT[:, i % 2, 0:n], m.aux2[:].rearrange("p a n -> p (a n)")[:, 0:n],
                                         ACT.Copy).then_inc(S("aT"), 1)

                def take(i):
                    need(act, "o_mm", c, par, KC, i + 1)
                    if i == 0 and not start:
                        need(act, "o_t", c, par, 1, 1, 1)
                    nc.scalar.activation(o[:, i, :], m.acc[i % 2][:, 2, 0:P], ACT.Copy).then_inc(S("o"), 1)

                two("k", krow, io["k_prompt"], c, par)
                exps(0)
                two("v", vrow, io["v_prompt"], c, par)
                for i in range(1, KC):
                    turned(i - 1)
                    exps(i)
                    take(i - 1)
                turned(KC - 1)
                take(KC - 1)
                need(act, "ss", c, par)
                nc.scalar.activation(ss[:], ss[:], ACT.Sqrt, bias=eps[:, 0:1], scale=1.0 / P).then_inc(S("rms"), 1)
                need(act, "o_t", c, par)
                if not start:
                    act.wait_ge(S("mix_out"), c * 32 + par * 16)
                nc.scalar.activation(outT[:].rearrange("p (a n) -> p a n", a=2), m.aux2[:, :, :], ACT.Copy,
                                     scale=gcol[:, 0:1]).then_inc(S("outT"), 1)
                need(act, "outT", c, par)
                nc.scalar.dma_start(m.scr[S_MIX, bass.ds(c * 2 + par, 1), :, 0:SEQ].rearrange("a p t -> (a p) t"),
                                    outT[:]).then_inc(S("mix_out"), 16)
            loop(act, body)
            for par in range(2):
                for name in ("k", "v"):
                    act.wait_ge(S(f"{name}_out{par}"), 16 * KC // 2)
            act.wait_ge(S("mix_out"), 16 * KC)


def sample_attention_phase(m, qs, ks, vs, lam):
    nc, io = m.nc, m.io
    NP, NH = 8, 8
    with ExitStack() as ctx:
        pc = Piece(m, ctx, "paged")
        S = pc.S
        NK, NVB = 3, 2
        kp = pc.sb("k_page", [P, NK, D])
        prod = pc.sb("k_prod", [P, 2, D])
        qb = pc.sb("q_rows_all", [P, 2, D])
        vp = pc.sb("v_pages", [P, NVB, NP, D])
        sc = pc.sb("scores", [P, NP, NS, 16])
        rows = pc.sb("rows", [NS, 3, D])
        pr = pc.sb("probs", [P, NP * P + 1])
        prT = pc.sb("prob_cols", [P, NP, P])
        at = pc.sb("attn", [P, NP, NS, NH])
        newT, anew = pc.sb("new_row", [1, P]), pc.sb("attn_new", [1, NS * NH])
        half = pc.sb("halves", [P, 2])
        pn = pc.sb("new_prod", [P, NS, NH, 2])
        qk = pc.sb("qk_new", [P, NH, NS])
        mx, l, w, sign = (pc.sb(x, [P, 1]) for x in ("max", "sum", "weight", "sign"))
        res, o2, bc = (pc.sb(x, [P, NS, NH]) for x in ("res", "res2", "attn_new_all"))
        eps, gcol, ones = pc.sb("eps", [P, 1]), pc.sb("subln_g", [P, 1]), pc.sb("ones", [P, P])
        tab = pc.sb("table", [1, NS * NP], I32)
        cm = pc.sb("cm", [P, 2])
        outc = pc.sb("out_cols", [P, NH, NS])
        block = ctx.enter_context(nc.Block())
        NPAGE = NS * NP
        pool_rows = io["cache_k"].shape[0]
        kflat = io["cache_k"].rearrange("g p h m n -> g p (h m n)")
        vflat = io["cache_v"].rearrange("g p h n -> g p (h n)")
        qrow_dram = m.yrows

        @block.sync
        def _(sp):
            nc.sync.dma_start(tab[:], io["page_table"].rearrange("(o b) n -> o (b n)", o=1)).then_inc(S("table_in"), 16)
            nc.sync.dma_start(gcol[:], io["b_subln_g"].rearrange("a (n o) -> (a n) o", o=1)).then_inc(S("const_in"), 16)
            nc.sync.dma_start(half[:], io["masks"][:, C_BLOCK:C_BLOCK + P:64], allow_slow_non_contiguous=True).then_inc(S("const_in"), 16)
            nc.sync.dma_start(sign[:], io["masks"][:, C_SIGN:C_SIGN + 1], allow_slow_non_contiguous=True).then_inc(S("const_in"), 16)
            sp.wait_ge(S("table_in"), 16)
            sp.wait_ge(S("rows"), 1)
            nc.sync.dma_start(io["k_sample"].rearrange("b o h m n -> (b o) (h m n)"), rows[:, 1, :]).then_inc(S("rows_out"), 16)
            nc.sync.dma_start(io["v_sample"].rearrange("b o h n -> (b o) (h n)"), rows[:, 2, :]).then_inc(S("rows_out"), 16)
            nc.sync.dma_start(qrow_dram, rows[:, 0, :]).then_inc(S("q_out"), 16)
            sp.wait_ge(S("q_out"), 16)
            for u in range(NPAGE):
                b, g = u // NP, u % NP
                if g == 0:
                    if b >= 2:
                        sp.wait_ge(S("prod"), NP * (b - 1))
                    nc.sync.dma_start(qb[:, b % 2, :], qrow_dram[b:b + 1, :].to_broadcast([P, D])).then_inc(S(f"qb{b % 2}"), 16)
                page = sp.value_load(tab[0:1, u:u + 1], min_val=0, max_val=pool_rows - 1)
                if u >= NK:
                    sp.wait_ge(S("prod"), u - NK + 1)
                nc.sync.dma_start(kp[:, u % NK, :], kflat[bass.ds(page, 1)].rearrange("a p n -> (a p) n")).then_inc(S(f"k_in{u % NK}"), 16)
            sp.wait_ge(S("out"), 1)
            nc.sync.dma_start(m.scr[S_MIX, :, :, SEQ:T].rearrange("h p n -> p h n"), outc[:]).then_inc(S("mix_out"), 16)
            sp.wait_ge(S("mix_out"), 16)
            sp.wait_ge(S("rows_out"), 32)

        @block.scalar
        def _(act):
            act.wait_ge(S("table_in"), 16)
            act.wait_ge(S("rows_t"), 1)
            for i in range(3):
                last = nc.scalar.activation(rows[:, i, :].rearrange("p (a n) -> p a n", a=2), (m.acc[0], m.acc[1], m.aux2)[i][0:NS, 0:2, :],
                                            ACT.Copy)
            last.then_inc(S("rows"), 1)

            def load_v(b):
                if b >= NVB:
                    act.wait_ge(S("pv"), b - NVB + 1)
                for g in range(NP):
                    u = b * NP + g
                    page = act.value_load(tab[0:1, u:u + 1], min_val=0, max_val=pool_rows - 1)
                    nc.scalar.dma_start(vp[:, b % NVB, g, :], vflat[bass.ds(page, 1)].rearrange("a p n -> (a p) n")).then_inc(S(f"v_in{b % NVB}"), 16)

            load_v(0)
            load_v(1)
            for g in range(NP // 4):
                act.wait_ge(S("sc_t"), g + 1)
                nc.scalar.activation(pr[:, g * 512:(g + 1) * 512], m.acc[0][:, g, :], ACT.Copy)
            act.wait_ge(S("new_mm"), 1)
            nc.scalar.activation(pr[:, NP * P:NP * P + 1], m.acc[1][:, 0, 0:1], ACT.Copy).then_inc(S("pr"), 1)
            act.wait_ge(S("nb"), 2)
            nc.scalar.activation(pr[:], pr[:], ACT.Exp, bias=mx[:, 0:1], scale=ATTN_SCALE, accum_out=l[:, 0:1]).then_inc(S("exp"), 1)
            for b in range(NVB, NS):
                load_v(b)
            act.wait_ge(S("ms"), 1)
            nc.scalar.activation(o2[:].rearrange("p b h -> p (b h)"), m.acc[0][:, 0, 0:NS * NH], ACT.Sqrt, bias=eps[:, 0:1]).then_inc(S("rms"), 1)

        @block.gpsimd
        def _(pool):
            for u in range(NPAGE):
                b = u // NP
                pool.wait_ge(S(f"k_in{u % NK}"), 16 * (u // NK + 1))
                if u % NP == 0:
                    pool.wait_ge(S(f"qb{b % 2}"), 16 * (b // 2 + 1))
                if u >= 2:
                    pool.wait_ge(S("red"), u - 1)
                nc.gpsimd.tensor_tensor(prod[:, u % 2, :], kp[:, u % NK, :], qb[:, b % 2, :], ALU.mult).then_inc(S("prod"), 1)

        @block.tensor
        def _(pe):
            for i, t in enumerate((qs, ks, vs)):
                for h in range(NH):
                    last = nc.tensor.transpose((m.acc[0], m.acc[1], m.aux2)[i][0:NS, h // 4, (h % 4) * P:(h % 4 + 1) * P], t[:, h, :], m.ident[:])
            last.then_inc(S("rows_t"), 1)
            pe.wait_ge(S("rows"), 1)
            pe.wait_ge(S("pn"), 1)
            pe.wait_ge(S("ones"), 1)
            nc.tensor.matmul(m.acc[1][:, 0, 0:1], pn[:].rearrange("p b h m -> p (b h m)"), ones[:, 0:1], start=True, stop=True).then_inc(S("new_mm"), 1)
            pe.wait_ge(S("red"), NPAGE)
            for g in range(NP):
                last = nc.tensor.transpose(m.acc[0][:, g // 4, (g % 4) * P:(g % 4 + 1) * P], sc[:, g].rearrange("p b n -> p (b n)"), m.ident[:])
                if g % 4 == 3:
                    last.then_inc(S("sc_t"), 1)
            pe.wait_ge(S("weighted"), 1)
            for g in range(NP):
                last = nc.tensor.transpose(m.acc[0][:, g // 4, (g % 4) * P:(g % 4 + 1) * P], pr[:, g * P:(g + 1) * P], m.ident[:])
            nc.tensor.transpose(m.acc[1][0:1, 0, 0:P], pr[:, NP * P:NP * P + 1], m.ident[:]).then_inc(S("pr_t"), 1)
            pe.wait_ge(S("at"), 1)
            for b in range(NS):
                pe.wait_ge(S(f"v_in{b % NVB}"), 16 * NP * (b // NVB + 1))
                for h in range(NH):
                    for g in range(NP):
                        last = nc.tensor.matmul(m.aux[0][:, b * NH + h:b * NH + h + 1], vp[:, b % NVB, g, h * P:(h + 1) * P],
                                                at[:, g, b, h:h + 1], start=(g == 0), stop=(g == NP - 1))
                last.then_inc(S("pv"), 1)
            pe.wait_ge(S("anew"), 1)
            nc.tensor.matmul(m.aux[1][:, 0:NS * NH], ones[0:1, :], anew[:], start=True, stop=True).then_inc(S("bc_mm"), 1)
            pe.wait_ge(S("sq"), 1)
            nc.tensor.matmul(m.acc[0][:, 0, 0:NS * NH], ones[:], o2[:].rearrange("p b h -> p (b h)"), start=True, stop=True).then_inc(S("ms"), 1)

        @block.vector
        def _(dve):
            V = nc.vector
            V.memset(ones[:], 1.0).then_inc(S("ones"), 1)
            V.memset(eps[:], P * SUBLN_EPS).then_inc(S("ones"), 1)
            dve.wait_ge(S("const_in"), 48)
            V.tensor_tensor(qk[:], qs[:], ks[:], ALU.mult).then_inc(S("qk"), 1)
            V.tensor_scalar(gcol[:], gcol[:], (1.0 - LAM_INIT) * math.sqrt(P), None, ALU.mult).then_inc(S("qk"), 1)
            V.tensor_scalar(cm[:, 0:1], sign[:], -1.0, 1.0, ALU.mult, ALU.add).then_inc(S("qk"), 1)
            V.tensor_tensor(cm[:, 1:2], sign[:], lam[:], ALU.mult).then_inc(S("qk"), 1)
            dve.wait_ge(S("qk"), 4)
            V.tensor_tensor(cm[:, 0:1], cm[:, 0:1], cm[:, 1:2], ALU.add).then_inc(S("qk"), 1)
            for mp in range(2):
                last = V.tensor_scalar(pn[:, :, :, mp], qk[:].rearrange("p h b -> p b h"), half[:, mp:mp + 1], None, ALU.mult)
            last.then_inc(S("pn"), 1)
            for u in range(NPAGE):
                b, g = u // NP, u % NP
                dve.wait_ge(S("prod"), u + 1)
                V.tensor_reduce(sc[:, g, b, :], prod[:, u % 2, :].rearrange("p (h n) -> p h n", n=64), AX.X, ALU.add).then_inc(S("red"), 1)
            dve.wait_ge(S("pr"), 1)
            V.tensor_reduce(mx[:], pr[:], AX.X, ALU.max).then_inc(S("nb"), 1)
            dve.wait_ge(S("nb"), 1)
            V.tensor_scalar(mx[:], mx[:], -ATTN_SCALE, None, ALU.mult).then_inc(S("nb"), 1)
            dve.wait_ge(S("exp"), 1)
            V.reciprocal(w[:], l[:]).then_inc(S("w"), 1)
            dve.wait_ge(S("w"), 1)
            V.tensor_tensor(w[:], w[:], cm[:, 0:1], ALU.mult).then_inc(S("w"), 1)
            dve.wait_ge(S("w"), 2)
            V.tensor_scalar(pr[:], pr[:], w[:, 0:1], None, ALU.mult).then_inc(S("weighted"), 1)
            dve.wait_ge(S("pr_t"), 1)
            V.tensor_copy(prT[:].rearrange("p (a g) n -> p a (g n)", a=2), m.acc[0][:, 0:2, :])
            V.tensor_copy(newT[:], m.acc[1][0:1, 0, 0:P]).then_inc(S("prT"), 1)
            dve.wait_ge(S("prT"), 1)
            pv = prT[:].rearrange("p g (b h m) -> p (g b h) m", h=NH, m=2)
            V.tensor_tensor(at[:].rearrange("p g b h -> p (g b h)"), pv[:, :, 0], pv[:, :, 1], ALU.add).then_inc(S("at"), 1)
            nv = newT[:].rearrange("p (n m) -> p n m", m=2)
            V.tensor_tensor(anew[:], nv[:, :, 0], nv[:, :, 1], ALU.add).then_inc(S("anew"), 1)
            dve.wait_ge(S("bc_mm"), 1)
            V.tensor_tensor(bc[:], m.aux[1][:, 0:NS * NH].rearrange("p (b h) -> p b h", b=NS), vs[:].rearrange("p h b -> p b h"), ALU.mult).then_inc(S("bc"), 1)
            dve.wait_ge(S("pv"), NS)
            dve.wait_ge(S("bc"), 1)
            V.tensor_tensor(res[:], m.aux[0][:, 0:NS * NH].rearrange("p (b h) -> p b h", b=NS), bc[:], ALU.add).then_inc(S("res"), 1)
            dve.wait_ge(S("res"), 1)
            V.tensor_tensor(o2[:], res[:], res[:], ALU.mult).then_inc(S("sq"), 1)
            dve.wait_ge(S("rms"), 1)
            V.reciprocal(bc[:], o2[:]).then_inc(S("rrms"), 1)
            dve.wait_ge(S("rrms"), 1)
            V.tensor_tensor(res[:], res[:], bc[:], ALU.mult).then_inc(S("normed"), 1)
            dve.wait_ge(S("normed"), 1)
            V.tensor_scalar(outc[:], res[:].rearrange("p b h -> p h b"), gcol[:, 0:1], None, ALU.mult).then_inc(S("out"), 1)


def y_phase(m, z):
    nc, io = m.nc, m.io
    with ExitStack() as ctx:
        pc = Piece(m, ctx, "y")
        tmp = pc.sb("tmp", [P, 2, T])
        rows = pc.sb("rows", [P, 2, D])
        norm = Norm(m, ctx, "norm3", z, 3, tmp)
        S = pc.S
        block = ctx.enter_context(nc.Block())
        NT = KC + 1

        @block.tensor
        def _(pe):
            norm.tensor(pe)
            pe.wait_ge(norm.S("x"), KC)
            for t in range(NT):
                n = P if t < KC else NS
                if t >= 2:
                    pe.wait_ge(S("in"), t - 1)
                for c in range(KC):
                    last = nc.tensor.transpose(m.acc[t % 2][0:n, c // 4, (c % 4) * P:(c % 4 + 1) * P],
                                               z[:, c, t * P:t * P + n], m.ident[:])
                last.then_inc(S("turned"), 1)

        @block.vector
        def _(dve):
            norm.vector(dve)

        @block.scalar
        def _(act):
            norm.scalar(act)
            for t in range(NT):
                n = P if t < KC else NS
                act.wait_ge(S("turned"), t + 1)
                if t >= 2:
                    act.wait_ge(S(f"out{t % 2}"), 16 * (t // 2))
                nc.scalar.activation(rows[0:n, t % 2, :].rearrange("p (a n) -> p a n", a=2), m.acc[t % 2][0:n, 0:2, :],
                                     ACT.Copy).then_inc(S("in"), 1)

        @block.sync
        def _(sp):
            for t in range(NT):
                sp.wait_ge(S("in"), t + 1)
                if t < KC:
                    nc.sync.dma_start(io["y_prompt"][0, t * P:(t + 1) * P, :], rows[:, t % 2, :]).then_inc(S(f"out{t % 2}"), 16)
                else:
                    nc.sync.dma_start(io["y_sample"].rearrange("b o d -> (b o) d"), rows[0:NS, t % 2, :]).then_inc(S(f"out{t % 2}"), 16)
            sp.wait_ge(S("out0"), 16 * 5)
            sp.wait_ge(S("out1"), 16 * 4)


def program(nc, io):
    with ExitStack() as ctx:
        m = Machine(nc, io, ctx)
        setup_phase(m)
        m.end_phase()
        with ExitStack() as mix:
            h = mix.enter_context(nc.sbuf_tensor("h", [P, KC, T], F32))
            xx = mix.enter_context(nc.sbuf_tensor("xx", [P, KC, T], F32))
            input_phase(m, h, xx)
            m.end_phase()
            project_phase(m, h, xx)
            m.end_phase()
        with ExitStack() as mix:
            bs = mix.enter_context(nc.sbuf_tensor("bonus_sample", [P, KC, NS], F32))
            gs = mix.enter_context(nc.sbuf_tensor("gate_sample", [P, KC, NS], F32))
            scan_phase(m, bs, gs)
            m.end_phase()
            sample_scan_phase(m, bs, gs)
            m.end_phase()
        with nc.sbuf_tensor("z", [P, KC, T], F32) as z:
            output_phase(m, z, 0, M_GTM)
            m.end_phase()
            mlp_phase(m, z, 0)
            m.end_phase()
            qkv_phase(m, z)
            m.end_phase()
        with ExitStack() as att:
            qs, ks, vs = (att.enter_context(nc.sbuf_tensor(f"sample_{x}", [P, KC, NS], F32)) for x in "qkv")
            lam = att.enter_context(nc.sbuf_tensor("neg_lambda", [P, 1], F32))
            attention_phase(m, qs, ks, vs, lam)
            m.end_phase()
            sample_attention_phase(m, qs, ks, vs, lam)
            m.end_phase()
        with nc.sbuf_tensor("z1", [P, KC, T], F32) as z:
            output_phase(m, z, 1, 6 + M_GTM)
            m.end_phase()
            mlp_phase(m, z, 1)
            m.end_phase()
            y_phase(m, z)
            m.end_phase()


_OUTS = [(1, SEQ, D), (NS, 1, D), (1, SEQ, 8, 2, 64), (1, SEQ, 8, P), (1, 1, 16, 64, 64), (1, 1, D),
         (NS, 1, 8, 2, 64), (NS, 1, 8, P), (1, NS, 16, 64, 64), (1, NS, D)]
_OUT_NAMES = ["y_prompt", "y_sample", "k_prompt", "v_prompt", "wkv_prompt", "shift_prompt",
              "k_sample", "v_sample", "wkv_sample", "shift_sample"]


def masks():
    import numpy as np

    t = np.arange(P)
    row, colm = t[:, None], t[None, :]
    out = np.zeros((P, C_ALL), np.float32)
    for l in range(7):
        level = (row >> (l + 1) == colm >> (l + 1)) & ((row >> l) & 1 == 1) & ((colm >> l) & 1 == 0)
        out[:, C_LEVEL + l * P:C_LEVEL + (l + 1) * P] = level.T if l == 0 else level
    out[:, C_UPPER:C_UPPER + P] = row < colm
    out[:, C_UPPER + P:C_UPPER + 2 * P] = row <= colm
    out[:, C_BLOCK:C_BLOCK + P] = row // 64 == colm // 64
    out[:, C_CAUSAL:C_CAUSAL + P] = np.where(colm <= row, 0, NEG)
    out[:, C_RESET:C_RESET + P] = colm > 0
    out[:, C_SIGN] = t % 2
    return out


def kernel(**inputs):
    import numpy as np
    import concourse.bacc as bacc
    from concourse.bass_utils import run_bass_kernel_spmd

    nc = bacc.Bacc("TRN2", target_bir_lowering=False, num_devices=1)
    arrays, io = {}, {}
    inputs["masks"] = masks()
    for name, value in inputs.items():
        a = np.ascontiguousarray(value)
        arrays[f"in_{name}"] = a
        io[name] = nc.dram_tensor(f"in_{name}", a.shape, mybir.dt.from_np(a.dtype), kind="ExternalInput").ap()
    for name, shape in zip(_OUT_NAMES, _OUTS):
        io[name] = nc.dram_tensor(f"out_{name}", shape, F32, kind="ExternalOutput").ap()
    program(nc, io)
    r = run_bass_kernel_spmd(nc, [arrays], core_ids=[0])
    return tuple(r.results[0][f"out_{name}"] for name in _OUT_NAMES)
```

```python
from contextlib import ExitStack
import math

import concourse.bass as bass
from concourse import mybir

F32 = mybir.dt.float32
F32R = mybir.dt.float32r
I32 = mybir.dt.int32
ALU = mybir.AluOpType
ACT = mybir.ActivationFunctionType
AX = mybir.AxisListType

P = 128
D = 1024
KC = D // P
SEQ = 1024
NS = 8
T = SEQ + NS
NG = 3
G = T // NG
SLAB = KC * P
ALPHA = 4.0 ** 0.25
LN_EPS = 1e-5
GN_EPS = 64e-5
SUBLN_EPS = 1e-5
LAM_INIT = 0.8 - 0.6 * math.exp(-0.3)
ATTN_SCALE = 64 ** -0.5
NEG = -1e30
DECAY_SCALE = -math.exp(-0.5)

VEC_NAMES = (["ada_b0"] * 6 + ["ada_b1"] * 6 + ["kv_b"] * 2 + ["ln_g"] * 4 + ["ln_b"] * 4 + ["mu"] * 6
             + ["w0", "a0", "k_k", "k_a", "r_k", "gn_g", "gn_b"])
NV = len(VEC_NAMES)
V_LNG, V_LNB, V_MU = 14, 18, 22
V_W0, V_A0, V_KK, V_KA, V_RK, V_GNG, V_GNB = range(28, 35)
NM = 14
M_SHM, M_SCM, M_GTM, M_SHF, M_SCF, M_GTF = range(6)
M_KVSH, M_KVSC = 12, 13
S_R, S_K, S_V, S_LW, S_A, S_G, S_MIX = range(1, 8)


C_LEVEL = 0
C_UPPER = 7 * P
C_BLOCK = C_UPPER + 2 * P
C_CAUSAL = C_BLOCK + P
C_RESET = C_CAUSAL + P
C_SIGN = C_RESET + P
C_ALL = C_SIGN + 1


class Machine:

    def __init__(self, nc, io, ctx):
        self.nc, self.io = nc, io

        def sb(name, shape, dt=F32):
            return ctx.enter_context(nc.sbuf_tensor(name, shape, dt))

        self.ident = sb("ident", [P, P])
        self.mean = sb("mean_matrix", [P, P])
        self.eps = sb("eps", [P, 1])
        self.mods = sb("mods", [P, NM, KC, 1 + NS])
        self.cT = sb("c_cols", [P, KC, 1 + NS])
        self.vecs = sb("vecs", [P, NV * KC])
        self.w_raw = sb("w_raw", [P, 2, KC, P])
        self.w_hi = sb("w_hi", [P, 2, KC, P], F32R)
        self.w_lo = sb("w_lo", [P, 2, KC, P], F32R)
        self.acc = [ctx.enter_context(nc.psum_tensor(f"acc{i}", [P, NG, 512], F32)) for i in range(2)]
        self.aux2 = ctx.enter_context(nc.psum_tensor("aux", [P, 2, 512], F32))
        self.aux = [self.aux2[:, i, :] for i in range(2)]

        def sem(name):
            return ctx.enter_context(nc.semaphore(name))

        self.w_landed = [sem("w_landed0"), sem("w_landed1")]
        self.hi_done = sem("w_hi_done")
        self.lo_done = sem("w_lo_done")
        self.mm_done = sem("mm_done")
        self.acc_free = [sem("acc_free0"), sem("acc_free1")]
        self.t_free = sem("stage_free")
        self.staged = 0
        self.phase_sems = []
        self.sem_names = set()
        self.phases = 0
        self.slabs = 0
        self.xt = nc.dram_tensor("scratch_x", (KC, P, T), F32, kind="Internal").ap()
        self.srows = nc.dram_tensor("scratch_sample_rows", (6, NS, D), F32, kind="Internal").ap()
        self.yrows = nc.dram_tensor("scratch_sample_y", (NS, D), F32, kind="Internal").ap()
        self.scr = nc.dram_tensor("scratch_mix", (8, KC, P, T), F32, kind="Internal").ap()

    def phase_sem(self, name):
        self.phase_sems.append(self.nc.alloc_semaphore(name=f"{name}_{self.phases}" if name in self.sem_names else name))
        self.sem_names.add(name)
        return self.phase_sems[-1]

    def end_phase(self):
        self.nc.clear_and_free_semaphores(self.phase_sems)
        self.nc.all_engine_barrier()
        self.phase_sems = []
        self.phases += 1

    def vec(self, v, c):
        return self.vecs[:, v * KC + c:v * KC + c + 1]

    def mod(self, m, c):
        return self.mods[:, m, c, 0:1]


def landed_at(s):
    return 16 * (s // 2 + 1)


def slab_of(w, mo, width=P):
    return w[:, mo * P:mo * P + width].rearrange("(k p) n -> p k n", p=P)


def slab_at(w, mo):
    return w[:, bass.ds(mo * P, P)].rearrange("(k p) n -> p k n", p=P)



def ring_load(m, sp, src, s, p, width=P, first=False):
    if not first:
        sp.wait_ge(m.lo_done, s - 1)
    m.nc.sync.dma_start(m.w_raw[:, p, :, 0:width], src).then_inc(m.w_landed[p], 16)


def ring_high(m, act, s, p, n, width=P, first=False):
    act.wait_ge(m.w_landed[p], n)
    if not first:
        act.wait_ge(m.mm_done, s - 1)
    m.nc.scalar.activation(m.w_hi[:, p, :, 0:width], m.w_raw[:, p, :, 0:width], ACT.Copy).then_inc(m.hi_done, 1)


def ring_low(m, pool, s, p, width=P):
    pool.wait_ge(m.hi_done, s + 1)
    m.nc.gpsimd.tensor_tensor(m.w_lo[:, p, :, 0:width], m.w_raw[:, p, :, 0:width],
                              m.w_hi[:, p, :, 0:width].bitcast(F32), ALU.subtract).then_inc(m.lo_done, 1)


def ring_mul(m, pe, s, p, xh, xl, width=P, first=False, ready=None, free=None):
    pe.wait_ge(m.lo_done, s + 1)
    if not first:
        pe.wait_ge(m.acc_free[p], s - p)
    for k in range(KC):
        if ready is not None:
            pe.wait_ge(ready[0], ready[1] + k + 1)
        hi, lo = m.w_hi[:, p, k, 0:width], m.w_lo[:, p, k, 0:width]
        for g in range(NG):
            out = m.acc[p][0:width, g, 0:G]
            cols = slice(g * G, (g + 1) * G)
            m.nc.tensor.matmul(out, hi, xh[:, k, cols], start=(k == 0), stop=False)
            m.nc.tensor.matmul(out, hi, xl[:, k, cols], start=False, stop=False)
            last = m.nc.tensor.matmul(out, lo, xh[:, k, cols], start=False, stop=(k == KC - 1))
        if free is not None and k < KC - 1:
            last.then_inc(free, 1)
    last.then_inc(m.mm_done, 1)


def acc_view(m, p, rows=P):
    return m.acc[p][0:rows, :, 0:G]


def as3(ap):
    return ap.rearrange("p (g n) -> p g n", g=NG)


def setup_phase(m):
    nc, io = m.nc, m.io
    with ExitStack() as ctx:
        def sb(name, shape, dt=F32):
            return ctx.enter_context(nc.sbuf_tensor(name, shape, dt))

        def sem(name):
            return m.phase_sem(name)

        rows = sb("vec_rows", [P, 3, P])
        crow = sb("c_rows", [1 + NS, D])
        cexp = sb("c_exp", [1 + NS, D])
        cden = sb("c_den", [1 + NS, D])
        cT = m.cT
        NB = 4
        wide = sb("ada_slab", [P, NB, KC, 512])
        mrow = sb("mod_rows", [1 + NS, 2, 512])
        small, c_in, ident0, ident1 = sem("rows_in"), sem("c_in"), sem("ident_zero"), sem("ident_done")
        landed = [sem(f"ada_landed{i}") for i in range(NB)]
        cexped, csteps, ct_done, ct_in = sem("c_exped"), sem("c_steps"), sem("c_turned"), sem("c_cols_in")
        vt_done, vt_in = sem("vecs_turned"), sem("vecs_in")
        ada_mm, row_in, mod_t, mod_in = sem("ada_mm"), sem("mod_row_in"), sem("mod_turned"), sem("mod_in")
        block = ctx.enter_context(nc.Block())
        NU = 4

        def ada_src(u):
            mod, half = u // 2, u % 2
            w = io["ada_w"][0, :, mod * D + half * 512:mod * D + half * 512 + 512]
            return w.rearrange("(k p) n -> p k n", p=P)

        @block.sync
        def _(sp):
            nc.sync.dma_start(crow[0:1, :], io["c_prompt"]).then_inc(c_in, 16)
            nc.sync.dma_start(crow[1:1 + NS, :], io["c_sample"]).then_inc(c_in, 16)
            at = 0
            for src, n in ((io["ada_b"], 12), (io["kv_ada_b"], 2), (io["ln_g"], 4), (io["ln_b"], 4), (io["a_mu"], 6),
                           (io["a_w0"], 1), (io["a_a0"], 1), (io["a_k_k"], 1), (io["a_k_a"], 1), (io["a_r_k"], 1),
                           (io["a_gn_g"], 1), (io["a_gn_b"], 1)):
                flat = src
                if len(src.shape) == 3:
                    flat = src.rearrange("a b c -> (a b c)")
                elif len(src.shape) == 2:
                    flat = src.rearrange("a b -> (a b)")
                flat = flat.rearrange("(r n) -> r n", n=P)
                done = 0
                while done < n * KC:
                    q = min(n * KC - done, P - at % P)
                    nc.sync.dma_start(rows[at % P:at % P + q, at // P, :], flat[done:done + q, :]).then_inc(small, 16)
                    at += q
                    done += q
            for u in range(NU):
                if u >= NB:
                    sp.wait_ge(ada_mm, u - NB + 1)
                nc.sync.dma_start(wide[:, u % NB, :, :], ada_src(u)).then_inc(landed[u % NB], 16)

        @block.gpsimd
        def _(pool):
            nc.gpsimd.memset(m.mean[:], 1.0 / D)
            nc.gpsimd.memset(m.eps[:], LN_EPS).then_inc(m.t_free, 2)
            nc.gpsimd.memset(m.ident[:], 0.0).then_inc(ident0, 1)
            pool.wait_ge(ident0, 1)
            nc.gpsimd.affine_select(out=m.ident[:], in_=m.ident[:], compare_op=ALU.not_equal, fill=1.0, base=0,
                                    pattern=[[-1, P]], channel_multiplier=1).then_inc(ident1, 1)

        @block.scalar
        def _(act):
            act.wait_ge(c_in, 32)
            nc.scalar.activation(cexp[:], crow[:], ACT.Exp, scale=-1.0).then_inc(cexped, 1)
            for u in range(NU):
                act.wait_ge(ada_mm, u + 1)
                if u >= 2:
                    act.wait_ge(mod_t, u - 1)
                nc.scalar.activation(mrow[:, u % 2, :], m.acc[0][0:1 + NS, u % 3, :], ACT.Copy).then_inc(row_in, 1)

        @block.vector
        def _(dve):
            dve.wait_ge(cexped, 1)
            nc.vector.tensor_scalar_add(cden[:], cexp[:], 1.0).then_inc(csteps, 1)
            dve.wait_ge(csteps, 1)
            nc.vector.reciprocal(cexp[:], cden[:]).then_inc(csteps, 1)
            dve.wait_ge(csteps, 2)
            nc.vector.tensor_tensor(crow[:], crow[:], cexp[:], ALU.mult).then_inc(csteps, 1)
            dve.wait_ge(vt_done, 1)
            nc.vector.tensor_copy(m.vecs[:], m.aux[0][:, 0:NV * KC]).then_inc(vt_in, 1)
            dve.wait_ge(ct_done, 1)
            nc.vector.tensor_copy(cT[:], m.aux[1][:, 0:KC * (1 + NS)].rearrange("p (k n) -> p k n", k=KC)).then_inc(ct_in, 1)
            dve.wait_ge(vt_in, 1)
            for u in range(NU):
                mod, half = u // 2, u % 2
                dve.wait_ge(mod_t, u + 1)
                nc.vector.tensor_tensor(
                    m.mods[:, mod, 4 * half:4 * half + 4, :],
                    m.aux[u % 2][:, 0:4 * (1 + NS)].rearrange("p (k n) -> p k n", k=4),
                    m.vecs[:, mod * KC + 4 * half:mod * KC + 4 * half + 4].unsqueeze(2).to_broadcast([P, 4, 1 + NS]),
                    ALU.add).then_inc(mod_in, 1)
            dve.wait_ge(mod_in, NU)
            nc.vector.tensor_scalar_add(m.mods[:, M_SCM, :, :], m.mods[:, M_SCM, :, :], 1.0).then_inc(mod_in, 1)

        @block.tensor
        def _(pe):
            pe.wait_ge(ident1, 1)
            pe.wait_ge(small, 16 * N_SMALL)
            left = NV * KC
            for t in range(3):
                q = min(P, left - t * P)
                last = nc.tensor.transpose(m.aux[0][:, t * P:t * P + q], rows[0:q, t, :], m.ident[0:q, 0:q])
            last.then_inc(vt_done, 1)
            pe.wait_ge(csteps, 3)
            n = 1 + NS
            for k in range(KC):
                last = nc.tensor.transpose(m.aux[1][:, k * n:(k + 1) * n], crow[:, k * P:(k + 1) * P], m.ident[0:n, 0:n])
            last.then_inc(ct_done, 1)

            def turn(u):
                pe.wait_ge(row_in, u + 1)
                if u < 2:
                    pe.wait_ge(ct_in, 1)
                    pe.wait_ge(vt_in, 1)
                else:
                    pe.wait_ge(mod_in, u - 1)
                for q in range(4):
                    last = nc.tensor.transpose(m.aux[u % 2][:, q * n:(q + 1) * n], mrow[:, u % 2, q * P:(q + 1) * P],
                                               m.ident[0:n, 0:n])
                last.then_inc(mod_t, 1)

            pe.wait_ge(ct_in, 1)
            for u in range(NU):
                pe.wait_ge(landed[u % NB], 16 * (u // NB + 1))
                if u >= 3:
                    pe.wait_ge(row_in, u - 2)
                for k in range(KC):
                    last = nc.tensor.matmul(m.acc[0][0:n, u % 3, :], cT[:, k, :], wide[:, u % NB, k, :],
                                            start=(k == 0), stop=(k == KC - 1))
                last.then_inc(ada_mm, 1)
                if u >= 1:
                    turn(u - 1)
            turn(NU - 1)


N_SMALL = 13


def input_phase(m, h, xx):
    nc, io = m.nc, m.io
    with ExitStack() as ctx:
        def sb(name, shape, dt=F32):
            return ctx.enter_context(nc.sbuf_tensor(name, shape, dt))

        def sem(name):
            return m.phase_sem(name)

        xin = sb("x_rows", [P, KC, D])
        xs = sb("x_sample_rows", [NS, D])
        shin = sb("shift_rows", [NS, D])
        shT = sb("shift_cols", [P, KC, NS])
        stage = sb("x_cols", [P, 2, T])
        lastrows = sb("last_rows", [1 + NS, D])
        x_in = [sem(f"x_in{i}") for i in range(KC)]
        xs_in, turned, staged, h_done, xt_out = sem("xs_in"), sem("x_turned"), sem("x_staged"), sem("h_done"), [sem("xt_out0"), sem("xt_out1")]
        sh_t, sh_in, hs_done, xx_done = sem("shift_turned"), sem("shift_in"), sem("h_sample_done"), sem("xx_done")
        rows_t, rows_in, rows_out = sem("last_turned"), sem("last_in"), sem("last_out")
        block = ctx.enter_context(nc.Block())

        @block.sync
        def _(sp):
            nc.sync.dma_start(xs[:], io["x_sample"].rearrange("b o d -> (b o) d")).then_inc(xs_in, 16)
            nc.sync.dma_start(shin[:], io["state_shift"][0]).then_inc(xs_in, 16)
            for t in range(KC):
                nc.sync.dma_start(xin[:, t, :], io["x_prompt"][0, t * P:(t + 1) * P, :]).then_inc(x_in[t], 16)
            for c in range(KC):
                sp.wait_ge(staged, c + 1)
                nc.sync.dma_start(m.xt[c], stage[:, c % 2, :]).then_inc(xt_out[c % 2], 16)
            sp.wait_ge(rows_in, 1)
            nc.sync.dma_start(io["shift_prompt"][0], lastrows[0:1, :]).then_inc(rows_out, 16)
            nc.sync.dma_start(io["shift_sample"][0], lastrows[1:1 + NS, :]).then_inc(rows_out, 16)
            sp.wait_ge(rows_out, 32)
            for p in range(2):
                sp.wait_ge(xt_out[p], 16 * KC // 2)

        @block.tensor
        def _(pe):
            pe.wait_ge(xs_in, 32)
            for k in range(KC):
                last = nc.tensor.transpose(m.aux[0][:, k * NS:(k + 1) * NS], shin[:, k * P:(k + 1) * P], m.ident[0:NS, 0:NS])
            last.then_inc(sh_t, 1)
            for c in range(KC):
                if c >= 2:
                    pe.wait_ge(staged, c - 1)
                for t in range(KC):
                    if c == 0:
                        pe.wait_ge(x_in[t], 16)
                    nc.tensor.transpose(m.acc[c % 2][:, t // 4, (t % 4) * P:(t % 4 + 1) * P], xin[:, t, c * P:(c + 1) * P],
                                        m.ident[:])
                nc.tensor.transpose(m.acc[c % 2][:, 2, 0:NS], xs[:, c * P:(c + 1) * P], m.ident[0:NS, 0:NS]).then_inc(turned, 1)
            pe.wait_ge(h_done, KC)
            pe.wait_ge(hs_done, 2)
            n = 1 + NS
            for c in range(KC):
                last = nc.tensor.transpose(m.acc[0][0:n, c // 4, (c % 4) * P:(c % 4 + 1) * P], h[:, c, SEQ - 1:T], m.ident[:])
            last.then_inc(rows_t, 1)

        @block.scalar
        def _(act):
            for c in range(KC):
                act.wait_ge(turned, c + 1)
                if c >= 2:
                    act.wait_ge(xt_out[c % 2], 16 * (c // 2))
                    act.wait_ge(h_done, c - 1)
                nc.scalar.activation(stage[:, c % 2, 0:SEQ].rearrange("p (a n) -> p a n", a=2), m.acc[c % 2][:, 0:2, :],
                                     ACT.Copy)
                nc.scalar.activation(stage[:, c % 2, SEQ:T], m.acc[c % 2][:, 2, 0:NS], ACT.Copy).then_inc(staged, 1)
            act.wait_ge(rows_t, 1)
            nc.scalar.activation(lastrows[:].rearrange("p (a n) -> p a n", a=2), m.acc[0][0:1 + NS, 0:2, :],
                                 ACT.Copy).then_inc(rows_in, 1)

        @block.vector
        def _(dve):
            dve.wait_ge(sh_t, 1)
            nc.vector.tensor_copy(shT[:], m.aux[0][:, 0:KC * NS].rearrange("p (k n) -> p k n", k=KC)).then_inc(sh_in, 1)
            for c in range(KC):
                dve.wait_ge(staged, c + 1)
                nc.vector.tensor_copy(h[:, c, SEQ:T], stage[:, c % 2, SEQ:T])
                nc.vector.tensor_scalar(h[:, c, 0:SEQ], stage[:, c % 2, 0:SEQ], m.mod(M_SCM, c), m.mod(M_SHM, c),
                                        ALU.mult, ALU.add).then_inc(h_done, 1)
            dve.wait_ge(h_done, KC)
            hs = h[:, :, SEQ:T]
            nc.vector.tensor_tensor(hs, hs, m.mods[:, M_SCM, :, 1:], ALU.mult).then_inc(hs_done, 1)
            dve.wait_ge(hs_done, 1)
            nc.vector.tensor_tensor(hs, hs, m.mods[:, M_SHM, :, 1:], ALU.add).then_inc(hs_done, 1)
            dve.wait_ge(hs_done, 2)
            nc.vector.tensor_tensor(xx[:, :, 1:SEQ], h[:, :, 0:SEQ - 1], h[:, :, 1:SEQ], ALU.subtract)
            nc.vector.tensor_scalar(xx[:, :, 0:1], h[:, :, 0:1], -1.0, None, ALU.mult)
            dve.wait_ge(sh_in, 1)
            nc.vector.tensor_tensor(xx[:, :, SEQ:T], shT[:], hs, ALU.subtract).then_inc(xx_done, 1)


def project_phase(m, h, xx):
    nc, io = m.nc, m.io
    with ExitStack() as ctx:
        def sb(name, shape, dt=F32):
            return ctx.enter_context(nc.sbuf_tensor(name, shape, dt))

        def sem(name):
            return m.phase_sem(name)

        xh = sb("mix_hi", [P, KC, T], F32R)
        xl = sb("mix_lo", [P, KC, T], F32R)
        lw1 = sb("lora_w", [64, T])
        la1 = sb("lora_a", [64, T])
        lg1 = sb("lora_g", [P, T])
        lg2 = sb("lora_g_tail", [32, T])
        w2w = sb("w2_w", [64, D])
        w2a = sb("w2_a", [64, D])
        w2g = sb("w2_g", [P, D])
        w2t = sb("w2_g_tail", [32, D])
        tmp = sb("mix_tmp", [P, T])
        stage = sb("proj_stage", [P, 2, T])
        mixes = [(0, [P] * KC), (1, [P] * KC), (2, [P] * KC), (3, [64]), (4, [64]), (5, [P, 32])]
        w_src = {3: io["a_w1"][0], 4: io["a_a1"][0], 5: io["a_g1"][0]}
        scr_flat = m.scr.rearrange("j c p t -> (j c) p t")
        mix_f, mix_h, mix_l, x_free = sem("mix_made"), sem("mix_hi_made"), sem("mix_lo_made"), sem("mix_chunk_free")
        w2_in, out_done = sem("w2_in"), [sem("scratch_out0"), sem("scratch_out1")]
        mm2, st2, fin2, out2 = sem("mm2"), sem("stage2_in"), sem("decay_done"), [sem("out2_0"), sem("out2_1")]
        block = ctx.enter_context(nc.Block())
        s0 = m.slabs
        NL = 4
        sL = s0 + 3 * KC

        @block.sync
        def _(sp):
            for j in range(3):
                w = io["a_w_rkv"][0, j]
                for q in range(2):
                    ring_load(m, sp, slab_of(w, q), s0 + j * KC + q, q, first=(j == 0 and s0 == 0))
                with sp.Fori(1, KC // 2) as i:
                    for q in range(2):
                        ring_load(m, sp, slab_at(w, i * 2 + q), i * 2 + (s0 + j * KC + q), q)
            n = 0
            for j in (3, 4, 5):
                for mo, width in enumerate(mixes[j][1]):
                    ring_load(m, sp, slab_of(w_src[j], mo, width), sL + n, n % 2, width)
                    n += 1

        @block.gpsimd
        def _(pool):
            nc.gpsimd.dma_start(w2w[:], io["a_w2"][0]).then_inc(w2_in, 16)
            nc.gpsimd.dma_start(w2a[:], io["a_a2"][0]).then_inc(w2_in, 16)
            nc.gpsimd.dma_start(w2g[:], io["a_g2"][0, 0:P, :]).then_inc(w2_in, 16)
            nc.gpsimd.dma_start(w2t[:], io["a_g2"][0, P:160, :]).then_inc(w2_in, 16)
            for j in range(3):
                with pool.Fori(0, KC // 2) as i:
                    for q in range(2):
                        ring_low(m, pool, i * 2 + (s0 + j * KC + q), q)
            n = 0
            for j in (3, 4, 5):
                for width in mixes[j][1]:
                    ring_low(m, pool, sL + n, n % 2, width)
                    n += 1

        @block.tensor
        def _(pe):
            for j in range(3):
                for q in range(2):
                    ring_mul(m, pe, s0 + j * KC + q, q, xh, xl, first=(j == 0 and s0 == 0),
                             ready=(mix_l, KC * j) if q == 0 else None)
                with pe.Fori(1, KC // 2 - 1) as i:
                    for q in range(2):
                        ring_mul(m, pe, i * 2 + (s0 + j * KC + q), q, xh, xl)
                for q in range(2):
                    ring_mul(m, pe, s0 + j * KC + KC - 2 + q, q, xh, xl, free=x_free if q else None)
            n = 0
            for j in (3, 4, 5):
                for i, width in enumerate(mixes[j][1]):
                    ring_mul(m, pe, sL + n, n % 2, xh, xl, width, ready=(mix_l, KC * j) if i == 0 else None,
                             free=x_free if j < 5 else None)
                    n += 1
            pe.wait_ge(w2_in, 64)
            for p in range(2):
                pe.wait_ge(m.acc_free[p], sL + NL)
            for u in range(3 * KC):
                kind, mo = u // KC, u % KC
                if u >= 2:
                    pe.wait_ge(st2, u - 1)
                parts = {0: [(w2w, lw1)], 1: [(w2a, la1)], 2: [(w2g, lg1), (w2t, lg2)]}[kind]
                for g in range(NG):
                    for i, (w, x) in enumerate(parts):
                        last = nc.tensor.matmul(m.acc[u % 2][:, g, 0:G], w[:, mo * P:(mo + 1) * P], x[:, g * G:(g + 1) * G],
                                                start=(i == 0), stop=(i == len(parts) - 1))
                last.then_inc(mm2, 1)

        @block.vector
        def _(dve):
            for j in range(6):
                for c in range(KC):
                    if j and c < KC - 1:
                        dve.wait_ge(x_free, (KC - 1) * (j - 1) + c + 1)
                    elif j:
                        dve.wait_ge(m.mm_done, s0 + KC * j if j <= 3 else sL + j - 3)
                    if j or c:
                        dve.wait_ge(mix_l, j * KC + c)
                    nc.vector.scalar_tensor_tensor(tmp[:], xx[:, c, :], m.vec(V_MU + j, c), h[:, c, :],
                                                   ALU.mult, ALU.add).then_inc(mix_f, 1)
                    dve.wait_ge(mix_f, j * KC + c + 1)
                    nc.vector.tensor_copy(xh[:, c, :], tmp[:]).then_inc(mix_h, 1)
                    dve.wait_ge(mix_h, j * KC + c + 1)
                    nc.vector.tensor_tensor(xl[:, c, :], tmp[:], xh[:, c, :].bitcast(F32), ALU.subtract).then_inc(mix_l, 1)
            for u in range(KC):
                dve.wait_ge(st2, u + 1)
                nc.vector.tensor_scalar(stage[:, u % 2, :], stage[:, u % 2, :], DECAY_SCALE, None,
                                        ALU.mult).then_inc(fin2, 1)

        @block.scalar
        def _(act):
            def store(s, chunk, p, stored):
                act.wait_ge(m.mm_done, s + 1)
                if stored is not None:
                    act.wait_ge(out_done[p], stored)
                nc.scalar.activation(as3(stage[:, p, :]), acc_view(m, p), ACT.Copy).then_inc(m.acc_free[p], 2)
                act.wait_ge(m.acc_free[p], s - p + 2)
                nc.scalar.dma_start(scr_flat[bass.ds(chunk + S_R * KC, 1)].rearrange("a p t -> (a p) t"),
                                    stage[:, p, :]).then_inc(out_done[p], 16)

            widths = [64, 64, P, 32]
            for p in range(2):
                ring_high(m, act, s0 + p, p, landed_at(s0 + p), first=(s0 == 0))
            for p in range(2):
                ring_high(m, act, s0 + 2 + p, p, landed_at(s0 + 2 + p))
                store(s0 + p, p, p, None)
            with act.Fori(1, 3 * KC // 2 - 1) as i:
                for p in range(2):
                    ring_high(m, act, i * 2 + (s0 + 2 + p), p, i * 16 + landed_at(s0 + 2 + p))
                    store(i * 2 + (s0 + p), i * 2 + p, p, i * 16)
            for p in range(2):
                ring_high(m, act, sL + p, p, landed_at(sL + p), widths[p])
                store(sL - 2 + p, 3 * KC - 2 + p, p, 16 * (3 * KC // 2 - 1))
            outs = [(lw1, ACT.Tanh, 1.0), (la1, ACT.Copy, 1.0), (lg1, ACT.Sigmoid, 1.0), (lg2, ACT.Sigmoid, 1.0)]
            for n in range(NL):
                s = sL + n
                act.wait_ge(m.mm_done, s + 1)
                if n + 2 < NL:
                    ring_high(m, act, s + 2, n % 2, landed_at(s + 2), widths[n + 2])
                t, f, sc = outs[n]
                nc.scalar.activation(as3(t[:]), acc_view(m, n % 2, widths[n]), f, scale=sc).then_inc(m.acc_free[n % 2], 2)
            for u in range(3 * KC):
                kind, mo, p = u // KC, u % KC, u % 2
                act.wait_ge(mm2, u + 1)
                if u < 2:
                    act.wait_ge(out_done[p], 16 * 12)
                else:
                    act.wait_ge(out2[p], 16 * (u // 2))
                if kind < 2:
                    nc.scalar.activation(as3(stage[:, p, :]), acc_view(m, p), ACT.Sigmoid,
                                         bias=m.vec(V_W0 + kind, mo)).then_inc(st2, 1)
                    if kind == 0:
                        act.wait_ge(fin2, u + 1)
                    else:
                        act.wait_ge(st2, u + 1)
                else:
                    nc.scalar.activation(as3(stage[:, p, :]), acc_view(m, p), ACT.Copy).then_inc(st2, 1)
                    act.wait_ge(st2, u + 1)
                nc.scalar.dma_start(m.scr[S_LW + kind, mo], stage[:, p, :]).then_inc(out2[p], 16)
            for p in range(2):
                act.wait_ge(out_done[p], 16 * 12)
                act.wait_ge(out2[p], 16 * 12)
        m.slabs = sL + NL


def scan_phase(m, bs, gs):
    nc, io = m.nc, m.io
    with ExitStack() as ctx:
        def sb(name, shape, dt=F32):
            return ctx.enter_context(nc.sbuf_tensor(name, shape, dt))

        sems = {}

        def S(name):
            if name not in sems:
                sems[name] = m.phase_sem(name)
            return sems[name]

        def need(eng, name, c, n=1, k=1):
            eng.wait_ge(S(name), c * n + k)

        consts = sb("scan_masks", [P, C_ALL])
        r, k, v, lw, a, g = (sb(f"pair_{x}", [P, T]) for x in ("r", "k", "v", "lw", "a", "g"))
        tiles = {"k": (k, S_K), "a": (a, S_A), "lw": (lw, S_LW), "r": (r, S_R), "v": (v, S_V), "g": (g, S_G)}
        t1, t2, t3, k2, kb = (sb(x, [P, T]) for x in ("t1", "t2", "t3", "k2", "kk_a"))
        kk = sb("kk", [P, T])
        cum = sb("cum", [P, SEQ])
        bonus, bonus_next = sb("bonus", [P, T]), sb("bonus_next", [P, T])
        reset = sb("reset", [P, SEQ])
        ar = sb("ar", [P, KC, 2, P])
        bt, kt = sb("bt", [P, KC, P]), sb("kt", [P, KC, P])
        vT, bT, kT = sb("vT", [P, KC, P]), sb("bT", [P, KC, P]), sb("kT", [P, KC, P])
        fac, facn, mid = sb("fac", [P, KC]), sb("fac_next", [P, KC]), sb("chunk_mid", [P, KC])
        smp = sb("smp", [P, P // NS, NS])
        smprow = sb("smprow", [48, P])
        ntrb = sb("ntrb", [P, 4, 4, 2, P])
        akrk = sb("akrk", [P, 4, 4, 2, P])
        xT = sb("xT", [P, 4, 4, P])
        x = sb("x", [P, 2, 4, P])
        tm = sb("tm", [P, 2, 4, P])
        st = sb("st", [P, P])
        rs, sa = sb("rs", [P, P]), sb("sa", [P, P])
        y = sb("y", [P, 16, 64])
        tail = sb("tail", [P, SEQ])
        stat, stat2 = sb("stat", [P, 16]), sb("stat2", [P, 16])
        wkv = sb("wkv_out", [64, P])
        epst = sb("eps_gn", [P, 1])
        omka = sb("one_minus_ka", [P, KC])
        ones64 = consts[:, C_BLOCK:C_BLOCK + P]
        upper = consts[:, C_UPPER:C_UPPER + 2 * P]
        NA, NBUF = NM - 2, 4
        more = sb("more_slabs", [P, 2, KC, P])
        slabs = [m.w_raw[:, 0], m.w_raw[:, 1], more[:, 0], more[:, 1]]
        n9 = 1 + NS
        mods_ps = m.acc[0][:, 2, 0:NA * n9]
        psx, pst, psT = [m.acc[q][:, 1, :] for q in range(2)], [m.acc[q][:, 0, :] for q in range(2)], \
            [m.acc[q][:, 2, :] for q in range(2)]
        chunks = "p (j n) -> p j n"
        block = ctx.enter_context(nc.Block())

        def lev(l):
            return consts[:, C_LEVEL + l * P:C_LEVEL + (l + 1) * P].unsqueeze(1).to_broadcast([P, 4, P])

        def halves(ap, l, second):
            return ap.rearrange("p u (m s b) -> p u m s b", s=2, b=2 ** l)[:, :, :, second, :]

        def unit_half(ap, l, second):
            return ap.rearrange("p (m s b) -> p m s b", s=2, b=2 ** l)[:, :, second, :]

        def loop(eng, body):
            body(0, True, False)
            with eng.Fori(1, KC - 1) as c:
                body(c, False, False)
            body(KC - 1, False, True)

        def col(vi, c, d=0):
            return m.vecs[:, bass.ds(c + (vi * KC + d), 1)]

        @block.sync
        def _(sp):
            nc.sync.dma_start(consts[:], io["masks"]).then_inc(S("masks_in"), 16)
            last_use = {"k": "nrm2", "a": "kb", "lw": "at", "r": "smp_v", "v": "vT", "g": "gated"}

            def load(name, c, d, wait=True):
                tile, j = tiles[name]
                if wait:
                    need(sp, last_use[name], c)
                nc.sync.dma_start(tile[:], m.scr[j, bass.ds(c + d, 1)].rearrange("a p t -> (a p) t")).then_inc(S("in_" + name), 16)

            def slab_load(n, c):
                w, at = (io["ada_w"][(n + 2) // 6], (n + 2) % 6) if n < 10 else (io["kv_ada_w"], n - 10)
                nc.sync.dma_start(slabs[n % NBUF], w[:, bass.ds(c * P + at * D, P)].rearrange("(k p) n -> p k n", p=P)
                                  ).then_inc(S(f"slab_in{n % NBUF}"), 16)

            for name in tiles:
                load(name, 0, 0, False)

            def body(c, first, last):
                if not last:
                    for name in ("k", "a", "lw", "r", "v"):
                        load(name, c, 1)
                need(sp, "smprow", c)
                nc.sync.dma_start(m.srows[:, :, bass.ds(c * P, P)].rearrange("v b n -> (v b) n"), smprow[:]).then_inc(S("smp_out"), 16)
                if not first:
                    need(sp, "slab_mm", c - 1, NA, NA)
                for n in range(NA):
                    if n >= NBUF:
                        need(sp, "slab_mm", c, NA, n - NBUF + 1)
                    slab_load(n, c)
                need(sp, "wkv", c)
                nc.sync.dma_start(io["wkv_prompt"][0, 0, bass.ds(c * 2, 2)].rearrange("h i j -> i h j"),
                                  wkv[:].rearrange("i (h j) -> i h j", h=2)).then_inc(S("wkv_out"), 16)
                need(sp, "gated", c)
                nc.sync.dma_start(m.scr[S_MIX, bass.ds(c, 1), :, 0:SEQ].rearrange("a p t -> (a p) t"), tail[:]).then_inc(S("mixed_out"), 16)
                if not last:
                    load("g", c, 1)

            loop(sp, body)
            for name in ("smp_out", "wkv_out", "mixed_out"):
                sp.wait_ge(S(name), 16 * KC)

        @block.gpsimd
        def _(pool):
            def body(c, first, last):
                for q in range(4):
                    need(pool, "ntrb", c, 4, q + 1)
                    if not first:
                        need(pool, "y_mm", c - 1, KC, KC)
                    nc.gpsimd.tensor_tensor(xT[:, q], ntrb[:, q, :, 0, :], lev(0), ALU.mult).then_inc(S("xt0"), 1)
                    need(pool, "xt0", c, 4, q + 1)
                    nc.gpsimd.tensor_tensor(xT[:, q], xT[:, q], m.ident[:].unsqueeze(1).to_broadcast([P, 4, P]),
                                            ALU.add).then_inc(S("xt1"), 1)
            pool.wait_ge(S("masks_in"), 16)
            loop(pool, body)

        @block.tensor
        def _(pe):
            def body(c, first, last_pair):
                def cols3(dst, src):
                    for gi in range(NG):
                        last = nc.tensor.matmul(dst[:, gi, 0:G], ones64, src[:, gi * G:(gi + 1) * G], start=True, stop=True)
                    return last

                if not first:
                    need(pe, "yT_in", c - 1)
                    need(pe, "st_in", c - 1, KC, KC)

                def head_sums(d):
                    need(pe, "sq", c, 1, 1 + d)
                    cols3(m.acc[0], t1).then_inc(S("ss_mm"), 1)
                    need(pe, "rk", c, 1, 1 + d)
                    cols3(m.acc[1], t3).then_inc(S("bonus_mm"), 1)

                if first:
                    head_sums(0)
                need(pe, "smp_v", c)
                nc.tensor.transpose(m.aux[0][:, 0:P], smp[:].rearrange("p v b -> p (v b)"), m.ident[:]).then_inc(S("smp_t"), 1)
                need(pe, "nrm", c)
                for name, src, dst, q in (("vT_t", v, vT, 0), ("bT_t", bt, bT, 1), ("kT_t", kt, kT, 0)):
                    if name == "bT_t":
                        need(pe, "bt", c)
                        need(pe, "bonus", c)
                    if name == "kT_t":
                        need(pe, "kt", c)
                        need(pe, "vT", c)
                    for j in range(KC):
                        s_ = src[:, j * P:(j + 1) * P] if name == "vT_t" else src[:, j, :]
                        last = nc.tensor.transpose(m.acc[q][:, j // 4, (j % 4) * P:(j % 4 + 1) * P], s_, m.ident[:])
                    last.then_inc(S(name), 1)
                need(pe, "at", c)
                need(pe, "rt", c)

                def unit(gq, u):
                    return 2 * gq + u % 2, 64 * (u // 2)

                def products(gq):
                    q = gq % 2
                    if gq < 2:
                        need(pe, "bT" if q == 1 else "kT", c)
                    else:
                        need(pe, "xt_in", c, 4 * 7, 14)
                    for lhs, name, back in ((bt, "ntrb_mm", None), (kt, "akrk_mm", "ntrb")):
                        if back:
                            need(pe, back, c, 4, gq + 1)
                        for u in range(4):
                            j, h0 = unit(gq, u)
                            last = nc.tensor.matmul(m.acc[q][:, u // 2, (u % 2) * 256:(u % 2) * 256 + 256],
                                                    lhs[h0:h0 + 64, j, :],
                                                    ar[h0:h0 + 64, j].rearrange("p a n -> p (a n)"), start=True, stop=True)
                        last.then_inc(S(name), 1)

                def seed(gq):
                    q = gq % 2
                    need(pe, "xt1", c, 4, gq + 1)
                    need(pe, "akrk", c, 4, gq + 1)
                    for u in range(4):
                        nc.tensor.matmul(psx[q][:, u * P:(u + 1) * P], xT[:, gq, u, :], m.ident[:], start=(u == 0), stop=(u == 3),
                                         skip_group_check=True)
                        last = nc.tensor.matmul(psT[q][:, u * P:(u + 1) * P], m.ident[:], xT[:, gq, u, :], start=(u == 0),
                                                stop=(u == 3), skip_group_check=True)
                    last.then_inc(S("lev_mm"), 1)

                def level_t(gq, l):
                    q = gq % 2
                    need(pe, "x_in", c, 4 * 6, 6 * 2 * (gq // 2) + 2 * (l - 1) + q + 1)
                    for u in range(4):
                        last = nc.tensor.matmul(unit_half(pst[q][:, u * P:(u + 1) * P], l, 0), ntrb[:, gq, u, 0, :],
                                                unit_half(x[:, q, u, :], l, 0), start=True, stop=True)
                    last.then_inc(S("t_mm"), 1)

                def level_x(gq, l):
                    q = gq % 2
                    need(pe, "t_in", c, 4 * 6, 6 * 2 * (gq // 2) + 2 * (l - 1) + q + 1)
                    need(pe, "xt_in", c, 4 * 7, 7 * 2 * (gq // 2) + 2 * (l - 1) + q + 1)
                    for u in range(4):
                        if l < 6:
                            nc.tensor.matmul(unit_half(psx[q][:, u * P:(u + 1) * P], l, 0), xT[:, gq, u, :],
                                             unit_half(tm[:, q, u, :], l, 0), start=False, stop=False, skip_group_check=True)
                        last = nc.tensor.matmul(unit_half(psT[q][:, u * P:(u + 1) * P], l, 1), tm[:, q, u, :],
                                                unit_half(xT[:, gq, u, :], l, 1), start=False, stop=False,
                                                skip_group_check=True)
                    last.then_inc(S("lev_mm"), 1)

                def chain_r(j):
                    gq, ub = j // 2, j % 2
                    if j == 0:
                        need(pe, "smprow", c)
                    if j:
                        need(pe, "y", c, KC, j)
                    else:
                        need(pe, "st_zero", c)
                    need(pe, "xt_in", c, 4 * 7, 28 if j > 3 else 14)
                    for hd in range(2):
                        h = slice(64 * hd, 64 * hd + 64)
                        nc.tensor.matmul(m.aux[hd][:, 0:64], ar[h, j, 0, :], st[h, 0:64], start=True, stop=False)
                        last = nc.tensor.matmul(m.aux[hd][:, 0:64], akrk[:, gq, ub + 2 * hd, 0, :], vT[:, j, h], start=False, stop=True)
                    last.then_inc(S("r_mm"), 1)

                def chain_s(j):
                    gq, ub = j // 2, j % 2
                    need(pe, "rs", c, KC, j + 1)
                    for hd in range(2):
                        h = slice(64 * hd, 64 * hd + 64)
                        last = nc.tensor.matmul(m.aux[hd][:, 64:128], xT[:, gq, ub + 2 * hd, :], rs[:, h], start=True, stop=True)
                    last.then_inc(S("sa_mm"), 1)

                def chain_y(j):
                    gq, ub = j // 2, j % 2
                    need(pe, "sa", c, KC, j + 1)
                    if j:
                        need(pe, "y", c, KC, j)
                    elif not first:
                        need(pe, "wkv", c - 1)
                    for hd in range(2):
                        h = slice(64 * hd, 64 * hd + 64)
                        o = m.aux[hd][h, 256:320]
                        nc.tensor.matmul(o, kT[:, j, h], vT[:, j, h], start=True, stop=False)
                        nc.tensor.matmul(o, bT[:, j, h], sa[:, h], start=False, stop=False)
                        last = nc.tensor.matmul(o, m.ident[:, h], st[:, 0:64], start=False, stop=True)
                    last.then_inc(S("st_mm"), 1)
                    for hd in range(2):
                        h = slice(64 * hd, 64 * hd + 64)
                        o = m.aux[hd][:, 128:192]
                        nc.tensor.matmul(o, ar[h, j, 1, :], st[h, 0:64], start=True, stop=False)
                        nc.tensor.matmul(o, akrk[:, gq, ub + 2 * hd, 1, :], vT[:, j, h], start=False, stop=False)
                        last = nc.tensor.matmul(o, ntrb[:, gq, ub + 2 * hd, 1, :], sa[:, h], start=False, stop=True)
                    last.then_inc(S("y_mm"), 1)

                def chain(n):
                    j, step = n // 3, n % 3
                    (chain_r, chain_s, chain_y)[step](j)

                for half in range(2):
                    if half and not last_pair:
                        need(pe, "xt_in", c, 4 * 7, 14)
                        head_sums(1)
                        need(pe, "nrm", c, 1, 2)
                    products(2 * half)
                    if half and not last_pair:
                        need(pe, "bonus", c, 1, 2)
                    products(2 * half + 1)
                    seed(2 * half)
                    seed(2 * half + 1)
                    n = 0
                    for l in range(1, 7):
                        for stage in (level_t, level_x):
                            stage(2 * half, l)
                            stage(2 * half + 1, l)
                            if half:
                                chain(n)
                                n += 1
                def slab_mul(n, ks):
                    if ks[0] == 0:
                        pe.wait_ge(S(f"slab_in{n % NBUF}"), c * (16 * (NA // NBUF)) + 16 * (n // NBUF + 1))
                    for k in ks:
                        last = nc.tensor.matmul(m.acc[1][0:n9, n // 4, (n % 4) * P:(n % 4 + 1) * P], m.cT[:, k, :],
                                                slabs[n % NBUF][:, k, :],
                                                start=(k == 0), stop=(k == KC - 1))
                    if ks[-1] == KC - 1:
                        last.then_inc(S("slab_mm"), 1)

                need(pe, "xt_in", c, 4 * 7, 28)
                for n in range(12, 24):
                    chain(n)
                    slab_mul((n - 12) // 2, range(4) if n % 2 == 0 else range(4, KC))
                need(pe, "y", c, KC, KC)
                nc.tensor.transpose(m.aux[1][:, 384:512], st[:], m.ident[:]).then_inc(S("wkv_t"), 1)
                for n in range(NA // 2, NA):
                    slab_mul(n, range(KC))
                need(pe, "yn", c)
                for j in range(KC):
                    last = nc.tensor.transpose(m.acc[0][:, j // 4, (j % 4) * P:(j % 4 + 1) * P],
                                               y[:, 2 * j:2 * j + 2, :].rearrange("p h n -> p (h n)"), m.ident[:])
                last.then_inc(S("yT_t"), 1)
                need(pe, "mod_rows", c)
                for n in range(NA):
                    rows = x[0:n9, n // 4, n % 4, :] if n < 8 else tm[0:n9, 0, n % 4, :]
                    last = nc.tensor.matmul(mods_ps[:, n * n9:(n + 1) * n9], rows, m.ident[0:n9, 0:n9], start=True, stop=True)
                last.then_inc(S("mod_t"), 1)
            pe.wait_ge(S("masks_in"), 16)
            loop(pe, body)

        @block.scalar
        def _(act):
            def square(c, d):
                need(act, "in_k", c, 16, 16 + 16 * d)
                nc.scalar.activation(t1[:], k[:], ACT.Square, scale=col(V_KK, c, d)).then_inc(S("sq"), 1)

            def norm(c, d):
                need(act, "ss_mm", c, 1, 1 + d)
                nc.scalar.activation(as3(t2[:]), m.acc[0][:, :, 0:G], ACT.Sqrt).then_inc(S("nrm"), 1)

            def exp_p(c, d):
                need(act, "lc", c, 1, 1 + d)
                nc.scalar.activation(t1[:, 0:SEQ], cum[:], ACT.Exp).then_inc(S("ep"), 1)

            def exp_before(c, d):
                need(act, "lx", c, 1, 1 + d)
                nc.scalar.activation(lw[:, 0:SEQ], lw[:, 0:SEQ], ACT.Exp).then_inc(S("ex"), 1)
                need(act, "smp_w", c, 1, 1 + d)
                nc.scalar.activation(smp[:, 1, :], smp[:, 1, :], ACT.Exp).then_inc(S("smp_w2"), 1)

            def exp_inverse(c, d):
                need(act, "bonus_mm", c, 1, 1 + d)
                nc.scalar.activation(t3[:, 0:SEQ], cum[:], ACT.Exp, scale=-1.0).then_inc(S("en"), 1)

            def body(c, first, last_pair):
                if first:
                    square(c, 0)
                    norm(c, 0)
                    exp_p(c, 0)
                    exp_before(c, 0)
                    exp_inverse(c, 0)
                need(act, "fac0", c, 2, 2)
                if not first:
                    need(act, "st_in", c - 1, KC, KC)
                nc.scalar.activation(fac[:], facn[:], ACT.Exp).then_inc(S("fac"), 1)
                need(act, "smp_t", c)
                if not first:
                    act.wait_ge(S("smp_out"), c * 16)
                nc.scalar.activation(smprow[:], m.aux[0][0:48, 0:P], ACT.Copy).then_inc(S("smprow"), 1)
                for name, dst, q in (("vT", vT, 0), ("bT", bT, 1), ("kT", kT, 0)):
                    need(act, name + "_t", c)
                    nc.scalar.activation(dst[:].rearrange("p (a j) n -> p a (j n)", a=2), m.acc[q][:, 0:2, :],
                                         ACT.Copy).then_inc(S(name), 1)
                ch = [0]

                def chain_in(n):
                    j, step = n // 3, n % 3
                    if step == 0:
                        need(act, "r_mm", c, KC, j + 1)
                        nc.scalar.activation(rs[:].rearrange("p (h n) -> p h n", h=2), m.aux2[:, :, 0:64], ACT.Copy).then_inc(S("rs"), 1)
                    elif step == 1:
                        need(act, "sa_mm", c, KC, j + 1)
                        nc.scalar.activation(sa[:].rearrange("p (h n) -> p h n", h=2), m.aux2[:, :, 64:128], ACT.Copy).then_inc(S("sa"), 1)
                    else:
                        need(act, "y_mm", c, KC, j + 1)
                        for h in (slice(0, 64), slice(64, P)):
                            last = nc.scalar.activation(st[h, 0:64], m.aux2[h, h.start // 64, 256:320], ACT.Copy,
                                                        scale=fac[h, j:j + 1])
                        last.then_inc(S("st_in"), 1)
                        nc.scalar.activation(y[:, 2 * j:2 * j + 2, :], m.aux2[:, :, 128:192],
                                             ACT.Copy).then_inc(S("y"), 1)

                for half in range(2):
                    def x_in(q, l):
                        xd, td = x[:, q], xT[:, 2 * half + q]
                        xs_, ts_ = (t.rearrange("p (u n) -> p u n", u=4) for t in (psx[q], psT[q]))
                        if l:
                            xd, xs_, td, ts_ = halves(xd, l, 0), halves(xs_, l, 0), halves(td, l, 1), halves(ts_, l, 1)
                        if l < 6:
                            nc.scalar.activation(xd, xs_, ACT.Copy).then_inc(S("x_in"), 1)
                        nc.scalar.activation(td, ts_, ACT.Copy).then_inc(S("xt_in"), 1)

                    for q in range(2):
                        need(act, "lev_mm", c, 4 * 7, 14 * half + q + 1)
                        x_in(q, 0)
                    for l in range(1, 7):
                        if not last_pair:
                            if not half and l == 2:
                                need(act, "rt", c)
                                square(c, 1)
                            if half and l == 2:
                                exp_p(c, 1)
                            if half and l == 3:
                                exp_before(c, 1)
                            if half and l == 4:
                                exp_inverse(c, 1)
                        for q in range(2):
                            if half and q == 0:
                                chain_in(2 * (l - 1))
                            need(act, "lev_mm", c, 4 * 7, 14 * half + 2 * l + q + 1)
                            x_in(q, l)
                        if half:
                            chain_in(2 * (l - 1) + 1)
                    if not half and not last_pair:
                        need(act, "kk_done", c)
                        norm(c, 1)
                for n in range(12, 24):
                    chain_in(n)
                need(act, "wkv_t", c)
                if not first:
                    act.wait_ge(S("wkv_out"), c * 16)
                nc.scalar.activation(wkv[:], m.aux[1][0:64, 384:512], ACT.Copy).then_inc(S("wkv"), 1)
                need(act, "yc", c)
                if not first:
                    act.wait_ge(S("mixed_out"), c * 16)
                nc.scalar.activation(tail[:], y[:].rearrange("p h n -> p (h n)"), ACT.Square).then_inc(S("ysq"), 1)
                need(act, "var", c)
                nc.scalar.activation(stat2[:], stat[:], ACT.Sqrt, bias=epst[:, 0:1], scale=1.0 / 64).then_inc(S("std"), 1)
                need(act, "slab_mm", c, NA, NA)
                nc.scalar.activation(x[0:n9].rearrange("p q u n -> p q (u n)"), m.acc[1][0:n9, 0:2, :], ACT.Copy)
                nc.scalar.activation(tm[0:n9, 0].rearrange("p u n -> p (u n)"), m.acc[1][0:n9, 2, :],
                                     ACT.Copy).then_inc(S("mod_rows"), 1)
                need(act, "yT_t", c)
                nc.scalar.activation(tail[:].rearrange("p (a n) -> p a n", a=2), m.acc[0][:, 0:2, :], ACT.Identity,
                                     bias=col(V_GNB, c), scale=col(V_GNG, c)).then_inc(S("yT_in"), 1)
            act.wait_ge(S("consts"), 5)
            loop(act, body)

        @block.vector
        def _(dve):
            dve.wait_ge(S("masks_in"), 16)
            nc.vector.memset(epst[:], GN_EPS).then_inc(S("consts"), 1)
            nc.vector.memset(st[:], 0.0).then_inc(S("consts"), 1)
            nc.vector.memset(smp[:], 0.0).then_inc(S("consts"), 1)
            nc.vector.tensor_scalar(omka[:], m.vecs[:, V_KA * KC:(V_KA + 1) * KC], -1.0, 1.0, ALU.mult, ALU.add).then_inc(S("consts"), 1)
            nc.vector.tensor_copy(reset[:].rearrange(chunks, j=KC),
                                  consts[:, C_RESET:C_RESET + P].unsqueeze(1).to_broadcast([P, KC, P])).then_inc(S("consts"), 1)
            dve.wait_ge(S("consts"), 5)

            V = nc.vector

            def keys(c, d, step):
                if step == 0:
                    need(dve, "in_a", c, 16, 16 + 16 * d)
                    need(dve, "in_k", c, 16, 16 + 16 * d)
                    V.tensor_scalar(k2[:], a[:], col(V_KA, c, d), omka[:, bass.ds(c + d, 1)], ALU.mult, ALU.add).then_inc(S("k2a"), 1)
                if step == 1:
                    V.tensor_scalar(kk[:], k[:], col(V_KK, c, d), None, ALU.mult).then_inc(S("kkf"), 1)
                if step == 2:
                    need(dve, "k2a", c, 1, 1 + d)
                    V.tensor_tensor(k2[:], k2[:], k[:], ALU.mult).then_inc(S("k2"), 1)
                if step == 3:
                    need(dve, "in_r", c, 16, 16 + 16 * d)
                    need(dve, "k2", c, 1, 1 + d)
                    V.scalar_tensor_tensor(t3[:], r[:], col(V_RK, c, d), k2[:], ALU.mult, ALU.mult).then_inc(S("rk"), 1)

            def decays(c, d, step):
                c3 = cum[:].rearrange(chunks, j=KC)
                if step == 0:
                    need(dve, "in_lw", c, 16, 16 + 16 * d)
                    V.tensor_tensor_scan(cum[:], reset[:], lw[:, 0:SEQ], 0.0, ALU.mult, ALU.add).then_inc(S("scan"), 1)
                    if d:
                        need(dve, "smp_t", c)
                    V.tensor_copy(smp[:, 1, :], lw[:, SEQ:T]).then_inc(S("smp_w"), 1)
                if step == 1:
                    need(dve, "scan", c, 1, 1 + d)
                    if d:
                        need(dve, "fac", c)
                    V.tensor_tensor(facn[:, 0:KC - 1], c3[:, 0:KC - 1, P - 1], c3[:, 1:KC, 63], ALU.add)
                    V.tensor_copy(facn[:, KC - 1:KC], c3[:, KC - 1, P - 1:P]).then_inc(S("fac0"), 1)
                    need(dve, "fac0", c, 2, 1 + 2 * d)
                    V.tensor_tensor(facn[:], facn[:], c3[:, :, 63], ALU.subtract).then_inc(S("fac0"), 1)
                    V.tensor_copy(mid[:], c3[:, :, 63]).then_inc(S("mid"), 1)
                    need(dve, "mid", c, 1, 1 + d)
                    need(dve, "fac0", c, 2, 2 + 2 * d)
                    V.tensor_tensor(c3, c3, mid[:].unsqueeze(2).to_broadcast([P, KC, P]), ALU.subtract).then_inc(S("lc"), 1)
                if step == 2:
                    need(dve, "lc", c, 1, 1 + d)
                    V.tensor_tensor(lw[:, 0:SEQ], cum[:], lw[:, 0:SEQ], ALU.subtract).then_inc(S("lx"), 1)

            def take_bonus(c, d):
                need(dve, "bonus_mm", c, 1, 1 + d)
                need(dve, "in_v", c, 16, 16 + 16 * d)
                V.tensor_tensor(as3(bonus_next[:]), m.acc[1][:, :, 0:G], as3(v[:]), ALU.mult).then_inc(S("bonus"), 1)

            def guard(c, d):
                need(dve, "nrm", c, 1, 1 + d)
                V.tensor_scalar_max(t2[:], t2[:], 1e-12).then_inc(S("nrm2"), 1)

            def directions(c, d):
                need(dve, "nrm2", c, 1, 1 + d)
                V.reciprocal(t2[:], t2[:]).then_inc(S("rinv"), 1)
                need(dve, "rinv", c, 1, 1 + d)
                need(dve, "kkf", c, 1, 1 + d)
                V.tensor_tensor(kk[:], kk[:], t2[:], ALU.mult).then_inc(S("kk_done"), 1)
                need(dve, "kk_done", c, 1, 1 + d)
                V.tensor_tensor(kb[:], kk[:], a[:], ALU.mult).then_inc(S("kb"), 1)
                need(dve, "en", c, 1, 1 + d)
                need(dve, "kb", c, 1, 1 + d)
                V.tensor_tensor(bt[:].rearrange("p j n -> p (j n)"), kb[:, 0:SEQ], t3[:, 0:SEQ], ALU.mult).then_inc(S("bt"), 1)
                V.tensor_tensor(kt[:].rearrange("p j n -> p (j n)"), k2[:, 0:SEQ], t3[:, 0:SEQ], ALU.mult).then_inc(S("kt"), 1)

            def body(c, first, last_pair):
                if first:
                    for step in range(3):
                        decays(c, 0, step)
                    for step in range(4):
                        keys(c, 0, step)
                    guard(c, 0)
                    take_bonus(c, 0)
                    directions(c, 0)
                need(dve, "kk_done", c)
                need(dve, "ex", c)
                V.scalar_tensor_tensor(ar[:, :, 0, :], kk[:, 0:SEQ].rearrange(chunks, j=KC), -1.0,
                                       lw[:, 0:SEQ].rearrange(chunks, j=KC), ALU.mult, ALU.mult).then_inc(S("at"), 1)
                need(dve, "ep", c)
                V.tensor_tensor(ar[:, :, 1, :], r[:, 0:SEQ].rearrange(chunks, j=KC), t1[:, 0:SEQ].rearrange(chunks, j=KC),
                                ALU.mult).then_inc(S("rt"), 1)
                for i, src in ((0, r), (2, k2), (3, v), (5, kb)):
                    V.tensor_copy(smp[:, i, :], src[:, SEQ:T])
                need(dve, "smp_w2", c)
                V.tensor_scalar(smp[:, 4, :], kk[:, SEQ:T], -1.0, None, ALU.mult).then_inc(S("smp_v"), 1)
                need(dve, "bonus", c)
                if not first:
                    need(dve, "plus", c - 1)
                V.tensor_copy(bonus[:], bonus_next[:]).then_inc(S("bonus_in"), 1)
                need(dve, "fac", c)
                V.memset(st[:, 0:64], 0.0).then_inc(S("st_zero"), 1)
                need(dve, "smp_v", c)
                need(dve, "kt", c)

                mask4 = upper.unsqueeze(1).to_broadcast([P, 4, 2 * P])
                for half in range(2):
                    for gq in (2 * half, 2 * half + 1):
                        q = gq % 2
                        need(dve, "ntrb_mm", c, 4, gq + 1)
                        V.tensor_tensor(ntrb[:, gq].rearrange("p u a n -> p u (a n)"),
                                        m.acc[q][:, 0:2, :].rearrange("p b (u n) -> p (b u) n", u=2), mask4,
                                        ALU.mult).then_inc(S("ntrb"), 1)
                        need(dve, "akrk_mm", c, 4, gq + 1)
                        V.tensor_tensor(akrk[:, gq].rearrange("p u a n -> p u (a n)"),
                                        m.acc[q][:, 0:2, :].rearrange("p b (u n) -> p (b u) n", u=2), mask4,
                                        ALU.mult).then_inc(S("akrk"), 1)
                    if not half and not last_pair:
                        decays(c, 1, 0)
                    if half and not last_pair:
                        guard(c, 1)
                    for l in range(1, 7):
                        if not last_pair:
                            if not half and 2 <= l <= 5:
                                keys(c, 1, l - 2)
                            if half and l <= 2:
                                decays(c, 1, l)
                        for q in range(2):
                            need(dve, "t_mm", c, 4 * 6, 12 * half + 2 * (l - 1) + q + 1)
                            V.tensor_tensor(tm[:, q], pst[q].rearrange("p (u n) -> p u n", u=4), lev(l), ALU.mult).then_inc(S("t_in"), 1)
                    if not half and not last_pair:
                        take_bonus(c, 1)
                if not last_pair:
                    directions(c, 1)
                need(dve, "y", c, KC, KC)
                V.tensor_reduce(stat[:], y[:], AX.X, ALU.add).then_inc(S("ysum"), 1)
                need(dve, "ysum", c)
                V.tensor_scalar(stat2[:], stat[:], 1.0 / 64, None, ALU.mult).then_inc(S("ymean"), 1)
                need(dve, "ymean", c)
                V.tensor_tensor(y[:], y[:], stat2[:].unsqueeze(2).to_broadcast([P, 16, 64]), ALU.subtract).then_inc(S("yc"), 1)
                need(dve, "ysq", c)
                V.tensor_reduce(stat[:], tail[:].rearrange("p (h n) -> p h n", n=64), AX.X, ALU.add).then_inc(S("var"), 1)
                need(dve, "std", c)
                V.reciprocal(stat[:], stat2[:]).then_inc(S("rstd"), 1)
                need(dve, "rstd", c)
                V.tensor_tensor(y[:], y[:], stat[:].unsqueeze(2).to_broadcast([P, 16, 64]), ALU.mult).then_inc(S("yn"), 1)
                need(dve, "in_g", c, 16, 16)
                V.tensor_copy(gs[:, bass.ds(c, 1), :].rearrange("p a n -> p (a n)"), g[:, SEQ:T])
                V.tensor_copy(bs[:, bass.ds(c, 1), :].rearrange("p a n -> p (a n)"), bonus[:, SEQ:T]).then_inc(S("gs"), 1)
                need(dve, "yT_in", c)
                V.tensor_tensor(tail[:], tail[:], bonus[:, 0:SEQ], ALU.add).then_inc(S("plus"), 1)
                need(dve, "mod_t", c)
                bias = m.vecs[:, 2 * KC:NM * KC].rearrange("p (v k) -> p v k", k=KC)[:, :, bass.ds(c, 1)]
                V.tensor_tensor(m.mods[:, 2:NM, bass.ds(c, 1), :].rearrange("p v a n -> p v (a n)"),
                                mods_ps.rearrange("p (v n) -> p v n", n=n9), bias.to_broadcast([P, NA, n9]),
                                ALU.add).then_inc(S("mods"), 1)
                need(dve, "plus", c)
                V.tensor_tensor(tail[:], tail[:], g[:, 0:SEQ], ALU.mult).then_inc(S("gated"), 1)
            loop(dve, body)
            dve.wait_ge(S("mods"), KC)
            for mod in (2, 4, 5, 7, 8, 10, 11, 13):
                V.tensor_scalar_add(m.mods[:, mod, :, :], m.mods[:, mod, :, :], 1.0)


def sample_scan_phase(m, bs, gs):
    nc, io = m.nc, m.io
    with ExitStack() as ctx:
        def sb(name, shape, dt=F32):
            return ctx.enter_context(nc.sbuf_tensor(name, shape, dt))

        sems = {}

        def S(name):
            if name not in sems:
                sems[name] = m.phase_sem(name)
            return sems[name]

        vec = sb("sample_vecs", [P, 6, 64])
        st = sb("sample_state", [P, 64, 64])
        tmp = sb("sample_tmp", [P, 64, 64])
        sa, y, y2 = sb("sample_sa", [P, 64]), sb("sample_y", [P, 64]), sb("sample_y2", [P, 64])
        s1, s2, eps = sb("sum1", [P, 1]), sb("sum2", [P, 1]), sb("eps_gn_sample", [P, 1])
        yr = sb("sample_rows", [NS, D])
        yT = sb("sample_cols", [P, KC, NS])
        r, w, k, v, a, b = range(6)
        block = ctx.enter_context(nc.Block())

        def over_i(n):
            return vec[:, n, :].unsqueeze(1).to_broadcast([P, 64, 64])

        def over_j(t):
            return t.unsqueeze(2).to_broadcast([P, 64, 64])

        @block.sync
        def _(sp):
            nc.sync.dma_start(st[:], io["state_wkv"][0].rearrange("b h i j -> (b h) i j")).then_inc(S("in"), 16)
            nc.sync.dma_start(vec[:], m.srows.rearrange("v b (h n) -> (b h) v n", n=64)).then_inc(S("in"), 16)
            sp.wait_ge(S("state"), 3)
            nc.sync.dma_start(io["wkv_sample"][0].rearrange("b h i j -> (b h) i j"), st[:]).then_inc(S("state_out"), 16)
            sp.wait_ge(S("yn"), 1)
            nc.sync.dma_start(m.yrows.rearrange("b (h n) -> (b h) n", n=64), y2[:]).then_inc(S("y_out"), 16)
            sp.wait_ge(S("y_out"), 16)
            nc.sync.dma_start(yr[:], m.yrows).then_inc(S("y_back"), 16)
            sp.wait_ge(S("out"), 4)
            nc.sync.dma_start(m.scr[S_MIX, :, :, SEQ:T].rearrange("c p n -> p c n"), yT[:]).then_inc(S("mixed"), 16)
            sp.wait_ge(S("mixed"), 16)
            sp.wait_ge(S("state_out"), 16)

        @block.vector
        def _(dve):
            V = nc.vector
            V.memset(eps[:], GN_EPS).then_inc(S("eps"), 1)
            dve.wait_ge(S("in"), 32)
            V.tensor_tensor(tmp[:], st[:], over_i(a), ALU.mult).then_inc(S("sa"), 1)
            dve.wait_ge(S("sa"), 1)
            V.tensor_reduce(sa[:], tmp[:], AX.X, ALU.add).then_inc(S("sa"), 1)
            V.tensor_tensor(st[:], st[:], over_i(w), ALU.mult).then_inc(S("state"), 1)
            dve.wait_ge(S("sa"), 2)
            V.tensor_tensor(tmp[:], over_j(sa[:]), over_i(b), ALU.mult).then_inc(S("ab"), 1)
            dve.wait_ge(S("ab"), 1)
            dve.wait_ge(S("state"), 1)
            V.tensor_tensor(st[:], st[:], tmp[:], ALU.add).then_inc(S("state"), 1)
            dve.wait_ge(S("state"), 2)
            V.tensor_tensor(tmp[:], over_j(vec[:, v, :]), over_i(k), ALU.mult).then_inc(S("vk"), 1)
            dve.wait_ge(S("vk"), 1)
            V.tensor_tensor(st[:], st[:], tmp[:], ALU.add).then_inc(S("state"), 1)
            dve.wait_ge(S("state"), 3)
            V.tensor_tensor(tmp[:], st[:], over_i(r), ALU.mult).then_inc(S("sr"), 1)
            dve.wait_ge(S("sr"), 1)
            V.tensor_reduce(y[:], tmp[:], AX.X, ALU.add).then_inc(S("y"), 1)
            dve.wait_ge(S("y"), 1)
            V.tensor_reduce(s1[:], y[:], AX.X, ALU.add).then_inc(S("gn"), 1)
            dve.wait_ge(S("gn"), 1)
            V.tensor_scalar(s1[:], s1[:], -1.0 / 64, None, ALU.mult).then_inc(S("gn"), 1)
            dve.wait_ge(S("gn"), 2)
            V.tensor_scalar(y[:], y[:], s1[:, 0:1], None, ALU.add).then_inc(S("gn"), 1)
            dve.wait_ge(S("gn"), 3)
            V.tensor_tensor(y2[:], y[:], y[:], ALU.mult).then_inc(S("gn"), 1)
            dve.wait_ge(S("gn"), 4)
            V.tensor_reduce(s2[:], y2[:], AX.X, ALU.add).then_inc(S("gn"), 1)
            dve.wait_ge(S("std"), 1)
            V.reciprocal(s1[:], s2[:]).then_inc(S("gn"), 1)
            dve.wait_ge(S("gn"), 6)
            V.tensor_scalar(y2[:], y[:], s1[:, 0:1], None, ALU.mult).then_inc(S("yn"), 1)
            dve.wait_ge(S("turned"), 1)

            def per_channel(vi):
                return m.vecs[:, vi * KC:(vi + 1) * KC].unsqueeze(2).to_broadcast([P, KC, NS])

            V.tensor_tensor(yT[:], m.aux[0][:, 0:KC * NS].rearrange("p (c n) -> p c n", c=KC), per_channel(V_GNG),
                            ALU.mult).then_inc(S("out"), 1)
            for n, other, op in ((1, per_channel(V_GNB), ALU.add), (2, bs[:], ALU.add), (3, gs[:], ALU.mult)):
                dve.wait_ge(S("out"), n)
                V.tensor_tensor(yT[:], yT[:], other, op).then_inc(S("out"), 1)

        @block.scalar
        def _(act):
            act.wait_ge(S("eps"), 1)
            act.wait_ge(S("gn"), 5)
            nc.scalar.activation(s2[:], s2[:], ACT.Sqrt, bias=eps[:, 0:1], scale=1.0 / 64).then_inc(S("std"), 1)

        @block.tensor
        def _(pe):
            pe.wait_ge(S("y_back"), 16)
            for c in range(KC):
                last = nc.tensor.transpose(m.aux[0][:, c * NS:(c + 1) * NS], yr[:, c * P:(c + 1) * P], m.ident[0:NS, 0:NS])
            last.then_inc(S("turned"), 1)


class Piece:

    def __init__(self, m, ctx, tag):
        self.m, self.nc, self.ctx, self.tag, self.sems = m, m.nc, ctx, tag, {}

    def sb(self, name, shape, dt=F32):
        return self.ctx.enter_context(self.nc.sbuf_tensor(f"{self.tag}_{name}", shape, dt))

    def S(self, name):
        if name not in self.sems:
            self.sems[name] = self.m.phase_sem(f"{self.tag}_{name}")
        return self.sems[name]


class Norm(Piece):

    def __init__(self, m, ctx, tag, z, which, tmp):
        super().__init__(m, ctx, tag)
        self.z, self.which, self.tmp = z, which, tmp
        self.rstd = self.sb("rstd", [P, T])

    def tensor(self, pe):
        m, nc = self.m, self.nc
        for k in range(KC):
            for g in range(NG):
                last = nc.tensor.matmul(m.acc[0][:, g, 0:G], m.mean[:], self.z[:, k, g * G:(g + 1) * G],
                                        start=(k == 0), stop=(k == KC - 1))
        last.then_inc(self.S("mean"), 1)
        for k in range(KC):
            pe.wait_ge(self.S("squared"), k + 1)
            for g in range(NG):
                last = nc.tensor.matmul(m.acc[1][:, g, 0:G], m.mean[:], self.tmp[:, k % 2, g * G:(g + 1) * G],
                                        start=(k == 0), stop=(k == KC - 1))
            last.then_inc(self.S("var"), 1)

    def vector(self, dve):
        m, nc, z = self.m, self.nc, self.z
        dve.wait_ge(self.S("mean"), 1)
        for k in range(KC):
            nc.vector.tensor_tensor(as3(z[:, k, :]), as3(z[:, k, :]), acc_view(m, 0), ALU.subtract).then_inc(self.S("centred"), 1)
        dve.wait_ge(self.S("std"), 1)
        nc.vector.reciprocal(self.rstd[:], self.rstd[:]).then_inc(self.S("rstd"), 1)
        dve.wait_ge(self.S("rstd"), 1)
        for k in range(KC):
            nc.vector.tensor_tensor(z[:, k, :], z[:, k, :], self.rstd[:], ALU.mult).then_inc(self.S("scaled"), 1)

    def scalar(self, act):
        m, nc, z = self.m, self.nc, self.z
        for k in range(KC):
            act.wait_ge(self.S("centred"), k + 1)
            if k >= 2:
                act.wait_ge(self.S("var"), k - 1)
            nc.scalar.activation(self.tmp[:, k % 2, :], z[:, k, :], ACT.Square).then_inc(self.S("squared"), 1)
        act.wait_ge(self.S("var"), KC)
        nc.scalar.activation(as3(self.rstd[:]), acc_view(m, 1), ACT.Sqrt, bias=m.eps[:, 0:1]).then_inc(self.S("std"), 1)
        for k in range(KC):
            act.wait_ge(self.S("scaled"), k + 1)
            nc.scalar.activation(z[:, k, :], z[:, k, :], ACT.Identity, bias=m.vec(V_LNB + self.which, k),
                                 scale=m.vec(V_LNG + self.which, k)).then_inc(self.S("x"), 1)


class Modulate(Piece):

    def __init__(self, m, ctx, tag, x, scale, shift, xh, xl, tmp, alpha=False):
        super().__init__(m, ctx, tag)
        self.x, self.scale, self.shift, self.xh, self.xl, self.tmp, self.alpha = x, scale, shift, xh, xl, tmp, alpha

    def vector(self, dve, ready):
        m, nc = self.m, self.nc
        for k in range(KC):
            ready(k)
            if k >= 2:
                dve.wait_ge(self.S("lo"), k - 1)
            t, s = self.tmp[:, k % 2, :], slice(SEQ, T)
            nc.vector.tensor_tensor(t[:, s], self.x[:, k, s], m.mods[:, self.scale, k, 1:], ALU.mult).then_inc(self.S("s1"), 1)
            nc.vector.tensor_scalar(t[:, 0:SEQ], self.x[:, k, 0:SEQ], m.mod(self.scale, k), m.mod(self.shift, k),
                                    ALU.mult, ALU.add)
            dve.wait_ge(self.S("s1"), k + 1)
            nc.vector.tensor_tensor(t[:, s], t[:, s], m.mods[:, self.shift, k, 1:], ALU.add).then_inc(self.S("h"), 1)
            dve.wait_ge(self.S("h"), k + 1)
            nc.vector.tensor_copy(self.xh[:, k, :], t).then_inc(self.S("hi"), 1)

    def gpsimd(self, pool):
        for k in range(KC):
            pool.wait_ge(self.S("hi"), k + 1)
            self.nc.gpsimd.tensor_tensor(self.xl[:, k, :], self.tmp[:, k % 2, :], self.xh[:, k, :].bitcast(F32),
                                         ALU.subtract).then_inc(self.S("lo"), 1)

    def scalar(self, act):
        for k in range(KC):
            act.wait_ge(self.S("h"), k + 1)
            self.nc.scalar.activation(self.x[:, k, :], self.x[:, k, :], ACT.Copy, scale=ALPHA).then_inc(self.S("alpha"), 1)


def job_loads(m, sp, w, s, col0=0):
    with sp.Fori(0, KC // 2) as i:
        for p in range(2):
            ring_load(m, sp, slab_at(w, i * 2 + (col0 + p)), i * 2 + (s + p), p)


def job_lows(m, pool, s, n=KC):
    with pool.Fori(0, n // 2) as i:
        for p in range(2):
            ring_low(m, pool, i * 2 + (s + p), p)


def job_muls(m, pe, s, xh, xl, ready=None, free=None):
    for p in range(2):
        ring_mul(m, pe, s + p, p, xh, xl, ready=(ready, 0) if ready is not None and p == 0 else None)
    with pe.Fori(1, KC // 2 - 1) as i:
        for p in range(2):
            ring_mul(m, pe, i * 2 + (s + p), p, xh, xl)
    for p in range(2):
        ring_mul(m, pe, s + KC - 2 + p, p, xh, xl, free=free if p else None)


def add_gated(m, dve, z, gate, c, s, p, sums, tmp8):
    nc = m.nc
    dve.wait_ge(m.mm_done, s + 1)
    zc = z[:, bass.ds(c, 1), :].rearrange("p a t -> p (a t)")
    sg = m.mods[:, gate, bass.ds(c, 1), 1:].rearrange("p a n -> p (a n)")
    pg = m.mods[:, gate, bass.ds(c, 1), 0:1].rearrange("p a n -> p (a n)")
    nc.vector.tensor_tensor(tmp8[:], m.acc[p][:, 2, G - NS:G], sg, ALU.mult).then_inc(sums, 1)
    nc.vector.scalar_tensor_tensor(zc[:, 0:2 * G].rearrange("p (g n) -> p g n", g=2), m.acc[p][:, 0:2, 0:G], pg,
                                   zc[:, 0:2 * G].rearrange("p (g n) -> p g n", g=2), ALU.mult, ALU.add)
    nc.vector.scalar_tensor_tensor(zc[:, 2 * G:SEQ], m.acc[p][:, 2, 0:G - NS], pg, zc[:, 2 * G:SEQ],
                                   ALU.mult, ALU.add).then_inc(m.acc_free[p], 2)


def add_sample(m, dve, z, c, sums, tmp8, n):
    dve.wait_ge(sums, n)
    zs = z[:, bass.ds(c, 1), SEQ:T].rearrange("p a t -> p (a t)")
    m.nc.vector.tensor_tensor(zs, zs, tmp8[:], ALU.add).then_inc(sums, 1)
    dve.wait_ge(sums, n + 1)


def output_phase(m, z, layer, gate):
    nc, io = m.nc, m.io
    with ExitStack() as ctx:
        pc = Piece(m, ctx, f"out{layer}")
        xh, xl = pc.sb("hi", [P, KC, T], F32R), pc.sb("lo", [P, KC, T], F32R)
        tmp, tmp8 = pc.sb("in", [P, 2, T]), pc.sb("tmp8", [P, NS])
        w = io["a_w_o" if layer == 0 else "b_w_o"][0]
        s0 = m.slabs
        S = pc.S
        block = ctx.enter_context(nc.Block())

        @block.sync
        def _(sp):
            ring_load(m, sp, slab_of(w, 0), s0, 0)
            ring_load(m, sp, slab_of(w, 1), s0 + 1, 1)
            for k in range(KC):
                if k >= 2:
                    sp.wait_ge(S("lo"), k - 1)
                nc.sync.dma_start(tmp[:, k % 2, :], m.scr[S_MIX, k]).then_inc(S(f"in{k % 2}"), 16)
            with sp.Fori(1, KC // 2) as i:
                for p in range(2):
                    ring_load(m, sp, slab_at(w, i * 2 + p), i * 2 + (s0 + p), p)

        @block.gpsimd
        def _(pool):
            nc.gpsimd.dma_start(z[:], m.xt.rearrange("c p t -> p c t")).then_inc(S("x"), 16)
            for k in range(KC):
                pool.wait_ge(S("hi"), k + 1)
                nc.gpsimd.tensor_tensor(xl[:, k, :], tmp[:, k % 2, :], xh[:, k, :].bitcast(F32), ALU.subtract).then_inc(S("lo"), 1)
            job_lows(m, pool, s0)

        @block.tensor
        def _(pe):
            job_muls(m, pe, s0, xh, xl, ready=S("lo"))

        @block.scalar
        def _(act):
            ring_high(m, act, s0, 0, landed_at(s0))
            ring_high(m, act, s0 + 1, 1, landed_at(s0 + 1))
            act.wait_ge(S("x"), 16)
            for k in range(KC):
                nc.scalar.activation(z[:, k, :], z[:, k, :], ACT.Copy, scale=ALPHA).then_inc(S("alpha"), 1)
            with act.Fori(0, KC // 2 - 1) as i:
                for p in range(2):
                    ring_high(m, act, i * 2 + (s0 + 2 + p), p, i * 16 + landed_at(s0 + 2 + p))

        @block.vector
        def _(dve):
            for k in range(KC):
                dve.wait_ge(S(f"in{k % 2}"), 16 * (k // 2 + 1))
                nc.vector.tensor_copy(xh[:, k, :], tmp[:, k % 2, :]).then_inc(S("hi"), 1)
            dve.wait_ge(S("alpha"), KC)
            with dve.Fori(0, KC // 2) as i:
                for p in range(2):
                    add_gated(m, dve, z, gate, i * 2 + p, i * 2 + (s0 + p), p, S("sum8"), tmp8)
                    add_sample(m, dve, z, i * 2 + p, S("sum8"), tmp8, i * 4 + (2 * p + 1))
        m.slabs = s0 + KC


def mlp_phase(m, z, layer):
    nc, io = m.nc, m.io
    with ExitStack() as ctx:
        pc = Piece(m, ctx, f"mlp{layer}")
        tmp = pc.sb("tmp", [P, 2, T])
        xh, xl = pc.sb("hi", [P, KC, T], F32R), pc.sb("lo", [P, KC, T], F32R)
        hh, hl = pc.sb("hid_hi", [P, KC, T], F32R), pc.sb("hid_lo", [P, KC, T], F32R)
        tmp8 = pc.sb("tmp8", [P, NS])
        norm = Norm(m, ctx, f"norm{2 * layer}", z, 2 * layer, tmp)
        mod = Modulate(m, ctx, f"modf{layer}", z, 6 * layer + M_SCF, 6 * layer + M_SHF, xh, xl, tmp, alpha=True)
        gate = 6 * layer + M_GTF
        w1, w2 = io["ffn_w1"][layer], io["ffn_w2"][layer]
        NF = 4
        s0, e0 = m.slabs, m.staged
        S = pc.S
        block = ctx.enter_context(nc.Block())

        @block.sync
        def _(sp):
            for f in range(NF):
                job_loads(m, sp, w1, s0 + 16 * f, f * KC)
                job_loads(m, sp, w2[f * D:(f + 1) * D, :], s0 + 16 * f + 8)

        @block.gpsimd
        def _(pool):
            ring_low(m, pool, s0, 0)
            ring_low(m, pool, s0 + 1, 1)
            mod.gpsimd(pool)
            job_lows(m, pool, s0 + 2, 16 * NF - 2)

        @block.tensor
        def _(pe):
            norm.tensor(pe)
            with pe.Fori(0, NF) as f:
                with pe.Fori(0, KC // 2) as i:
                    for p in range(2):
                        ring_mul(m, pe, f * 16 + (i * 2 + (s0 + p)), p, xh, xl, ready=(mod.S("lo"), 0) if p == 0 else None)
                for p in range(2):
                    ring_mul(m, pe, f * 16 + (s0 + 8 + p), p, hh, hl, ready=(S("hid"), f * 8) if p == 0 else None)
                with pe.Fori(1, KC // 2) as i:
                    for p in range(2):
                        ring_mul(m, pe, f * 16 + (i * 2 + (s0 + 8 + p)), p, hh, hl)

        @block.scalar
        def _(act):
            ring_high(m, act, s0, 0, landed_at(s0))
            ring_high(m, act, s0 + 1, 1, landed_at(s0 + 1))
            norm.scalar(act)
            mod.scalar(act)

            def hidden(s, p, e):
                act.wait_ge(m.mm_done, s + 1)
                act.wait_ge(m.t_free, e + 1)
                nc.scalar.activation(as3(tmp[:, p, :]), acc_view(m, p), ACT.Relu).then_inc(m.acc_free[p], 2)

            def first_block(f):
                with act.Fori(0, KC // 2) as i:
                    for p in range(2):
                        s = f * 16 + (i * 2 + (s0 + p))
                        ring_high(m, act, s + 2, p, f * 128 + (i * 16 + landed_at(s0 + 2 + p)))
                        hidden(s, p, f * 8 + (i * 2 + (e0 + p)))

            with act.Fori(0, NF - 1) as f:
                first_block(f)
                with act.Fori(0, KC // 2) as i:
                    for p in range(2):
                        ring_high(m, act, f * 16 + (i * 2 + (s0 + 10 + p)), p, f * 128 + (i * 16 + landed_at(s0 + 10 + p)))
            f = NF - 1
            first_block(f)
            with act.Fori(0, KC // 2 - 1) as i:
                for p in range(2):
                    ring_high(m, act, i * 2 + (s0 + 16 * f + 10 + p), p, i * 16 + landed_at(s0 + 16 * f + 10 + p))

        @block.vector
        def _(dve):
            norm.vector(dve)
            mod.vector(dve, lambda k: dve.wait_ge(norm.S("x"), k + 1))
            dve.wait_ge(mod.S("alpha"), KC)
            dve.wait_ge(mod.S("lo"), KC)
            with dve.Fori(0, NF) as f:
                with dve.Fori(0, KC // 2) as i:
                    for p in range(2):
                        c, n = i * 2 + p, f * 8 + (i * 2 + p)
                        t = tmp[:, p, :]
                        dve.wait_ge(m.acc_free[p], f * 16 + (i * 2 + (s0 + 2)))
                        nc.vector.tensor_tensor(t, t, t, ALU.mult).then_inc(S("sq"), 1)
                        dve.wait_ge(S("sq"), n + 1)
                        hc = hh[:, bass.ds(c, 1), :].rearrange("p a t -> p (a t)")
                        lc = hl[:, bass.ds(c, 1), :].rearrange("p a t -> p (a t)")
                        nc.vector.tensor_copy(hc, t).then_inc(S("hid_hi"), 1)
                        dve.wait_ge(S("hid_hi"), n + 1)
                        nc.vector.tensor_tensor(lc, t, hc.bitcast(F32), ALU.subtract).then_inc(S("hid"), 1)
                        dve.wait_ge(S("hid"), n + 1)
                        dve.sem_inc(m.t_free, 1)
                with dve.Fori(0, KC // 2) as i:
                    for p in range(2):
                        s = f * 16 + (i * 2 + (s0 + 8 + p))
                        add_gated(m, dve, z, gate, i * 2 + p, s, p, S("sum8"), tmp8)
                        add_sample(m, dve, z, i * 2 + p, S("sum8"), tmp8, f * 16 + (i * 4 + (2 * p + 1)))
        m.slabs = s0 + 16 * NF
        m.staged = e0 + KC * NF


def qkv_phase(m, z):
    nc, io = m.nc, m.io
    with ExitStack() as ctx:
        pc = Piece(m, ctx, "qkv")
        tmp = pc.sb("tmp", [P, 2, T])
        stage = pc.sb("stage", [P, 2, T])
        xh, xl = pc.sb("hi", [P, KC, T], F32R), pc.sb("lo", [P, KC, T], F32R)
        norm = Norm(m, ctx, "norm1", z, 1, tmp)
        mods = [Modulate(m, ctx, "modkv", z, M_KVSC, M_KVSH, xh, xl, tmp),
                Modulate(m, ctx, "modq", z, 6 + M_SCM, 6 + M_SHM, xh, xl, tmp)]
        jobs = [(io["kv_w_k"], S_K), (io["kv_w_v"], S_V), (io["b_w_q"][0], S_R)]
        s0 = m.slabs
        S = pc.S
        block = ctx.enter_context(nc.Block())

        @block.sync
        def _(sp):
            for j, (w, _) in enumerate(jobs):
                job_loads(m, sp, w, s0 + KC * j)

        @block.gpsimd
        def _(pool):
            ring_low(m, pool, s0, 0)
            ring_low(m, pool, s0 + 1, 1)
            mods[0].gpsimd(pool)
            job_lows(m, pool, s0 + 2, 2 * KC - 2)
            ring_low(m, pool, s0 + 2 * KC, 0)
            mods[1].gpsimd(pool)
            ring_low(m, pool, s0 + 2 * KC + 1, 1)
            job_lows(m, pool, s0 + 2 + 2 * KC, KC - 2)
            for k in range(KC):
                pool.wait_ge(norm.S("x"), k + 1)
            nc.gpsimd.dma_start(m.xt.rearrange("c p t -> p c t"), z[:]).then_inc(S("x_out"), 16)
            pool.wait_ge(S("x_out"), 16)

        @block.tensor
        def _(pe):
            norm.tensor(pe)
            job_muls(m, pe, s0, xh, xl, ready=mods[0].S("lo"))
            job_muls(m, pe, s0 + KC, xh, xl, free=S("x_free"))
            job_muls(m, pe, s0 + 2 * KC, xh, xl, ready=mods[1].S("lo"))

        @block.vector
        def _(dve):
            norm.vector(dve)
            mods[0].vector(dve, lambda k: dve.wait_ge(norm.S("x"), k + 1))
            dve.wait_ge(mods[0].S("lo"), KC)

            def chunk_free(k):
                if k < KC - 1:
                    dve.wait_ge(S("x_free"), k + 1)
                else:
                    dve.wait_ge(m.mm_done, s0 + 2 * KC)
            mods[1].vector(dve, chunk_free)

        @block.scalar
        def _(act):
            def store(s, j, c, p, stored):
                act.wait_ge(m.mm_done, s + 1)
                if stored is not None:
                    act.wait_ge(S(f"out{p}"), stored)
                nc.scalar.activation(as3(stage[:, p, :]), acc_view(m, p), ACT.Copy).then_inc(m.acc_free[p], 2)
                act.wait_ge(m.acc_free[p], s - p + 2)
                dst = m.scr[j, bass.ds(c, 1)].rearrange("a p t -> (a p) t")
                nc.scalar.dma_start(dst, stage[:, p, :]).then_inc(S(f"out{p}"), 16)

            ring_high(m, act, s0, 0, landed_at(s0))
            ring_high(m, act, s0 + 1, 1, landed_at(s0 + 1))
            norm.scalar(act)
            for j, (_, dst) in enumerate(jobs):
                b = s0 + KC * j
                n = 4 * j
                for p in range(2):
                    ring_high(m, act, b + 2 + p, p, landed_at(b + 2 + p))
                    store(b + p, dst, p, p, 16 * n if n else None)
                with act.Fori(1, KC // 2 - 1) as i:
                    for p in range(2):
                        ring_high(m, act, i * 2 + (b + 2 + p), p, i * 16 + landed_at(b + 2 + p))
                        store(i * 2 + (b + p), dst, i * 2 + p, p, i * 16 + 16 * n)
                for p in range(2):
                    if j < 2:
                        ring_high(m, act, b + KC + p, p, landed_at(b + KC + p))
                    store(b + KC - 2 + p, dst, KC - 2 + p, p, 16 * (n + 3))
            for p in range(2):
                act.wait_ge(S(f"out{p}"), 16 * 12)
        m.slabs = s0 + 3 * KC


def attention_phase(m, qs, ks, vs, lam):
    nc, io = m.nc, m.io
    with ExitStack() as ctx:
        pc = Piece(m, ctx, "attn")
        S = pc.S
        q, k, v = (pc.sb(x, [P, 2, T]) for x in ("q", "k", "v"))
        krow, vrow = pc.sb("k_rows", [P, 2, KC, P]), pc.sb("v_rows", [P, 2, KC, P])
        causal = pc.sb("causal", [P, P])
        pm = pc.sb("probs", [P, 2, 2, SEQ])
        at = pc.sb("attn", [P, 2, SEQ])
        aT = pc.sb("attn_cols", [P, 2, SEQ])
        o, osq = pc.sb("o", [P, 2, KC, P]), pc.sb("o_sq", [P, KC, P])
        outT = pc.sb("out_cols", [P, SEQ])
        mx, nb, l, rl = (pc.sb(x, [P, 2, 2]) for x in ("max", "neg_max", "sums", "weights"))
        ss, rs = pc.sb("ss", [P, KC]), pc.sb("rms", [P, KC])
        lq, eps, gcol = pc.sb("lam_rows", [P, 2, P]), pc.sb("eps", [P, 1]), pc.sb("subln_g", [P, 1])
        ls = pc.sb("lam_sums", [P, 2])
        block = ctx.enter_context(nc.Block())
        tiles = (("k", k, S_K), ("v", v, S_V), ("q", q, S_R))

        def need(eng, name, c, par, n=1, j=1, back=0):
            eng.wait_ge(S(name), c * (2 * n) + ((par - back) * n + j))

        def loop(eng, body):
            for par in range(2):
                body(0, par, True)
            with eng.Fori(1, KC // 2) as c:
                for par in range(2):
                    body(c, par, False)

        def chunk(t, base, c, par):
            return t[base, bass.ds(c * 2 + par, 1)].rearrange("a p t -> (a p) t")

        def rows_of(out, c, par):
            flat = out[0].rearrange("(t p) h n -> h p t n", p=P) if len(out.shape) == 4 else \
                out[0].rearrange("(t p) h m n -> h p t (m n)", p=P)
            return flat[bass.ds(c * 2 + par, 1)].rearrange("a p t n -> (a p) t n")

        @block.sync
        def _(sp):
            nc.sync.dma_start(causal[:], io["masks"][:, C_CAUSAL:C_CAUSAL + P]).then_inc(S("const_in"), 16)
            for i, name in enumerate(("b_lam_q", "b_lam_k")):
                nc.sync.dma_start(lq[:, i, :], io[name].rearrange("a m n -> a (m n)").to_broadcast([P, P])).then_inc(S("const_in"), 16)
            nc.sync.dma_start(gcol[:], io["b_subln_g"].rearrange("a (n o) -> (a n) o", o=1)).then_inc(S("const_in"), 16)

            def body(c, par, first):
                for name, tile, base in tiles:
                    if not first:
                        need(sp, "o_mm", c, par, KC, KC, 2)
                    nc.sync.dma_start(tile[:, par, :], chunk(m.scr, base, c, par)).then_inc(S(f"in_{name}{par}"), 16)
            loop(sp, body)

        @block.gpsimd
        def _(pool):
            def body(c, par, first):
                for name, tile, dst in (("q", q, qs), ("k", k, ks), ("v", v, vs)):
                    pool.wait_ge(S(f"in_{name}{par}"), c * 16 + 16)
                    last = nc.gpsimd.tensor_copy(dst[:, bass.ds(c * 2 + par, 1), :].rearrange("p a n -> p (a n)"),
                                                 tile[:, par, SEQ:T])
                last.then_inc(S("cols"), 1)
                need(pool, "o", c, par, KC, KC)
                if not (first and par == 0):
                    need(pool, "ss", c, par, 1, 1, 1)
                nc.gpsimd.tensor_tensor(osq[:], o[:, par], o[:, par], ALU.mult).then_inc(S("osq"), 1)
            loop(pool, body)

        @block.tensor
        def _(pe):
            def body(c, par, first):
                start = first and par == 0

                def turn(tile, name):
                    for j in range(KC):
                        last = nc.tensor.transpose(m.aux[j // 4][:, (j % 4) * P:(j % 4 + 1) * P],
                                                   tile[:, par, j * P:(j + 1) * P], m.ident[:])
                    last.then_inc(S(name), 1)

                def scores(i):
                    for mp in range(2):
                        if i:
                            need(pe, f"exp{mp}", c, par, KC, i)
                        elif not start:
                            need(pe, f"exp{mp}", c, par, KC, KC, 1)
                        h = slice(64 * mp, 64 * mp + 64)
                        n = (i + 1) * P
                        for b in range((n + 511) // 512):
                            w = min(512, n - 512 * b)
                            last = nc.tensor.matmul(m.acc[mp][:, b, 0:w], q[h, par, i * P:(i + 1) * P],
                                                    k[h, par, 512 * b:512 * b + w], start=True, stop=True)
                        last.then_inc(S(f"qk{mp}"), 1)

                def turn_attn(i):
                    need(pe, "attn", c, par, KC, i + 1)
                    if i:
                        need(pe, "aT", c, par, KC, i)
                    if i == 1 and not start:
                        need(pe, "outT", c, par, 1, 1, 1)
                    for j in range(i + 1):
                        last = nc.tensor.transpose(m.aux[j // 4][:, (j % 4) * P:(j % 4 + 1) * P],
                                                   at[:, i % 2, j * P:(j + 1) * P], m.ident[:])
                    last.then_inc(S("attn_t"), 1)

                def values(i):
                    need(pe, "aT", c, par, KC, i + 1)
                    if i >= 2:
                        need(pe, "o", c, par, KC, i - 1)
                    for j in range(i + 1):
                        last = nc.tensor.matmul(m.acc[i % 2][:, 2, 0:P], aT[:, i % 2, j * P:(j + 1) * P], vrow[:, par, j, :],
                                                start=(j == 0), stop=(j == i))
                    last.then_inc(S("o_mm"), 1)

                pe.wait_ge(S(f"in_k{par}"), c * 16 + 16)
                turn(k, "k_t")
                pe.wait_ge(S(f"in_q{par}"), c * 16 + 16)
                scores(0)
                pe.wait_ge(S(f"in_v{par}"), c * 16 + 16)
                need(pe, "krow", c, par)
                turn(v, "v_t")
                need(pe, "vrow", c, par)
                for i in range(1, KC):
                    scores(i)
                    turn_attn(i - 1)
                    values(i - 1)
                    if i == 1 and not start:
                        finish(c, par)
                turn_attn(KC - 1)
                values(KC - 1)

            def finish(c, par):
                need(pe, "on", c, par, 1, 1, 1)
                for j in range(KC):
                    last = nc.tensor.transpose(m.aux[j // 4][:, (j % 4) * P:(j % 4 + 1) * P], o[:, 1 - par, j, :], m.ident[:])
                last.then_inc(S("o_t"), 1)

            loop(pe, body)
            finish(KC // 2, 0)

        @block.vector
        def _(dve):
            V = nc.vector
            V.memset(eps[:], SUBLN_EPS).then_inc(S("eps"), 1)
            dve.wait_ge(S("const_in"), 64)
            V.tensor_tensor(lq[:, 0, :], lq[:, 0, :], lq[:, 1, :], ALU.mult).then_inc(S("lam"), 1)
            dve.wait_ge(S("lam"), 1)
            V.tensor_reduce(ls[:], lq[:, 0, :].rearrange("p (a n) -> p a n", a=2), AX.X, ALU.add).then_inc(S("lam"), 1)
            dve.wait_ge(S("lam_exp"), 1)
            V.tensor_tensor(lam[:], ls[:, 1:2], ls[:, 0:1], ALU.subtract).then_inc(S("lam"), 1)
            dve.wait_ge(S("lam"), 3)
            V.tensor_scalar_add(lam[:], lam[:], -LAM_INIT).then_inc(S("lam"), 1)
            V.tensor_scalar(gcol[:], gcol[:], 1.0 - LAM_INIT, None, ALU.mult).then_inc(S("lam"), 1)
            dve.wait_ge(S("lam"), 5)

            def body(c, par, first):
                start = first and par == 0

                def maxima(i):
                    n, ip = (i + 1) * P, i % 2
                    for mp in range(2):
                        need(dve, f"qk{mp}", c, par, KC, i + 1)
                        d = m.acc[mp][:, i // 4, (i % 4) * P:(i % 4 + 1) * P]
                        V.tensor_tensor(d, d, causal[:], ALU.add).then_inc(S(f"masked{mp}"), 1)
                        need(dve, f"masked{mp}", c, par, KC, i + 1)
                        V.tensor_reduce(mx[:, ip, mp:mp + 1], m.acc[mp][:].rearrange("p b n -> p (b n)")[:, 0:n], AX.X,
                                        ALU.max).then_inc(S(f"max{mp}"), 1)
                        need(dve, f"max{mp}", c, par, KC, i + 1)
                        V.tensor_scalar(nb[:, ip, mp:mp + 1], mx[:, ip, mp:mp + 1], -ATTN_SCALE, None,
                                        ALU.mult).then_inc(S(f"nb{mp}"), 1)

                def combine(i):
                    n, ip = (i + 1) * P, i % 2
                    for mp in range(2):
                        need(dve, f"exp{mp}", c, par, KC, i + 1)
                    V.reciprocal(rl[:, ip, :], l[:, ip, :]).then_inc(S("rl"), 1)
                    need(dve, "rl", c, par, KC, i + 1)
                    if i >= 2:
                        need(dve, "attn_t", c, par, KC, i - 1)
                    V.tensor_scalar(at[:, ip, 0:n], pm[:, ip, 0, 0:n], rl[:, ip, 0:1], None, ALU.mult).then_inc(S("at0"), 1)
                    V.tensor_tensor(rl[:, ip, 1:2], rl[:, ip, 1:2], lam[:], ALU.mult).then_inc(S("rl1"), 1)
                    need(dve, "at0", c, par, KC, i + 1)
                    need(dve, "rl1", c, par, KC, i + 1)
                    V.scalar_tensor_tensor(at[:, ip, 0:n], pm[:, ip, 1, 0:n], rl[:, ip, 1:2], at[:, ip, 0:n], ALU.mult,
                                           ALU.add).then_inc(S("attn"), 1)

                maxima(0)
                for i in range(1, KC):
                    combine(i - 1)
                    maxima(i)
                    if i == 1 and not start:
                        finish(c, par)
                need(dve, "cols", c, par)
                combine(KC - 1)

            def finish(c, par):
                need(dve, "osq", c, par, 1, 1, 1)
                V.tensor_reduce(ss[:], osq[:], AX.X, ALU.add).then_inc(S("ss"), 1)
                need(dve, "rms", c, par, 1, 1, 1)
                V.reciprocal(rs[:], ss[:]).then_inc(S("rrms"), 1)
                need(dve, "rrms", c, par, 1, 1, 1)
                V.tensor_tensor(o[:, 1 - par], o[:, 1 - par], rs[:].unsqueeze(2).to_broadcast([P, KC, P]),
                                ALU.mult).then_inc(S("on"), 1)

            loop(dve, body)
            finish(KC // 2, 0)

        @block.scalar
        def _(act):
            act.wait_ge(S("lam"), 2)
            act.wait_ge(S("eps"), 1)
            nc.scalar.activation(ls[:], ls[:], ACT.Exp).then_inc(S("lam_exp"), 1)

            def body(c, par, first):
                start = first and par == 0

                def two(name, dst, dram, c, par):
                    need(act, name + "_t", c, par)
                    if not first:
                        act.wait_ge(S(f"{name}_out{par}"), c * 16)
                        if name == "v":
                            need(act, "o_mm", c, par, KC, KC, 2)
                    nc.scalar.activation(dst[:, par].rearrange("p (a j) n -> p a (j n)", a=2), m.aux2[:, :, :],
                                         ACT.Copy).then_inc(S(name + "row"), 1)
                    need(act, name + "row", c, par)
                    nc.scalar.dma_start(rows_of(dram, c, par), dst[:, par]).then_inc(S(f"{name}_out{par}"), 16)

                def exps(i):
                    n, ip = (i + 1) * P, i % 2
                    for mp in range(2):
                        need(act, f"nb{mp}", c, par, KC, i + 1)
                        if i >= 2:
                            need(act, "attn", c, par, KC, i - 1)
                        elif not start:
                            need(act, "attn", c, par, KC, KC - 1 + i, 1)
                        nc.scalar.activation(pm[:, ip, mp, 0:n], m.acc[mp][:].rearrange("p b n -> p (b n)")[:, 0:n], ACT.Exp,
                                             bias=nb[:, ip, mp:mp + 1], scale=ATTN_SCALE,
                                             accum_out=l[:, ip, mp:mp + 1]).then_inc(S(f"exp{mp}"), 1)

                def turned(i):
                    need(act, "attn_t", c, par, KC, i + 1)
                    n = (i + 1) * P
                    if i >= 2:
                        need(act, "o_mm", c, par, KC, i - 1)
                    nc.scalar.activation(aT[:, i % 2, 0:n], m.aux2[:].rearrange("p a n -> p (a n)")[:, 0:n],
                                         ACT.Copy).then_inc(S("aT"), 1)

                def take(i):
                    need(act, "o_mm", c, par, KC, i + 1)
                    nc.scalar.activation(o[:, par, i, :], m.acc[i % 2][:, 2, 0:P], ACT.Copy).then_inc(S("o"), 1)

                two("k", krow, io["k_prompt"], c, par)
                exps(0)
                two("v", vrow, io["v_prompt"], c, par)
                for i in range(1, KC):
                    turned(i - 1)
                    exps(i)
                    take(i - 1)
                    if i == 1 and not start:
                        finish(c, par, first)
                turned(KC - 1)
                take(KC - 1)

            def finish(c, par, first):
                need(act, "ss", c, par, 1, 1, 1)
                nc.scalar.activation(ss[:], ss[:], ACT.Sqrt, bias=eps[:, 0:1], scale=1.0 / P).then_inc(S("rms"), 1)
                need(act, "o_t", c, par, 1, 1, 1)
                if not (first and par == 1):
                    act.wait_ge(S("mix_out"), c * 32 + (par - 1) * 16)
                nc.scalar.activation(outT[:].rearrange("p (a n) -> p a n", a=2), m.aux2[:, :, :], ACT.Copy,
                                     scale=gcol[:, 0:1]).then_inc(S("outT"), 1)
                need(act, "outT", c, par, 1, 1, 1)
                nc.scalar.dma_start(m.scr[S_MIX, bass.ds(c * 2 + (par - 1), 1), :, 0:SEQ].rearrange("a p t -> (a p) t"),
                                    outT[:]).then_inc(S("mix_out"), 16)
            loop(act, body)
            finish(KC // 2, 0, False)
            for par in range(2):
                for name in ("k", "v"):
                    act.wait_ge(S(f"{name}_out{par}"), 16 * KC // 2)
            act.wait_ge(S("mix_out"), 16 * KC)


def sample_attention_phase(m, qs, ks, vs, lam):
    nc, io = m.nc, m.io
    NP, NH = 8, 8
    with ExitStack() as ctx:
        pc = Piece(m, ctx, "paged")
        S = pc.S
        NK, NVB = 4, 2
        kp = pc.sb("k_page", [P, NK, D])
        prod = pc.sb("k_prod", [P, 2, D])
        own = pc.sb("k_prod_vector", [P, D])
        orow = pc.sb("o_rows", [1, 2, D])
        qb = pc.sb("q_rows_all", [P, 2, D])
        vp = pc.sb("v_pages", [P, NVB, NP, D])
        sc = pc.sb("scores", [P, NP, NS, 16])
        rows = pc.sb("rows", [NS, 3, D])
        pr = pc.sb("probs", [P, NP * P + 1])
        prT = pc.sb("prob_cols", [P, NP, P])
        at = pc.sb("attn", [P, NP, NS, NH])
        newT, anew = pc.sb("new_row", [1, P]), pc.sb("attn_new", [1, NS * NH])
        half = pc.sb("halves", [P, 2])
        pn = pc.sb("new_prod", [P, NS, NH, 2])
        qk = pc.sb("qk_new", [P, NH, NS])
        mx, l, w, sign = (pc.sb(x, [P, 1]) for x in ("max", "sum", "weight", "sign"))
        res, o2, bc = (pc.sb(x, [P, NS, NH]) for x in ("res", "res2", "attn_new_all"))
        eps, gcol, ones = pc.sb("eps", [P, 1]), pc.sb("subln_g", [P, 1]), pc.sb("ones", [P, P])
        tab = pc.sb("table", [1, NS * NP], I32)
        cm = pc.sb("cm", [P, 2])
        outc = pc.sb("out_cols", [P, NH, NS])
        block = ctx.enter_context(nc.Block())
        NPAGE = NS * NP
        pool_rows = io["cache_k"].shape[0]
        kflat = io["cache_k"].rearrange("g p h m n -> g p (h m n)")
        vflat = io["cache_v"].rearrange("g p h n -> g p (h n)")
        qrow_dram = m.yrows

        def by_pool(u):
            return 3 * (u // 4) + min(u % 4, 2) + 1

        def page_used(eng, u):
            if u % 4 == 3:
                eng.wait_ge(S("own_prod"), u // 4 + 1)
            else:
                eng.wait_ge(S("prod"), by_pool(u))

        @block.sync
        def _(sp):
            nc.sync.dma_start(tab[:], io["page_table"].rearrange("(o b) n -> o (b n)", o=1)).then_inc(S("table_in"), 16)
            nc.sync.dma_start(gcol[:], io["b_subln_g"].rearrange("a (n o) -> (a n) o", o=1)).then_inc(S("const_in"), 16)
            nc.sync.dma_start(half[:], io["masks"][:, C_BLOCK:C_BLOCK + P:64], allow_slow_non_contiguous=True).then_inc(S("const_in"), 16)
            nc.sync.dma_start(sign[:], io["masks"][:, C_SIGN:C_SIGN + 1], allow_slow_non_contiguous=True).then_inc(S("const_in"), 16)
            sp.wait_ge(S("table_in"), 16)
            sp.wait_ge(S("rows"), 1)
            nc.sync.dma_start(io["k_sample"].rearrange("b o h m n -> (b o) (h m n)"), rows[:, 1, :]).then_inc(S("rows_out"), 16)
            nc.sync.dma_start(io["v_sample"].rearrange("b o h n -> (b o) (h n)"), rows[:, 2, :]).then_inc(S("rows_out"), 16)
            nc.sync.dma_start(qrow_dram, rows[:, 0, :]).then_inc(S("q_out"), 16)
            sp.wait_ge(S("q_out"), 16)
            for u in range(NPAGE):
                b, g = u // NP, u % NP
                if g == 0:
                    if b >= 2:
                        page_used(sp, NP * (b - 1) - 2)
                        page_used(sp, NP * (b - 1) - 1)
                    nc.sync.dma_start(qb[:, b % 2, :], qrow_dram[b:b + 1, :].to_broadcast([P, D])).then_inc(S(f"qb{b % 2}"), 16)
                page = sp.value_load(tab[0:1, u:u + 1], min_val=0, max_val=pool_rows - 1)
                if u >= NK:
                    page_used(sp, u - NK)
                nc.sync.dma_start(kp[:, u % NK, :], kflat[bass.ds(page, 1)].rearrange("a p n -> (a p) n")).then_inc(S(f"k_in{u % NK}"), 16)
            sp.wait_ge(S("out"), 1)
            nc.sync.dma_start(m.scr[S_MIX, :, :, SEQ:T].rearrange("h p n -> p h n"), outc[:]).then_inc(S("mix_out"), 16)
            sp.wait_ge(S("mix_out"), 16)
            sp.wait_ge(S("rows_out"), 32)

        @block.scalar
        def _(act):
            act.wait_ge(S("table_in"), 16)
            act.wait_ge(S("rows_t"), 1)
            for i in range(3):
                last = nc.scalar.activation(rows[:, i, :].rearrange("p (a n) -> p a n", a=2), (m.acc[0], m.acc[1], m.aux2)[i][0:NS, 0:2, :],
                                            ACT.Copy)
            last.then_inc(S("rows"), 1)

            def load_v(b):
                if b >= NVB:
                    act.wait_ge(S("pv"), b - NVB + 1)
                for g in range(NP):
                    u = b * NP + g
                    page = act.value_load(tab[0:1, u:u + 1], min_val=0, max_val=pool_rows - 1)
                    nc.scalar.dma_start(vp[:, b % NVB, g, :], vflat[bass.ds(page, 1)].rearrange("a p n -> (a p) n")).then_inc(S(f"v_in{b % NVB}"), 16)

            load_v(0)
            load_v(1)
            for g in range(NP // 4):
                act.wait_ge(S("sc_t"), g + 1)
                nc.scalar.activation(pr[:, g * 512:(g + 1) * 512], m.acc[0][:, g, :], ACT.Copy)
            act.wait_ge(S("new_mm"), 1)
            nc.scalar.activation(pr[:, NP * P:NP * P + 1], m.acc[1][:, 0, 0:1], ACT.Copy).then_inc(S("pr"), 1)
            act.wait_ge(S("nb"), 2)
            nc.scalar.activation(pr[:], pr[:], ACT.Exp, bias=mx[:, 0:1], scale=ATTN_SCALE, accum_out=l[:, 0:1]).then_inc(S("exp"), 1)
            for b in range(NS):
                if b + NVB < NS:
                    load_v(b + NVB)
                act.wait_ge(S("pv"), b + 1)
                if b >= 2:
                    act.wait_ge(S("o_cols"), b - 1)
                nc.scalar.activation(orow[:, b % 2, :].rearrange("p (a n) -> p a n", a=2), m.acc[b % 2][0:1, 0:2, :],
                                     ACT.Copy).then_inc(S("orow"), 1)
            act.wait_ge(S("ms"), 1)
            nc.scalar.activation(o2[:].rearrange("p b h -> p (b h)"), m.acc[0][:, 0, 0:NS * NH], ACT.Sqrt, bias=eps[:, 0:1]).then_inc(S("rms"), 1)

        @block.gpsimd
        def _(pool):
            for u in range(NPAGE):
                b, n = u // NP, by_pool(u) - 1
                if u % 4 == 3:
                    continue
                pool.wait_ge(S(f"k_in{u % NK}"), 16 * (u // NK + 1))
                if u % NP == 0:
                    pool.wait_ge(S(f"qb{b % 2}"), 16 * (b // 2 + 1))
                if n >= 2:
                    pool.wait_ge(S("red"), 4 * ((n - 2) // 3) + (n - 2) % 3 + 1)
                nc.gpsimd.tensor_tensor(prod[:, n % 2, :], kp[:, u % NK, :], qb[:, b % 2, :], ALU.mult).then_inc(S("prod"), 1)

        @block.tensor
        def _(pe):
            for i, t in enumerate((qs, ks, vs)):
                for h in range(NH):
                    last = nc.tensor.transpose((m.acc[0], m.acc[1], m.aux2)[i][0:NS, h // 4, (h % 4) * P:(h % 4 + 1) * P], t[:, h, :], m.ident[:])
            last.then_inc(S("rows_t"), 1)
            pe.wait_ge(S("rows"), 1)
            pe.wait_ge(S("pn"), 1)
            pe.wait_ge(S("ones"), 1)
            nc.tensor.matmul(m.acc[1][:, 0, 0:1], pn[:].rearrange("p b h m -> p (b h m)"), ones[:, 0:1], start=True, stop=True).then_inc(S("new_mm"), 1)
            pe.wait_ge(S("red"), NPAGE)
            for g in range(NP):
                last = nc.tensor.transpose(m.acc[0][:, g // 4, (g % 4) * P:(g % 4 + 1) * P], sc[:, g].rearrange("p b n -> p (b n)"), m.ident[:])
                if g % 4 == 3:
                    last.then_inc(S("sc_t"), 1)
            pe.wait_ge(S("weighted"), 1)
            for g in range(NP):
                last = nc.tensor.transpose(m.acc[0][:, g // 4, (g % 4) * P:(g % 4 + 1) * P], pr[:, g * P:(g + 1) * P], m.ident[:])
            nc.tensor.transpose(m.acc[1][0:1, 0, 0:P], pr[:, NP * P:NP * P + 1], m.ident[:]).then_inc(S("pr_t"), 1)
            pe.wait_ge(S("at"), 1)

            def columns(b):
                pe.wait_ge(S("orow"), b + 1)
                for h in range(NH):
                    last = nc.tensor.matmul(m.aux[0][:, b * NH + h:b * NH + h + 1], orow[:, b % 2, h * P:(h + 1) * P],
                                            ones[0:1, 0:1], start=True, stop=True)
                last.then_inc(S("o_cols"), 1)

            for b in range(NS):
                pe.wait_ge(S(f"v_in{b % NVB}"), 16 * NP * (b // NVB + 1))
                if b >= 2:
                    pe.wait_ge(S("orow"), b - 1)
                for h in range(NH):
                    for g in range(NP):
                        last = nc.tensor.matmul(m.acc[b % 2][0:1, h // 4, (h % 4) * P:(h % 4 + 1) * P], at[:, g, b, h:h + 1],
                                                vp[:, b % NVB, g, h * P:(h + 1) * P], start=(g == 0), stop=(g == NP - 1))
                last.then_inc(S("pv"), 1)
                if b:
                    columns(b - 1)
            columns(NS - 1)
            pe.wait_ge(S("anew"), 1)
            nc.tensor.matmul(m.aux[1][:, 0:NS * NH], ones[0:1, :], anew[:], start=True, stop=True).then_inc(S("bc_mm"), 1)
            pe.wait_ge(S("sq"), 1)
            nc.tensor.matmul(m.acc[0][:, 0, 0:NS * NH], ones[:], o2[:].rearrange("p b h -> p (b h)"), start=True, stop=True).then_inc(S("ms"), 1)

        @block.vector
        def _(dve):
            V = nc.vector
            V.memset(ones[:], 1.0).then_inc(S("ones"), 1)
            V.memset(eps[:], P * SUBLN_EPS).then_inc(S("ones"), 1)
            dve.wait_ge(S("const_in"), 48)
            V.tensor_tensor(qk[:], qs[:], ks[:], ALU.mult).then_inc(S("qk"), 1)
            V.tensor_scalar(gcol[:], gcol[:], (1.0 - LAM_INIT) * math.sqrt(P), None, ALU.mult).then_inc(S("qk"), 1)
            V.tensor_scalar(cm[:, 0:1], sign[:], -1.0, 1.0, ALU.mult, ALU.add).then_inc(S("qk"), 1)
            V.tensor_tensor(cm[:, 1:2], sign[:], lam[:], ALU.mult).then_inc(S("qk"), 1)
            dve.wait_ge(S("qk"), 4)
            V.tensor_tensor(cm[:, 0:1], cm[:, 0:1], cm[:, 1:2], ALU.add).then_inc(S("qk"), 1)
            for mp in range(2):
                last = V.tensor_scalar(pn[:, :, :, mp], qk[:].rearrange("p h b -> p b h"), half[:, mp:mp + 1], None, ALU.mult)
            last.then_inc(S("pn"), 1)
            for u in range(NPAGE):
                b, g = u // NP, u % NP
                if u % 4 == 3:
                    dve.wait_ge(S(f"k_in{u % NK}"), 16 * (u // NK + 1))
                    dve.wait_ge(S(f"qb{b % 2}"), 16 * (b // 2 + 1))
                    if u > 3:
                        dve.wait_ge(S("red"), u - 3)
                    V.tensor_tensor(own[:], kp[:, u % NK, :], qb[:, b % 2, :], ALU.mult).then_inc(S("own_prod"), 1)
                page_used(dve, u)
                src = own[:] if u % 4 == 3 else prod[:, (by_pool(u) - 1) % 2, :]
                V.tensor_reduce(sc[:, g, b, :], src.rearrange("p (h n) -> p h n", n=64), AX.X, ALU.add).then_inc(S("red"), 1)
            dve.wait_ge(S("pr"), 1)
            V.tensor_reduce(mx[:], pr[:], AX.X, ALU.max).then_inc(S("nb"), 1)
            dve.wait_ge(S("nb"), 1)
            V.tensor_scalar(mx[:], mx[:], -ATTN_SCALE, None, ALU.mult).then_inc(S("nb"), 1)
            dve.wait_ge(S("exp"), 1)
            V.reciprocal(w[:], l[:]).then_inc(S("w"), 1)
            dve.wait_ge(S("w"), 1)
            V.tensor_tensor(w[:], w[:], cm[:, 0:1], ALU.mult).then_inc(S("w"), 1)
            dve.wait_ge(S("w"), 2)
            V.tensor_scalar(pr[:], pr[:], w[:, 0:1], None, ALU.mult).then_inc(S("weighted"), 1)
            dve.wait_ge(S("pr_t"), 1)
            V.tensor_copy(prT[:].rearrange("p (a g) n -> p a (g n)", a=2), m.acc[0][:, 0:2, :])
            V.tensor_copy(newT[:], m.acc[1][0:1, 0, 0:P]).then_inc(S("prT"), 1)
            dve.wait_ge(S("prT"), 1)
            pv = prT[:].rearrange("p g (b h m) -> p (g b h) m", h=NH, m=2)
            V.tensor_tensor(at[:].rearrange("p g b h -> p (g b h)"), pv[:, :, 0], pv[:, :, 1], ALU.add).then_inc(S("at"), 1)
            nv = newT[:].rearrange("p (n m) -> p n m", m=2)
            V.tensor_tensor(anew[:], nv[:, :, 0], nv[:, :, 1], ALU.add).then_inc(S("anew"), 1)
            dve.wait_ge(S("bc_mm"), 1)
            V.tensor_tensor(bc[:], m.aux[1][:, 0:NS * NH].rearrange("p (b h) -> p b h", b=NS), vs[:].rearrange("p h b -> p b h"), ALU.mult).then_inc(S("bc"), 1)
            dve.wait_ge(S("o_cols"), NS)
            dve.wait_ge(S("bc"), 1)
            V.tensor_tensor(res[:], m.aux[0][:, 0:NS * NH].rearrange("p (b h) -> p b h", b=NS), bc[:], ALU.add).then_inc(S("res"), 1)
            dve.wait_ge(S("res"), 1)
            V.tensor_tensor(o2[:], res[:], res[:], ALU.mult).then_inc(S("sq"), 1)
            dve.wait_ge(S("rms"), 1)
            V.reciprocal(bc[:], o2[:]).then_inc(S("rrms"), 1)
            dve.wait_ge(S("rrms"), 1)
            V.tensor_tensor(res[:], res[:], bc[:], ALU.mult).then_inc(S("normed"), 1)
            dve.wait_ge(S("normed"), 1)
            V.tensor_scalar(outc[:], res[:].rearrange("p b h -> p h b"), gcol[:, 0:1], None, ALU.mult).then_inc(S("out"), 1)


def y_phase(m, z):
    nc, io = m.nc, m.io
    with ExitStack() as ctx:
        pc = Piece(m, ctx, "y")
        tmp = pc.sb("tmp", [P, 2, T])
        rows = pc.sb("rows", [P, 2, D])
        norm = Norm(m, ctx, "norm3", z, 3, tmp)
        S = pc.S
        block = ctx.enter_context(nc.Block())
        NT = KC + 1

        @block.tensor
        def _(pe):
            norm.tensor(pe)
            pe.wait_ge(norm.S("x"), KC)
            for t in range(NT):
                n = P if t < KC else NS
                if t >= 2:
                    pe.wait_ge(S("in"), t - 1)
                for c in range(KC):
                    last = nc.tensor.transpose(m.acc[t % 2][0:n, c // 4, (c % 4) * P:(c % 4 + 1) * P],
                                               z[:, c, t * P:t * P + n], m.ident[:])
                last.then_inc(S("turned"), 1)

        @block.vector
        def _(dve):
            norm.vector(dve)

        @block.scalar
        def _(act):
            norm.scalar(act)
            for t in range(NT):
                n = P if t < KC else NS
                act.wait_ge(S("turned"), t + 1)
                if t >= 2:
                    act.wait_ge(S(f"out{t % 2}"), 16 * (t // 2))
                nc.scalar.activation(rows[0:n, t % 2, :].rearrange("p (a n) -> p a n", a=2), m.acc[t % 2][0:n, 0:2, :],
                                     ACT.Copy).then_inc(S("in"), 1)

        @block.sync
        def _(sp):
            for t in range(NT):
                sp.wait_ge(S("in"), t + 1)
                if t < KC:
                    nc.sync.dma_start(io["y_prompt"][0, t * P:(t + 1) * P, :], rows[:, t % 2, :]).then_inc(S(f"out{t % 2}"), 16)
                else:
                    nc.sync.dma_start(io["y_sample"].rearrange("b o d -> (b o) d"), rows[0:NS, t % 2, :]).then_inc(S(f"out{t % 2}"), 16)
            sp.wait_ge(S("out0"), 16 * 5)
            sp.wait_ge(S("out1"), 16 * 4)


def program(nc, io):
    with ExitStack() as ctx:
        m = Machine(nc, io, ctx)
        setup_phase(m)
        m.end_phase()
        with ExitStack() as mix:
            h = mix.enter_context(nc.sbuf_tensor("h", [P, KC, T], F32))
            xx = mix.enter_context(nc.sbuf_tensor("xx", [P, KC, T], F32))
            input_phase(m, h, xx)
            m.end_phase()
            project_phase(m, h, xx)
            m.end_phase()
        with ExitStack() as mix:
            bs = mix.enter_context(nc.sbuf_tensor("bonus_sample", [P, KC, NS], F32))
            gs = mix.enter_context(nc.sbuf_tensor("gate_sample", [P, KC, NS], F32))
            scan_phase(m, bs, gs)
            m.end_phase()
            sample_scan_phase(m, bs, gs)
            m.end_phase()
        with nc.sbuf_tensor("z", [P, KC, T], F32) as z:
            output_phase(m, z, 0, M_GTM)
            m.end_phase()
            mlp_phase(m, z, 0)
            m.end_phase()
            qkv_phase(m, z)
            m.end_phase()
        with ExitStack() as att:
            qs, ks, vs = (att.enter_context(nc.sbuf_tensor(f"sample_{x}", [P, KC, NS], F32)) for x in "qkv")
            lam = att.enter_context(nc.sbuf_tensor("neg_lambda", [P, 1], F32))
            attention_phase(m, qs, ks, vs, lam)
            m.end_phase()
            sample_attention_phase(m, qs, ks, vs, lam)
            m.end_phase()
        with nc.sbuf_tensor("z1", [P, KC, T], F32) as z:
            output_phase(m, z, 1, 6 + M_GTM)
            m.end_phase()
            mlp_phase(m, z, 1)
            m.end_phase()
            y_phase(m, z)
            m.end_phase()


_OUTS = [(1, SEQ, D), (NS, 1, D), (1, SEQ, 8, 2, 64), (1, SEQ, 8, P), (1, 1, 16, 64, 64), (1, 1, D),
         (NS, 1, 8, 2, 64), (NS, 1, 8, P), (1, NS, 16, 64, 64), (1, NS, D)]
_OUT_NAMES = ["y_prompt", "y_sample", "k_prompt", "v_prompt", "wkv_prompt", "shift_prompt",
              "k_sample", "v_sample", "wkv_sample", "shift_sample"]


def masks():
    import numpy as np

    t = np.arange(P)
    row, colm = t[:, None], t[None, :]
    out = np.zeros((P, C_ALL), np.float32)
    for l in range(7):
        level = (row >> (l + 1) == colm >> (l + 1)) & ((row >> l) & 1 == 1) & ((colm >> l) & 1 == 0)
        out[:, C_LEVEL + l * P:C_LEVEL + (l + 1) * P] = level.T if l == 0 else level
    out[:, C_UPPER:C_UPPER + P] = row < colm
    out[:, C_UPPER + P:C_UPPER + 2 * P] = row <= colm
    out[:, C_BLOCK:C_BLOCK + P] = row // 64 == colm // 64
    out[:, C_CAUSAL:C_CAUSAL + P] = np.where(colm <= row, 0, NEG)
    out[:, C_RESET:C_RESET + P] = colm > 0
    out[:, C_SIGN] = t % 2
    return out


def kernel(**inputs):
    import numpy as np
    import concourse.bacc as bacc
    from concourse.bass_utils import run_bass_kernel_spmd

    nc = bacc.Bacc("TRN2", target_bir_lowering=False, num_devices=1)
    arrays, io = {}, {}
    inputs["masks"] = masks()
    for name, value in inputs.items():
        a = np.ascontiguousarray(value)
        arrays[f"in_{name}"] = a
        io[name] = nc.dram_tensor(f"in_{name}", a.shape, mybir.dt.from_np(a.dtype), kind="ExternalInput").ap()
    for name, shape in zip(_OUT_NAMES, _OUTS):
        io[name] = nc.dram_tensor(f"out_{name}", shape, F32, kind="ExternalOutput").ap()
    program(nc, io)
    r = run_bass_kernel_spmd(nc, [arrays], core_ids=[0])
    return tuple(r.results[0][f"out_{name}"] for name in _OUT_NAMES)
```
